# Optimizing a Trainium2 kernel written in Bass

```python
import math
import jax, jax.numpy as jnp
from jax import lax
import numpy as np

D_MODEL = 1024
BATCH = 1
SEQ = 2048
DEPTH = 1
DEC_BATCH = 1
DEC_SEQ = 64
PAST_LEN = 512

CHUNK = 64
GROUP_W = D_MODEL // 4
HEAD_DIM = 64
EPS = 1e-6
GLA_HEADS = GROUP_W // HEAD_DIM
GLA_DK = HEAD_DIM // 2
GLA_DV = HEAD_DIM
GLA_RANK = 16
GLA_TAU = 16.0
RG_W = GROUP_W
RG_BLOCKS = 4
RG_BLOCK = RG_W // RG_BLOCKS
RG_CONV = 4
RG_C = 8.0
SB_HEADS = GROUP_W // HEAD_DIM
SB_DH = HEAD_DIM
SB_BLOCK = 128
SC_W = GROUP_W
SC_CONV = 3
D_FF = 4 * D_MODEL

IN_SIZES = (GLA_HEADS * GLA_DK, GLA_HEADS * GLA_DK, GLA_HEADS * GLA_DV, GLA_RANK, GROUP_W,
            RG_W, RG_W,
            SB_HEADS * SB_DH, SB_HEADS * SB_DH, SB_HEADS * SB_DH,
            SC_W, SC_W, SC_W)
N_IN = sum(IN_SIZES)

kernel_name = 'hybrid_stream_gla_rglru_stickbreak_shortconv_step'

def rmsnorm(x, g):
    xf = x.astype(jnp.float32)
    y = xf * lax.rsqrt(jnp.mean(xf * xf, axis=-1, keepdims=True) + EPS)
    return (y * g.astype(jnp.float32)).astype(x.dtype)

def head_rmsnorm(x, g):
    shp = x.shape
    xf = x.astype(jnp.float32).reshape(shp[:-1] + (shp[-1] // HEAD_DIM, HEAD_DIM))
    y = xf * lax.rsqrt(jnp.mean(xf * xf, axis=-1, keepdims=True) + EPS)
    return (y.reshape(shp) * g.astype(jnp.float32)).astype(x.dtype)

def split_cols(z):
    parts, off = [], 0
    for n in IN_SIZES:
        parts.append(z[..., off:off + n])
        off += n
    return parts

def causal_dwconv(x, buf, w):
    width = w.shape[0]
    t = x.shape[1]
    xp = jnp.concatenate([buf.astype(x.dtype), x], axis=1)
    y = xp[:, 0:t] * w[0]
    for i in range(1, width):
        y = y + xp[:, i:i + t] * w[i]
    return y, xp[:, t:]

def _affine_combine(e1, e2):
    a1, b1 = e1
    a2, b2 = e2
    return a1 * a2, a2 * b1 + b2

def linear_scan(a, u, h0):
    a_cum, u_cum = lax.associative_scan(_affine_combine, (a, u), axis=1)
    hs = u_cum + a_cum * h0[:, None]
    return hs, hs[:, -1]

def gla_chunked(s0, q, k, v, log_alpha, chunk):
    b, t, h, dk = q.shape
    dv = v.shape[-1]
    nc = t // chunk
    f32 = jnp.float32
    qc = q.astype(f32).reshape(b, nc, chunk, h, dk)
    kc = k.astype(f32).reshape(b, nc, chunk, h, dk)
    vc = v.astype(f32).reshape(b, nc, chunk, h, dv)
    g = jnp.cumsum(log_alpha.astype(f32).reshape(b, nc, chunk, h, dk), axis=2)
    g_end = g[:, :, -1]
    u = jnp.einsum('bclhk,bclhv->bchkv', kc * jnp.exp(g_end[:, :, None] - g), vc)
    dec = jnp.exp(g_end)[..., None]
    dec_cum, u_cum = lax.associative_scan(_affine_combine, (dec, u), axis=1)
    s = u_cum + dec_cum * s0.astype(f32)[:, None]
    o = jnp.einsum('bclhk,bchkv->bclhv', qc, s).reshape(b, t, h, dv)
    return o, s[:, -1]

def sb_block(qb, qpos, k, v, kpos):
    z = jnp.einsum('bqhd,bkhd->bhqk', qb, k).astype(jnp.float32) * (SB_DH ** -0.5)
    mask = kpos[None, :] < qpos[:, None]
    ls_neg = jax.nn.log_sigmoid(-z)
    ls_pos = ls_neg + z
    lneg = jnp.where(mask, ls_neg, 0.0)
    rest = lax.cumsum(lneg, axis=3, reverse=True) - lneg
    w = jnp.where(mask, jnp.exp(ls_pos + rest), 0.0)
    return jnp.einsum('bhqk,bkhd->bqhd', w, v.astype(jnp.float32))

def stick_breaking(q, k, v, q_pos, k_pos):
    b, t, h, d = q.shape
    if t <= SB_BLOCK:
        return sb_block(q, q_pos, k, v, k_pos)
    nb = t // SB_BLOCK
    qb = q.reshape(b, nb, SB_BLOCK, h, d).transpose(1, 0, 2, 3, 4)
    pb = q_pos.reshape(nb, SB_BLOCK)
    out = lax.map(lambda a: sb_block(a[0], a[1], k, v, k_pos), (qb, pb))
    return out.transpose(1, 0, 2, 3, 4).reshape(b, t, h, d)

def trunk_layer(x, c, state, p):
    (s_gla, h_rg, buf_rg, k_past, v_past, buf_sc) = state
    (ln1_g, ln2_g, w_ada, b_ada, w_in, gla_wa2, gla_ba, rg_conv_w, rg_conv_b,
     rg_wa, rg_ba, rg_wx, rg_bx, rg_lambda, sc_conv_w, out_norm_g, w_out, mlp_w1, mlp_w2) = p
    dt = x.dtype
    b, t, _ = x.shape
    mod = jax.nn.silu(c) @ w_ada + b_ada
    sh1, sc1, g1, sh2, sc2, g2 = jnp.split(mod[:, None, :], 6, axis=-1)
    hn = rmsnorm(x, ln1_g) * (1.0 + sc1) + sh1
    z = hn @ w_in
    (qa, ka, va, lra, ra, gb, xb, qc, kc, vc, bd, cd, xd) = split_cols(z)

    qa = qa.reshape(b, t, GLA_HEADS, GLA_DK) * (GLA_DK ** -0.5)
    ka = ka.reshape(b, t, GLA_HEADS, GLA_DK)
    va = va.reshape(b, t, GLA_HEADS, GLA_DV)
    log_alpha = jax.nn.log_sigmoid((lra @ gla_wa2 + gla_ba).astype(jnp.float32)) / GLA_TAU
    log_alpha = log_alpha.reshape(b, t, GLA_HEADS, GLA_DK)
    chunk = CHUNK if t >= CHUNK else t
    o_a, s_gla_new = gla_chunked(s_gla, qa, ka, va, log_alpha, chunk)
    o_a = (head_rmsnorm(o_a.reshape(b, t, GROUP_W), out_norm_g[0:GROUP_W]) * jax.nn.silu(ra.astype(jnp.float32))).astype(dt)

    xcv, buf_rg_new = causal_dwconv(xb, buf_rg, rg_conv_w)
    xcv = xcv + rg_conv_b
    xblk = xcv.reshape(b, t, RG_BLOCKS, RG_BLOCK)
    r_gate = jax.nn.sigmoid(jnp.einsum('btni,nij->btnj', xblk, rg_wa).reshape(b, t, RG_W) + rg_ba)
    i_gate = jax.nn.sigmoid(jnp.einsum('btni,nij->btnj', xblk, rg_wx).reshape(b, t, RG_W) + rg_bx)
    log_a = -RG_C * r_gate.astype(jnp.float32) * jax.nn.softplus(-rg_lambda.astype(jnp.float32))
    u = jnp.sqrt(-jnp.expm1(2.0 * log_a)) * (i_gate * xcv).astype(jnp.float32)
    hs, h_rg_new = linear_scan(jnp.exp(log_a), u, h_rg.astype(jnp.float32))
    o_b = head_rmsnorm(hs * jax.nn.gelu(gb.astype(jnp.float32)), out_norm_g[GROUP_W:2 * GROUP_W]).astype(dt)

    qc = qc.reshape(b, t, SB_HEADS, SB_DH)
    kc = kc.reshape(b, t, SB_HEADS, SB_DH)
    vc = vc.reshape(b, t, SB_HEADS, SB_DH)
    p_len = k_past.shape[1]
    k_all = jnp.concatenate([k_past.astype(dt), kc], axis=1)
    v_all = jnp.concatenate([v_past.astype(dt), vc], axis=1)
    q_pos = p_len + jnp.arange(t, dtype=jnp.int32)
    k_pos = jnp.arange(p_len + t, dtype=jnp.int32)
    o_c = stick_breaking(qc, k_all, v_all, q_pos, k_pos).reshape(b, t, GROUP_W)
    o_c = head_rmsnorm(o_c, out_norm_g[2 * GROUP_W:3 * GROUP_W]).astype(dt)

    yd, buf_sc_new = causal_dwconv(cd * xd, buf_sc, sc_conv_w)
    o_d = head_rmsnorm(bd * yd, out_norm_g[3 * GROUP_W:]).astype(dt)

    mix = jnp.concatenate([o_a, o_b, o_c, o_d], axis=-1) @ w_out
    x = x + g1 * mix
    h2 = rmsnorm(x, ln2_g) * (1.0 + sc2) + sh2
    x = x + g2 * (jnp.square(jax.nn.relu(h2 @ mlp_w1)) @ mlp_w2)
    new_state = (s_gla_new.astype(dt), h_rg_new.astype(dt), buf_rg_new, kc, vc, buf_sc_new)
    return x, new_state

def setup_inputs(seed: int = 0) -> dict:
    key = jax.random.key(seed)
    k = jax.random.split(key, 30)

    def nrm(kk, shape, scale=1.0):
        return scale * jax.random.normal(kk, shape, jnp.float32)

    a0 = jax.random.uniform(k[23], (DEPTH, RG_W), jnp.float32, minval=0.9, maxval=0.999)
    s_l = a0 ** (1.0 / RG_C)
    return {
        'x_prompt': nrm(k[0], (BATCH, SEQ, D_MODEL)),
        'x_sample': nrm(k[1], (DEC_BATCH, DEC_SEQ, D_MODEL)),
        'c_prompt': nrm(k[2], (BATCH, D_MODEL)),
        'c_sample': nrm(k[3], (DEC_BATCH, D_MODEL)),
        'state_gla': nrm(k[4], (DEPTH, DEC_BATCH, GLA_HEADS, GLA_DK, GLA_DV), 0.5),
        'state_rg_h': nrm(k[5], (DEPTH, DEC_BATCH, RG_W), 0.5),
        'state_rg_conv': nrm(k[6], (DEPTH, DEC_BATCH, RG_CONV - 1, RG_W)),
        'cache_sb_k': nrm(k[7], (DEPTH, DEC_BATCH, PAST_LEN, SB_HEADS, SB_DH)),
        'cache_sb_v': nrm(k[8], (DEPTH, DEC_BATCH, PAST_LEN, SB_HEADS, SB_DH)),
        'state_sc_conv': nrm(k[9], (DEPTH, DEC_BATCH, SC_CONV - 1, SC_W)),
        'ln1_g': 1.0 + nrm(k[10], (DEPTH, D_MODEL), 0.05),
        'ln2_g': 1.0 + nrm(k[11], (DEPTH, D_MODEL), 0.05),
        'w_ada': nrm(k[12], (DEPTH, D_MODEL, 6 * D_MODEL), 0.5 * D_MODEL ** -0.5),
        'b_ada': nrm(k[13], (DEPTH, 6 * D_MODEL), 0.02),
        'w_in': nrm(k[14], (DEPTH, D_MODEL, N_IN), D_MODEL ** -0.5),
        'gla_wa2': nrm(k[15], (DEPTH, GLA_RANK, GLA_HEADS * GLA_DK), GLA_RANK ** -0.5),
        'gla_ba': nrm(k[16], (DEPTH, GLA_HEADS * GLA_DK), 0.1),
        'rg_conv_w': nrm(k[17], (DEPTH, RG_CONV, RG_W), RG_CONV ** -0.5),
        'rg_conv_b': nrm(k[18], (DEPTH, RG_W), 0.02),
        'rg_wa': nrm(k[19], (DEPTH, RG_BLOCKS, RG_BLOCK, RG_BLOCK), RG_BLOCK ** -0.5),
        'rg_ba': nrm(k[20], (DEPTH, RG_W), 0.02),
        'rg_wx': nrm(k[21], (DEPTH, RG_BLOCKS, RG_BLOCK, RG_BLOCK), RG_BLOCK ** -0.5),
        'rg_bx': nrm(k[22], (DEPTH, RG_W), 0.02),
        'rg_lambda': jnp.log(s_l) - jnp.log1p(-s_l),
        'sc_conv_w': nrm(k[24], (DEPTH, SC_CONV, SC_W), SC_CONV ** -0.5),
        'out_norm_g': 1.0 + nrm(k[25], (DEPTH, D_MODEL), 0.05),
        'w_out': nrm(k[26], (DEPTH, D_MODEL, D_MODEL), D_MODEL ** -0.5),
        'mlp_w1': nrm(k[27], (DEPTH, D_MODEL, D_FF), D_MODEL ** -0.5),
        'mlp_w2': nrm(k[28], (DEPTH, D_FF, D_MODEL), D_FF ** -0.5),
        'final_g': 1.0 + nrm(k[29], (D_MODEL,), 0.05),
    }

def reference(x_prompt, x_sample, c_prompt, c_sample, state_gla, state_rg_h, state_rg_conv,
              cache_sb_k, cache_sb_v, state_sc_conv, ln1_g, ln2_g, w_ada, b_ada, w_in,
              gla_wa2, gla_ba, rg_conv_w, rg_conv_b, rg_wa, rg_ba, rg_wx, rg_bx, rg_lambda,
              sc_conv_w, out_norm_g, w_out, mlp_w1, mlp_w2, final_g):
    dt = x_prompt.dtype
    bp = x_prompt.shape[0]
    prompt_state0 = (jnp.zeros((bp, GLA_HEADS, GLA_DK, GLA_DV), dt),
                     jnp.zeros((bp, RG_W), dt),
                     jnp.zeros((bp, RG_CONV - 1, RG_W), dt),
                     jnp.zeros((bp, 0, SB_HEADS, SB_DH), dt),
                     jnp.zeros((bp, 0, SB_HEADS, SB_DH), dt),
                     jnp.zeros((bp, SC_CONV - 1, SC_W), dt))
    xp, xs = x_prompt, x_sample
    p_new, s_new = [], []
    for l in range(DEPTH):
        params = (ln1_g[l], ln2_g[l], w_ada[l], b_ada[l], w_in[l], gla_wa2[l], gla_ba[l],
                  rg_conv_w[l], rg_conv_b[l], rg_wa[l], rg_ba[l], rg_wx[l], rg_bx[l], rg_lambda[l],
                  sc_conv_w[l], out_norm_g[l], w_out[l], mlp_w1[l], mlp_w2[l])
        xp, st_p = trunk_layer(xp, c_prompt, prompt_state0, params)
        sample_state = (state_gla[l], state_rg_h[l], state_rg_conv[l], cache_sb_k[l], cache_sb_v[l], state_sc_conv[l])
        xs, st_s = trunk_layer(xs, c_sample, sample_state, params)
        p_new.append(st_p)
        s_new.append(st_s)

    def stk(lst, i):
        return jnp.stack([st[i] for st in lst], axis=0)

    y_prompt = rmsnorm(xp, final_g)
    y_sample = rmsnorm(xs, final_g)
    return (y_prompt, y_sample,
            stk(p_new, 0), stk(s_new, 0),
            stk(p_new, 1), stk(s_new, 1),
            stk(p_new, 2), stk(s_new, 2),
            stk(p_new, 3), stk(s_new, 3),
            stk(p_new, 4), stk(s_new, 4),
            stk(p_new, 5), stk(s_new, 5))


_drawn_inputs = setup_inputs


def setup_inputs(seed=0):
    import zlib

    import numpy as np

    out = dict(_drawn_inputs(seed))
    spreads = {}
    factors = {'state_gla': 8.0,
     'cache_sb_k': 5.33,
     'cache_sb_v': 3.05,
     'state_sc_conv': 3.781,
     'rg_ba': 8.0,
     'rg_bx': 8.0,
     'out_norm_g': 3.964,
     'ln2_g': 3.542}
    for name, (base, spread) in spreads.items():
        noise = np.random.default_rng([zlib.crc32(name.encode()), seed]).standard_normal(out[name].shape)
        drawn = base * np.exp(spread * noise) if base else spread * noise
        out[name] = __import__('jax').numpy.asarray(drawn.astype(out[name].dtype))
    for name, factor in factors.items():
        out[name] = (out[name] * factor).astype(out[name].dtype)
    return out
```

```python
from contextlib import ExitStack

import concourse.bass as bass
from concourse import mybir

ALU = mybir.AluOpType
ACT = mybir.ActivationFunctionType
F32 = mybir.dt.float32
F32R = mybir.dt.float32r

EXP_LN = "natural_log_exp_and_others"
P = 128
D_MODEL = 1024
KT = D_MODEL // P
SEQ = 2048
DEC = 64
PAST = 512
N_TOK = SEQ + DEC
BLK = 512
NBLK = SEQ // BLK
TPB = BLK // P
GW = D_MODEL // 4
HD = 64
HEADS = GW // HD
GLA_DK = 32
CHUNK = 64
CPB = BLK // CHUNK
RANK = 16
D_FF = 4 * D_MODEL
EPS = 1e-6
RG_C = 8.0
GLA_TAU = 16.0
NEG = -1e30

OFF_QA, OFF_KA, OFF_VA, OFF_LRA, OFF_RA, OFF_GB, OFF_XB = 0, 128, 256, 512, 528, 784, 1040
OFF_QC, OFF_KC, OFF_VC, OFF_BD, OFF_CD, OFF_XD = 1296, 1552, 1808, 2064, 2320, 2576

STRIPS_A = [("qa", 0, OFF_QA), ("ka", 0, OFF_KA), ("va", 0, OFF_VA), ("va", 1, OFF_VA + P),
            ("ra", 0, OFF_RA), ("ra", 1, OFF_RA + P)]
STRIPS_C = [(n, j, o + j * P) for n, o in (("qc", OFF_QC), ("kc", OFF_KC), ("vc", OFF_VC)) for j in range(2)]
STRIPS_B = [(n, j, o + j * P) for n, o in (("gb", OFF_GB), ("xb", OFF_XB)) for j in range(2)]
STRIPS_D = [(n, j, o + j * P) for n, o in (("cd", OFF_CD), ("xd", OFF_XD), ("bd", OFF_BD)) for j in range(2)]
STRIPS_IN = STRIPS_A + STRIPS_C + STRIPS_B + STRIPS_D
N_IN_STRIPS = len(STRIPS_IN)
N_STRIPS = N_IN_STRIPS + KT

ZP_LRA = 0
ZP_A = 1
ZP_C = ZP_A + 6
ZP_Y = ZP_C + 6
ZP_B = ZP_Y + 1
ZP_D = ZP_B + 4
ZP_G = ZP_D + 6
ZP_O = ZP_G + 4
ZP_MIX = ZP_O + 2
ZP_PER = ZP_MIX + KT
STRIP_USE = ([ZP_A + i for i in range(6)] + [ZP_C + i for i in range(6)] + [ZP_B + i for i in range(4)]
             + [ZP_D + i for i in range(6)] + [ZP_MIX + i for i in range(KT)])
TP_X = 0
TP_K = KT
TP_V = TP_K + 2
TP_VA = TP_V + 2
TP_KD = TP_VA + 2
TP_PER = TP_KD + 2
NORM_ORDER = [6, 7, 2, 3, 0, 1, 4, 5]
ST_PER = 1 + len(NORM_ORDER)
SQ_PER = KT + len(NORM_ORDER)
assert ZP_PER % 2 == 0 and TP_PER % 2 == 0 and N_STRIPS % 2 == 0

R1_BADA, R1_CP, R1_CS = 0, 48, 56
R2_LN1, R2_LN2, R2_FIN, R2_ON, R2_GBA = 0, 8, 16, 24, 32
R2_RCW, R2_RCB, R2_RBA, R2_RBX, R2_LAM, R2_SCW = 33, 41, 43, 45, 47, 49
R2_H, R2_RBUF, R2_SBUF, R2_ALL = 55, 57, 63, 67
M_SH1, M_SC1, M_G1, M_SH2, M_SC2, M_G2 = 0, 8, 16, 24, 32, 40


def wait(eng, sem, value):
    if not (isinstance(value, int) and value <= 0):
        eng.wait_ge(sem, value)


class Chain:

    def __init__(self, eng, sem):
        self.eng, self.sem, self.base, self.n = eng, sem, 0, 0

    def at(self, base):
        self.base, self.n = base, 0

    def link(self, ins):
        self.n += 1
        ins.then_inc(self.sem, 1)
        self.eng.wait_ge(self.sem, self.base + self.n)


def build(nc, x_prompt, x_sample, c_prompt, c_sample, state_gla, state_rg_h, state_rg_conv,
          cache_sb_k, cache_sb_v, state_sc_conv, ln1_g, ln2_g, w_ada, b_ada, w_in, gla_wa2, gla_ba,
          rg_conv_w, rg_conv_b, rg_wa, rg_ba, rg_wx, rg_bx, rg_lambda, sc_conv_w, out_norm_g, w_out,
          mlp_w1, mlp_w2, final_g, y_prompt, y_sample, gla_p, gla_s, rgh_p, rgh_s, rgc_p, rgc_s,
          sbk_p, sbk_s, sbv_p, sbv_s, scc_p, scc_s):
    x1_dram = nc.dram_tensor("x1_scratch", (D_MODEL, N_TOK), F32, kind="Internal").ap()
    x1_v = x1_dram.rearrange("(f p) t -> p f t", p=P)
    with ExitStack() as ctx:
        def sb(name, shape, dt=F32):
            return ctx.enter_context(nc.sbuf_tensor(name, shape, dt))

        const = dict(
            ident=sb("ident", [P, P]), ones=sb("ones", [P, P]), head_ones=sb("head_ones", [P, P]),
            prm1=sb("prm1", [P, 64]), prm2=sb("prm2", [P, R2_ALL]), modT=sb("modT", [P, 48, 2]),
            gs1=sb("gs1", [P, KT, 2]), gs2=sb("gs2", [P, KT, 2]), eps=sb("eps", [P, 1]))
        mix_ctx = ExitStack()
        with mix_ctx:
            def mb(name, shape, dt=F32):
                return mix_ctx.enter_context(nc.sbuf_tensor(name, shape, dt))

            mixc = dict(
                neg_mask=mb("neg_mask", [P, P]), bd_mask=mb("bd_mask", [P, 2 * P]),
                scan_mask=mb("scan_mask", [P, BLK]), rgw=mb("rgw", [P, 2, 2, P]), c8=mb("c8", [P, 2, 2]),
                wa2=mb("wa2", [RANK, P]), lra_hi=mb("lra_hi", [P, KT * RANK + P], F32R),
                lra_lo=mb("lra_lo", [P, KT * RANK + P], F32R))
            setup_phase(nc, const, mixc, c_prompt, c_sample, w_ada, b_ada, w_in, ln1_g, ln2_g, final_g,
                        out_norm_g, gla_ba, gla_wa2, rg_conv_w, rg_conv_b, rg_wa, rg_ba, rg_wx, rg_bx,
                        rg_lambda, sc_conv_w, state_rg_h, state_rg_conv, state_sc_conv)
            mixer_phase(nc, const, mixc, x_prompt, x_sample, state_gla, cache_sb_k, cache_sb_v, w_in, w_out,
                        x1_v, gla_p, gla_s, rgh_p, rgh_s, rgc_p, rgc_s, sbk_p, sbk_s, sbv_p, sbv_s,
                        scc_p, scc_s)
        mlp_phase(nc, const, x1_v, mlp_w1, mlp_w2, y_prompt, y_sample)


def setup_phase(nc, const, mixc, c_prompt, c_sample, w_ada, b_ada, w_in, ln1_g, ln2_g, final_g,
                out_norm_g, gla_ba, gla_wa2, rg_conv_w, rg_conv_b, rg_wa, rg_ba, rg_wx, rg_bx,
                rg_lambda, sc_conv_w, state_rg_h, state_rg_conv, state_sc_conv):
    CH = 512
    NCH = 6 * D_MODEL // CH
    CT = CH // P
    with ExitStack() as ctx:
        def sb(name, shape, dt=F32):
            return ctx.enter_context(nc.sbuf_tensor(name, shape, dt))

        def sem(name):
            return ctx.enter_context(nc.semaphore(name))

        rows1, rows2 = sb("rows1", [64, P]), sb("rows2", [R2_ALL, P])
        wada = [sb(f"wada{i}", [P, KT, CH]) for i in range(2)]
        lra_raw = sb("lra_raw", [P, KT * RANK])
        csil = sb("csil", [P, 2, KT])
        lam = sb("lam", [P, 4, 2])
        pt = ctx.enter_context(nc.psum_tensor("pt", [P, 2, 512], F32))
        pm = ctx.enter_context(nc.psum_tensor("pm", [P, 48, 2], F32))
        rows_in, wada_in = sem("rows_in"), [sem("wada_in0"), sem("wada_in1")]
        wada_used, zeroed, blocks_in, masks = sem("wada_used"), sem("zeroed"), sem("blocks_in"), sem("masks")
        rows_t, prm, silu_c, mod_full = sem("rows_t"), sem("prm"), sem("silu_c"), sem("mod_full")
        act_chain, dve_chain, lra_hi_ok, lra_in, lam_a = (
            sem("act_chain"), sem("dve_chain"), sem("lra_hi_ok"), sem("lra_in"), sem("lam_a"))
        wa_v = w_ada[0].rearrange("(k p) n -> p k n", p=P)
        block = ctx.enter_context(nc.Block())

        def rows(v):
            return v.rearrange("a (r p) -> (a r) p", p=P)

        @block.sync
        def _(sp):
            parts1 = [(R1_BADA, rows(b_ada)), (R1_CP, rows(c_prompt)), (R1_CS, rows(c_sample))]
            parts2 = [(R2_LN1, rows(ln1_g)), (R2_LN2, rows(ln2_g)),
                      (R2_FIN, final_g.rearrange("(r p) -> r p", p=P)), (R2_ON, rows(out_norm_g)),
                      (R2_GBA, rows(gla_ba)), (R2_RCW, rows(rg_conv_w[0])), (R2_RCB, rows(rg_conv_b)),
                      (R2_RBA, rows(rg_ba)), (R2_RBX, rows(rg_bx)), (R2_LAM, rows(rg_lambda)),
                      (R2_SCW, rows(sc_conv_w[0])), (R2_H, rows(state_rg_h[0])),
                      (R2_RBUF, rows(state_rg_conv[0, 0])), (R2_SBUF, rows(state_sc_conv[0, 0]))]
            for tile, parts in ((rows1, parts1), (rows2, parts2)):
                for r, src in parts:
                    sp.dma_start(tile[r:r + src.shape[0], :], src).then_inc(rows_in, 16)
            for c in range(NCH):
                wait(sp, wada_used, c - 1)
                sp.dma_start(wada[c % 2][:, :, :], wa_v[:, :, c * CH:(c + 1) * CH]).then_inc(wada_in[c % 2], 16)
                if c == 1:
                    sp.dma_start(lra_raw[:, :].rearrange("p (k n) -> p k n", n=RANK),
                                 w_in[0].rearrange("(k p) n -> p k n", p=P)[:, :, OFF_LRA:OFF_LRA + RANK]
                                 ).then_inc(lra_in, 16)
                    sp.dma_start(mixc["wa2"][:, :], gla_wa2[0]).then_inc(blocks_in, 16)
                    sp.wait_ge(zeroed, 1)
                    for n in range(4):
                        for g, w in enumerate((rg_wa, rg_wx)):
                            sp.dma_start(mixc["rgw"][64 * (n % 2):64 * (n % 2) + 64, g, n // 2,
                                                     64 * (n % 2):64 * (n % 2) + 64], w[0, n]).then_inc(blocks_in, 16)
            sp.wait_ge(blocks_in, 16 * 9)

        @block.gpsimd
        def _(pool):
            n = [0]

            def step(ins):
                n[0] += 1
                ins.then_inc(masks, 1)
                pool.wait_ge(masks, n[0])

            pool.memset(mixc["rgw"][:, :, :, :], 0.0).then_inc(zeroed, 1)
            step(pool.memset(const["ident"][:, :], 0.0))
            step(pool.affine_select(out=const["ident"][:, :], in_=const["ident"][:, :], compare_op=ALU.not_equal,
                                    fill=1.0, base=0, pattern=[[-1, P]], channel_multiplier=1))
            step(pool.memset(const["ones"][:, :], 1.0))
            step(pool.memset(const["eps"][:, :], EPS))
            step(pool.memset(const["head_ones"][:, :], 0.0))
            for i in range(2):
                step(pool.memset(const["head_ones"][64 * i:64 * i + 64, 64 * i:64 * i + 64], 1.0))
            step(pool.memset(mixc["bd_mask"][:, :], 0.0))
            for h in range(HEADS):
                step(pool.memset(mixc["bd_mask"][32 * h:32 * h + 32, HD * h:HD * h + HD], 1.0))
            step(pool.memset(mixc["scan_mask"][:, :], 1.0))
            step(pool.memset(mixc["scan_mask"][:, 0:BLK:CHUNK], 0.0))
            step(pool.memset(mixc["neg_mask"][:, :], 0.0))
            step(pool.affine_select(out=mixc["neg_mask"][:, :], in_=mixc["neg_mask"][:, :], compare_op=ALU.is_ge,
                                    fill=NEG, base=-1, pattern=[[-1, P]], channel_multiplier=1))

        @block.scalar
        def _(act):
            chain = Chain(act, act_chain)
            act.wait_ge(prm, 1)
            act.activation(csil[:, :, :], const["prm1"][:, R1_CP:64].rearrange("p (c k) -> p c k", c=2),
                           ACT.Silu).then_inc(silu_c, 1)
            act.wait_ge(lra_in, 16)
            act.activation(mixc["lra_hi"][:, 0:KT * RANK], lra_raw[:, :], ACT.Copy).then_inc(lra_hi_ok, 1)
            act.wait_ge(prm, 2)
            chain.link(act.activation(lam[:, 0, :], const["prm2"][:, R2_LAM:R2_LAM + 2], ACT.Abs))
            chain.link(act.activation(lam[:, 1, :], lam[:, 0, :], ACT.Exp, scale=-1.0))
            act.activation(lam[:, 2, :], lam[:, 1, :], ACT.Ln, bias=1.0).then_inc(lam_a, 1)

        @block.vector
        def _(dve):
            chain = Chain(dve, dve_chain)
            chain.link(dve.memset(mixc["lra_hi"][:, KT * RANK:].bitcast(F32), 0.0))
            chain.link(dve.memset(mixc["lra_lo"][:, KT * RANK:].bitcast(F32), 0.0))
            dve.wait_ge(rows_t, 1)
            dve.tensor_copy(const["prm1"][:, :], pt[:, 0, 0:64]).then_inc(prm, 1)
            dve.wait_ge(rows_t, 2)
            dve.tensor_copy(const["prm2"][:, :], pt[:, 1, 0:R2_ALL]).then_inc(prm, 1)
            dve.wait_ge(lra_hi_ok, 1)
            dve.tensor_tensor(mixc["lra_lo"][:, 0:KT * RANK], lra_raw[:, :],
                              mixc["lra_hi"][:, 0:KT * RANK].bitcast(F32), ALU.subtract)
            dve.wait_ge(prm, 2)
            chain.link(dve.tensor_scalar(lam[:, 3, :], const["prm2"][:, R2_LAM:R2_LAM + 2], -1.0, 0.0,
                                         ALU.mult, ALU.max))
            dve.wait_ge(lam_a, 1)
            chain.link(dve.tensor_tensor(lam[:, 3, :], lam[:, 3, :], lam[:, 2, :], ALU.add))
            chain.link(dve.tensor_scalar(mixc["c8"][:, 0, :], lam[:, 3, :], -RG_C, None, ALU.mult))
            chain.link(dve.tensor_scalar(mixc["c8"][:, 1, :], lam[:, 3, :], RG_C, None, ALU.mult))
            dve.wait_ge(mod_full, 1)
            for c in range(2):
                chain.link(dve.tensor_tensor(const["modT"][:, :, c], pm[:, :, c],
                                             const["prm1"][:, R1_BADA:R1_BADA + 48], ALU.add))
            for gs, m, g in ((const["gs1"], M_SC1, R2_LN1), (const["gs2"], M_SC2, R2_LN2)):
                for c in range(2):
                    chain.link(dve.scalar_tensor_tensor(
                        out=gs[:, :, c], in0=const["modT"][:, m:m + KT, c], scalar=1.0,
                        in1=const["prm2"][:, g:g + KT], op0=ALU.add, op1=ALU.mult))

        @block.tensor
        def _(pe):
            pe.wait_ge(rows_in, 16 * 17)
            pe.wait_ge(masks, 2)
            pe.transpose(pt[:, 0, 0:64], rows1[:, :], const["ident"][0:64, 0:64]).then_inc(rows_t, 1)
            pe.transpose(pt[:, 1, 0:R2_ALL], rows2[:, :], const["ident"][0:R2_ALL, 0:R2_ALL]).then_inc(rows_t, 1)
            pe.wait_ge(silu_c, 1)
            for c in range(NCH):
                pe.wait_ge(wada_in[c % 2], 16 * (c // 2 + 1))
                for t in range(CT):
                    for k in range(KT):
                        mm = pe.matmul(pm[:, c * CT + t, :], wada[c % 2][:, k, t * P:(t + 1) * P], csil[:, :, k],
                                       start=(k == 0), stop=(k == KT - 1))
                mm.then_inc(wada_used, 1)
            mm = pe.matmul(pt[0:2, 0, 0:2], csil[:, :, 0], csil[:, :, 0], start=True, stop=True)
            mm.then_inc(mod_full, 1)


def mixer_phase(nc, const, mixc, x_prompt, x_sample, state_gla, cache_sb_k, cache_sb_v, w_in, w_out,
                x1_v, gla_p, gla_s, rgh_p, rgh_s, rgc_p, rgc_s, sbk_p, sbk_s, sbv_p, sbv_s, scc_p, scc_s):
    prm2, modT, gs1 = const["prm2"], const["modT"], const["gs1"]
    ident, ones, head_ones, eps = const["ident"], const["ones"], const["head_ones"], const["eps"]
    with ExitStack() as ctx:
        def sb(name, shape, dt=F32):
            return ctx.enter_context(nc.sbuf_tensor(name, shape, dt))

        def sem(name):
            return ctx.enter_context(nc.semaphore(name))

        xT = sb("xT", [P, KT, BLK])
        halves_at = nc.sbuf_base
        hn_hi, hn_lo = sb("hn_hi", [P, KT, BLK], F32R), sb("hn_lo", [P, KT, BLK], F32R)
        oT = sb("oT", [P, KT, BLK])
        xrow = oT[:, :, :].rearrange("p k n -> p (k n)").rearrange("p (i n) -> p i n", n=D_MODEL)
        Kt = sb("Kt", [P, 2, SEQ])
        Vb = sb("Vb", [P, SEQ // P, GW])
        qp = sb("qp", [P, HEADS, BLK])
        kst = sb("kst", [P, 2, BLK])
        vst = sb("vst", [P, 2, BLK])
        gb = vst
        qa, ka = sb("qa", [P, BLK]), sb("ka", [P, BLK])
        va = sb("va", [P, 2, BLK])
        cd = va
        ra = sb("ra", [P, 2, BLK])
        lra = sb("lra", [RANK, BLK])
        bd = sb("bd", [P, 2, BLK])
        vtok = bd[:, :, :].rearrange("p j n -> p (j n)").rearrange("p (i c) -> p i c", c=GW)
        cxp = sb("cxp", [P, 2, BLK + 2])
        xbp = sb("xbp", [P, 2, BLK + 3])
        xcv = sb("xcv", [P, 2, BLK])
        ktok = xcv[:, :, :].rearrange("p j n -> p (j n)").rearrange("p (i c) -> p i c", c=GW)
        tmp = [sb(f"tmp{i}", [P, BLK]) for i in range(4)]
        S = sb("S", [P, CPB, 2 * P])
        kdt = sb("kdt", [P, TPB, P])
        vt = sb("vt", [P, TPB, GW])
        dec = sb("dec", [P, CPB])
        sq = [sb(f"sq{i}", [P, BLK]) for i in range(2)]
        rsh = [sb(f"rsh{i}", [P, BLK]) for i in range(2)]
        hst = sb("hst", [P, 2])
        stout = sb("stout", [P, 12])
        strow = sb("strow", [12, P])
        carry = sb("carry", [P, TPB * HEADS])
        wraw = [sb(f"wraw{i}", [P, KT, P]) for i in range(2)]
        w_hi = [sb(f"w_hi{i}", [P, KT, P], F32R) for i in range(2)]
        w_lo = [sb(f"w_lo{i}", [P, KT, P], F32R) for i in range(2)]
        att = nc.alloc_sbuf_tensor_at("att", [P, 2 * KT, BLK], F32, offset=halves_at)
        aR, aW, aT = ([att[:, at + 2 * i:at + 2 * i + 2, :] for i in range(2)] for at in (0, 4, 8))
        aC = osb = att[:, 12:14, :]
        um = att[:, 14, 0:GW]

        def banks(name):
            return ctx.enter_context(nc.psum_tensor(name, [P, 2, 512], F32))

        zp2, tp2, zs2, ob2 = banks("zp"), banks("tp"), banks("zs"), banks("ob")
        zp, tp, zs = ([v[:, i, :] for i in range(2)] for v in (zp2, tp2, zs2))
        ob, st = ob2[:, 0, :], ob2[:, 1, :]
        score_banks = [zs2, zp2]

        x_loaded, tp_full, tp_free = sem("x_loaded"), sem("tp_full"), sem("tp_free")
        zp_full, zp_free, st_free, dh_ready = sem("zp_full"), sem("zp_free"), sem("st_free"), sem("dh_ready")
        sq_ready, sq_used = sem("sq_ready"), sem("sq_used")
        rs_ready, norm_done = sem("rs_ready"), sem("norm_done")
        hf_ready, hi_ready, lo_ready = sem("hf_ready"), sem("hi_ready"), sem("lo_ready")
        w_in_sem = [sem("w_loaded0"), sem("w_loaded1")]
        w_hi_ready, w_lo_ready = sem("w_hi_ready"), sem("w_lo_ready")
        y_ready, gd_ready, kdec_ready, kd_ready = sem("y_ready"), sem("gd_ready"), sem("kdec_ready"), sem("kd_ready")
        u_full, u_used, s_ready = sem("u_full"), sem("u_used"), sem("s_ready")
        xcv_ready, halo_ready = sem("xcv_ready"), sem("halo_ready")
        rgate, rg_u, rg_sqrt, rg_done = sem("rgate"), sem("rg_u"), sem("rg_sqrt"), sem("rg_done")
        gelu_ready, silu_ready, d_ready = sem("gelu_ready"), sem("silu_ready"), sem("d_ready")
        kst_placed, ktok_stored, v_placed = sem("kst_placed"), sem("ktok_stored"), sem("v_placed")
        oh_ready, ol_ready, mixed, x1_ready, x1_stored = (
            sem("oh_ready"), sem("ol_ready"), sem("mixed"), sem("x1_ready"), sem("x1_stored"))
        sc_full, l_ready, x_done, w_ready, wtp_full, wt_ready, pv_done = (
            sem("sc_full"), sem("l_ready"), sem("x_done"), sem("w_ready"), sem("wtp_full"),
            sem("wt_ready"), sem("pv_done"))
        osb_ready, ot_full, ot_done = sem("osb_ready"), sem("ot_full"), sem("ot_done")
        act_c, act_a, dve_c, dve_a = sem("act_c"), sem("act_a"), sem("dve_c"), sem("dve_a")
        init_ok, q_zero, state_in, past_in, halo_zero, stout_ready, strow_full, strow_ready, out_stored = (
            sem("init_ok"), sem("q_zero"), sem("state_in"), sem("past_in"), sem("halo_zero"), sem("stout_ready"),
            sem("strow_full"), sem("strow_ready"), sem("out_stored"))

        win_v = w_in[0].rearrange("(k p) n -> p k n", p=P)
        wout_v = w_out[0].rearrange("(k p) n -> p k n", p=P)
        pastk_v = cache_sb_k[0, 0].rearrange("(i p) h d -> p i (h d)", p=P)
        pastv_v = cache_sb_v[0, 0].rearrange("(i p) h d -> p i (h d)", p=P)

        def strip_src(u):
            return win_v[:, :, STRIPS_IN[u][2]:STRIPS_IN[u][2] + P] if u < N_IN_STRIPS else \
                wout_v[:, :, (u - N_IN_STRIPS) * P:(u - N_IN_STRIPS + 1) * P]

        PAIRS = 2 * TPB

        def pairs_before(b):
            return (PAIRS // 2) * b * (b + 1)

        def pairs_after(b, sample):
            return N_PAIRS + 4 if sample else pairs_before(b) + PAIRS * (b + 1)

        N_PAIRS = pairs_before(NBLK)
        block = ctx.enter_context(nc.Block())

        def tp_base(b, sample):
            return b * TP_PER + (2 if sample else 0)

        def shape_of(sample):
            return (DEC, 1, 1, DEC) if sample else (BLK, TPB, CPB, P)

        def attend(eng, b, sample, key_block):
            rows = shape_of(sample)[3]
            q = N_PAIRS if sample else pairs_before(b)
            key_block(q, lambda s: rows * (s + 1), True, lambda: 1 if sample else b * -1 + (NBLK - 1))
            if sample:
                key_block(q + 2, lambda s: PAST, False, lambda: 0)
            elif not isinstance(b, int):
                with eng.Fori(1, b + 1) as c:
                    key_block(q + PAIRS * c, lambda s: BLK, False, lambda: nc.s_assert_within(
                        b * -1 + c + (NBLK - 1), 0, NBLK - 1, skip_runtime_bounds_check_because="c <= b"))

        @block.sync
        def _(sp):
            def store_states(gla, rgh, rgc, scc, n, last_step):
                sp.wait_ge(s_ready, last_step)
                slot = (CPB - 1) if n == 0 else 0
                for h in range(HEADS):
                    sp.dma_start(gla[0, 0, h], S[32 * h:32 * h + 32, slot, HD * h:HD * h + HD]).then_inc(out_stored, 16)
                sp.wait_ge(strow_ready, n + 1)
                sp.dma_start(rgh[0].rearrange("a (j p) -> (a j) p", p=P), strow[0:2, :]).then_inc(out_stored, 16)
                sp.dma_start(rgc[0, 0].rearrange("i (j p) -> (i j) p", p=P), strow[2:8, :]).then_inc(out_stored, 16)
                sp.dma_start(scc[0, 0].rearrange("i (j p) -> (i j) p", p=P), strow[8:12, :]).then_inc(out_stored, 16)

            def load_strip(g, u):
                wait(sp, w_hi_ready, g - 1)
                wait(sp, w_lo_ready, g - 1)
                sp.dma_start(wraw[u % 2][:, :, :], strip_src(u)).then_inc(w_in_sem[u % 2], 16)

            def body(b, sample):
                wait(sp, oh_ready, b * KT)
                wait(sp, ol_ready, b * KT)
                if sample:
                    sp.dma_start(xrow[0:DEC, 0, :], x_sample[0]).then_inc(x_loaded, 16)
                else:
                    sp.dma_start(xrow[:, :, :], x_prompt[0, bass.ds(b * BLK, BLK), :].rearrange("(i p) n -> p i n", p=P)
                                 ).then_inc(x_loaded, 16)
                for u in range(2, N_STRIPS if sample else N_STRIPS + 2):
                    load_strip(b * N_STRIPS + u, u % N_STRIPS)

            load_strip(0, 0)
            load_strip(1, 1)
            body(0, False)
            with sp.Fori(1, NBLK) as b:
                body(b, False)
            store_states(gla_p, rgh_p, rgc_p, scc_p, 0, NBLK * CPB)
            sp.wait_ge(out_stored, 16 * (HEADS + 3))
            sp.wait_ge(init_ok, 2)
            for h in range(HEADS):
                sp.dma_start(S[32 * h:32 * h + 32, CPB - 1, HD * h:HD * h + HD], state_gla[0, 0, h]).then_inc(state_in, 16)
            sp.wait_ge(pv_done, N_PAIRS)
            sp.dma_start(Vb[:, 0:PAST // P, :], pastv_v).then_inc(past_in, 16)
            sp.dma_start(ktok[:, :, :], pastk_v).then_inc(past_in, 16)
            sp.wait_ge(past_in, 32)
            body(NBLK, True)
            store_states(gla_s, rgh_s, rgc_s, scc_s, 1, NBLK * CPB + 1)
            sp.wait_ge(out_stored, 32 * (HEADS + 3))
            sp.wait_ge(x1_stored, 16 * KT * (NBLK + 1))
            sp.wait_ge(ktok_stored, 16 * (NBLK + 1))
            sp.wait_ge(v_placed, 32 * (NBLK + 1))
            sp.wait_ge(kst_placed, 16 * (NBLK + 1))

        @block.gpsimd
        def _(pool):
            pool.memset(qp[:, :, :], 0.0).then_inc(q_zero, 1)

            def strip_lo(g, slot, used):
                pool.wait_ge(w_hi_ready, g + 1)
                wait(pool, zp_full, used)
                pool.tensor_tensor(w_lo[slot][:, :, :], wraw[slot][:, :, :], w_hi[slot][:, :, :].bitcast(F32),
                                   ALU.subtract).then_inc(w_lo_ready, 1)

            def body(b, sample):
                n = shape_of(sample)[0]
                for f in range(KT):
                    pool.wait_ge(hi_ready, b * KT + f + 1)
                    pool.tensor_tensor(hn_lo[:, f, 0:n], tmp[f % 2][:, 0:n], hn_hi[:, f, 0:n].bitcast(F32),
                                       ALU.subtract).then_inc(lo_ready, 1)
                for u in range(N_STRIPS):
                    if u == N_IN_STRIPS:
                        for f in range(KT):
                            pool.wait_ge(oh_ready, b * KT + f + 1)
                            pool.tensor_tensor(hn_lo[:, f, 0:n], oT[:, f, 0:n], hn_hi[:, f, 0:n].bitcast(F32),
                                               ALU.subtract).then_inc(ol_ready, 1)
                    if not (sample and u >= N_STRIPS - 2):
                        strip_lo(b * N_STRIPS + u + 2, u % 2, b * ZP_PER + STRIP_USE[u] + 1)

            strip_lo(0, 0, 0)
            strip_lo(1, 1, 0)
            body(0, False)
            with pool.Fori(1, NBLK) as b:
                body(b, False)
            body(NBLK, True)

        act_links = {}

        @block.scalar
        def _(act):
            chain, achain = Chain(act, act_c), Chain(act, act_a)

            def strip_hi(g, slot, loads, used):
                act.wait_ge(w_in_sem[slot], 16 * loads)
                wait(act, zp_full, used)
                act.activation(w_hi[slot][:, :, :], wraw[slot][:, :, :], ACT.Copy).then_inc(w_hi_ready, 1)

            def body(b, sample):
                n, tiles, chunks, rows = shape_of(sample)
                m = 1 if sample else 0
                chain.at(b * act_links.get("block", 0))
                zb, tb, qb = b * ZP_PER, tp_base(b, sample), b * SQ_PER

                def evac(u, dst, src=None, func=ACT.Copy, **more):
                    act.wait_ge(zp_full, zb + u + 1)
                    src = zp[u % 2][:, 0:n] if src is None else src
                    return act.activation(dst, src, func, **more)

                def evac_tp(u, dst, src):
                    act.wait_ge(tp_full, tb + u + 1)
                    act.activation(dst, src, ACT.Copy).then_inc(tp_free, 1)

                def next_hi(u):
                    if not (sample and u + 2 >= N_STRIPS):
                        strip_hi(b * N_STRIPS + u + 2, u % 2, b * (N_STRIPS // 2) + (u + 2) // 2 + 1,
                                 zb + STRIP_USE[u] + 1)

                def norm(k):
                    t = NORM_ORDER[k]
                    wait(act, sq_used, qb + KT + k - 1)
                    act.activation(sq[k % 2][:, 0:n], oT[:, t, 0:n], ACT.Square).then_inc(sq_ready, 1)
                    act.wait_ge(sq_used, qb + KT + k + 1)
                    wait(act, norm_done, b * KT + k - 1)
                    act.activation(rsh[k % 2][:, 0:n], st[:, 0:n], ACT.Ln, scale=1.0 / HD,
                                   bias=eps[:, 0:1]).then_inc(st_free, 1)
                    act.wait_ge(st_free, b * ST_PER + k + 2)
                    act.activation(rsh[k % 2][:, 0:n], rsh[k % 2][:, 0:n], ACT.Exp, scale=-0.5).then_inc(rs_ready, 1)

                act.preload_act_table_set(EXP_LN)
                wait(act, x1_stored, 16 * KT * b)
                wait(act, norm_done, b * KT)
                for f in range(KT):
                    act.wait_ge(tp_full, tb + TP_X + f + 1)
                    wait(act, sq_used, qb + f - 1)
                    act.activation(sq[f % 2][:, 0:n], tp[f % 2][:, 0:n], ACT.Square).then_inc(sq_ready, 1)
                    act.activation(xT[:, f, 0:n], tp[f % 2][:, 0:n], ACT.Copy).then_inc(tp_free, 1)
                act.wait_ge(sq_used, qb + KT)
                act.activation(tmp[2][:, 0:n], st[:, 0:n], ACT.Ln, scale=1.0 / D_MODEL,
                               bias=eps[:, 0:1]).then_inc(st_free, 1)
                act.wait_ge(st_free, b * ST_PER + 1)
                act.activation(tmp[2][:, 0:n], tmp[2][:, 0:n], ACT.Exp, scale=-0.5).then_inc(rs_ready, 1)
                for f in range(KT):
                    act.wait_ge(hf_ready, b * KT + f + 1)
                    act.activation(hn_hi[:, f, 0:n], tmp[f % 2][:, 0:n], ACT.Copy).then_inc(hi_ready, 1)

                evac(ZP_LRA, lra[:, 0:n], zp[ZP_LRA % 2][0:RANK, 0:n]).then_inc(zp_free, 1)
                dst_a = [qa[:, 0:n], ka[:, 0:n], va[:, 0, 0:n], va[:, 1, 0:n], ra[:, 0, 0:n], ra[:, 1, 0:n]]
                for i in range(6):
                    evac(ZP_A + i, dst_a[i], scale=GLA_DK ** -0.5 if i == 0 else 1.0).then_inc(zp_free, 1)
                    next_hi(i)
                act.wait_ge(q_zero, 1)
                for i in range(6):
                    u, j = ZP_C + i, i % 2
                    if i < 2:
                        evac(u, qp[0:HD, 2 * j, 0:n], zp[u % 2][0:HD, 0:n], scale=HD ** -0.5)
                        evac(u, qp[HD:P, 2 * j + 1, 0:n], zp[u % 2][HD:P, 0:n], scale=HD ** -0.5).then_inc(zp_free, 1)
                    else:
                        if i == 2:
                            wait(act, kst_placed, 16 * b)
                            wait(act, rg_done, 2 * b)
                        evac(u, (kst if i < 4 else vst)[:, j, 0:n]).then_inc(zp_free, 1)
                    next_hi(6 + i)
                gba = prm2[:, R2_GBA:R2_GBA + 1]
                evac(ZP_Y, tmp[3][:, 0:n], func=ACT.Abs, bias=gba)
                evac(ZP_Y, tmp[2][:, 0:n], func=ACT.Identity, bias=gba).then_inc(zp_free, 1)
                act.wait_ge(zp_free, zb + ZP_Y + 1)
                chain.link(act.activation(tmp[3][:, 0:n], tmp[3][:, 0:n], ACT.Exp, scale=-1.0))
                act.activation(tmp[3][:, 0:n], tmp[3][:, 0:n], ACT.Ln, bias=1.0).then_inc(y_ready, 1)
                for u0, dst in ((TP_K, ktok), (TP_V, vtok), (TP_VA, vt)):
                    for j in range(2):
                        evac_tp(u0 + j, dst[0:rows, 0:tiles, j * P:(j + 1) * P],
                                tp[j][0:rows, 0:tiles * P].rearrange("p (i c) -> p i c", c=P))
                pos = 1 if sample else b * -1 + (NBLK - 1)
                act.wait_ge(tp_free, tb + TP_V + 2)
                act.dma_start(Kt[:, :, bass.ds(pos * BLK, n)], kst[:, :, 0:n]).then_inc(kst_placed, 16)
                if sample:
                    act.dma_start(sbk_s[0, 0].rearrange("t h d -> t (h d)"), ktok[0:DEC, 0, :]).then_inc(ktok_stored, 16)
                    act.dma_start(sbv_s[0, 0].rearrange("t h d -> t (h d)"), vtok[0:DEC, 0, :]).then_inc(v_placed, 16)
                    act.dma_start(Vb[0:DEC, TPB, :], vtok[0:DEC, 0, :]).then_inc(v_placed, 16)
                else:
                    for out, tok, done in ((sbk_p, ktok, ktok_stored), (sbv_p, vtok, v_placed)):
                        act.dma_start(out[0, 0, bass.ds(b * BLK, BLK)].rearrange("(i p) h d -> p i (h d)", p=P),
                                      tok[:, :, :]).then_inc(done, 16)
                    act.dma_start(Vb[:, bass.ds(pos * TPB, TPB), :], vtok[:, :, :]).then_inc(v_placed, 16)
                act.wait_ge(gd_ready, b + 1)
                act.activation(dec[:, 0:chunks], tmp[3][:, CHUNK - 1:n:CHUNK], ACT.Exp, scale=1.0 / GLA_TAU)
                act.activation(tmp[2][:, 0:n], tmp[2][:, 0:n], ACT.Exp, scale=1.0 / GLA_TAU).then_inc(kdec_ready, 1)
                act.wait_ge(halo_ready, b + 1)
                dst_b = [gb[:, 0, 0:n], gb[:, 1, 0:n], xbp[:, 0, 3:3 + n], xbp[:, 1, 3:3 + n]]
                for i in range(4):
                    evac(ZP_B + i, dst_b[i]).then_inc(zp_free, 1)
                    next_hi(12 + i)
                for i in range((tiles + 1) // 2):
                    w = min(2, tiles)
                    evac_tp(TP_KD + i, kdt[0:rows, 2 * i:2 * i + w, :],
                            tp[i % 2][0:rows, 0:w * P].rearrange("p (i c) -> p i c", c=P))
                act.wait_ge(dh_ready, b + 1)
                dst_d = [cd[:, 0, 0:n], cd[:, 1, 0:n], cxp[:, 0, 2:2 + n], cxp[:, 1, 2:2 + n],
                         bd[:, 0, 0:n], bd[:, 1, 0:n]]
                for i in range(6):
                    if i == 4:
                        act.wait_ge(v_placed, 32 * (b + 1))
                    evac(ZP_D + i, dst_d[i]).then_inc(zp_free, 1)
                    next_hi(16 + i)
                act.wait_ge(zp_free, zb + ZP_D + 6)
                act.activation(ra[:, :, 0:n], ra[:, :, 0:n], ACT.Silu).then_inc(silu_ready, 1)
                act.activation(gb[:, :, 0:n], gb[:, :, 0:n], ACT.Gelu_apprx_tanh).then_inc(gelu_ready, 1)
                act.wait_ge(kd_ready, b + 1)
                for j in range(2):
                    wait(act, rg_done, 2 * b + j)
                    evac(ZP_G + 2 * j, tmp[0][:, 0:n], func=ACT.Sigmoid,
                         bias=prm2[:, R2_RBA + j:R2_RBA + j + 1]).then_inc(zp_free, 1)
                    evac(ZP_G + 2 * j + 1, tmp[1][:, 0:n], func=ACT.Sigmoid,
                         bias=prm2[:, R2_RBX + j:R2_RBX + j + 1]).then_inc(zp_free, 1)
                    act.wait_ge(zp_free, zb + ZP_G + 2 * j + 2)
                    act.activation(tmp[2][:, 0:n], tmp[0][:, 0:n], ACT.Tanh, scale=mixc["c8"][:, 1, j:j + 1])
                    act.activation(tmp[0][:, 0:n], tmp[0][:, 0:n], ACT.Exp,
                                   scale=mixc["c8"][:, 0, j:j + 1]).then_inc(rgate, 1)
                    act.wait_ge(rg_u, 2 * b + j + 1)
                    act.activation(tmp[2][:, 0:n], tmp[2][:, 0:n], ACT.Sqrt).then_inc(rg_sqrt, 1)
                for j in range(2):
                    evac(ZP_O + j, oT[:, j, 0:n]).then_inc(zp_free, 1)
                act.preload_act_table_set(EXP_LN)
                act.wait_ge(d_ready, 2 * (b + 1))
                act.wait_ge(rg_done, 2 * (b + 1))
                act.wait_ge(zp_free, zb + ZP_O + 2)
                for k in range(6):
                    norm(k)

                def weights(q, i, w):
                    act.wait_ge(x_done, q + i + 1)
                    x = aW[i % 2][0:rows, :, 0:w]
                    act.activation(x, x, ACT.Exp).then_inc(w_ready, 1)

                def key_block(q, width, newest, place):
                    achain.at(2 * q)
                    for i in range(2 * tiles):
                        w = width(i // 2)
                        act.wait_ge(sc_full, q + i + 1)
                        lt = aR[i % 2][0:rows, :, 0:w]
                        achain.link(act.activation(lt, score_banks[i % 2][0:rows, :, 0:w], ACT.Abs))
                        achain.link(act.activation(lt, lt, ACT.Exp, scale=-1.0))
                        act.activation(lt, lt, ACT.Ln, bias=1.0).then_inc(l_ready, 1)
                        if i:
                            weights(q, i - 1, width((i - 1) // 2))
                    weights(q, 2 * tiles - 1, width(tiles - 1))

                attend(act, b, sample, key_block)
                act.wait_ge(pv_done, pairs_after(b, sample))
                if sample:
                    act.activation(osb[0:rows, 0, 0:GW], ob[0:rows, 0:GW], ACT.Copy).then_inc(osb_ready, 1)
                else:
                    act.activation(osb[:, :, :], ob2[:, :, :], ACT.Copy).then_inc(osb_ready, 1)
                act.wait_ge(ot_full, b + 1)
                act.activation(oT[:, 4:6, 0:n], tp2[:, :, 0:n], ACT.Copy).then_inc(ot_done, 1)
                act.wait_ge(ot_done, b + 1)
                for k in (6, 7):
                    norm(k)

                act.wait_ge(norm_done, KT * (b + 1))
                for f in range(KT):
                    act.activation(hn_hi[:, f, 0:n], oT[:, f, 0:n], ACT.Copy).then_inc(oh_ready, 1)
                def store(f):
                    act.wait_ge(x1_ready, b * KT + f + 1)
                    act.dma_start(x1_v[:, f, bass.ds(b * BLK, n)], xT[:, f, 0:n]).then_inc(x1_stored, 16)

                for f in range(KT):
                    wait(act, x1_ready, b * KT + f - 1)
                    evac(ZP_MIX + f, tmp[f % 2][:, 0:n], func=ACT.Identity,
                         scale=modT[:, M_G1 + f, m:m + 1]).then_inc(zp_free, 1)
                    next_hi(N_IN_STRIPS + f)
                    if f:
                        store(f - 1)
                store(KT - 1)
                if not sample:
                    assert act_links.setdefault("block", chain.n) == chain.n

            strip_hi(0, 0, 1, 0)
            strip_hi(1, 1, 1, 0)
            body(0, False)
            with act.Fori(1, NBLK) as b:
                body(b, False)
            for j in range(2):
                act.wait_ge(tp_full, NBLK * TP_PER + j + 1)
                act.activation(Kt[:, j, 0:PAST], tp[j][:, :], ACT.Copy).then_inc(tp_free, 1)
            body(NBLK, True)

        dve_links = {}

        @block.vector
        def _(dve):
            chain, achain = Chain(dve, dve_c), Chain(dve, dve_a)
            chain.at(0)
            chain.link(dve.memset(hst[:, :], 0.0))
            chain.link(dve.memset(S[:, CPB - 1, :], 0.0))
            dve.memset(xbp[:, :, 0:3], 0.0).then_inc(halo_ready, 1)
            dve.memset(cxp[:, :, 0:2], 0.0).then_inc(dh_ready, 1)
            setup_links = chain.n

            def body(b, sample):
                n, tiles, chunks, rows = shape_of(sample)
                m = 1 if sample else 0
                chain.at(setup_links + b * dve_links.get("block", 0) + (dve_links["between"] if sample else 0))
                zb = b * ZP_PER

                def norm(k):
                    t = NORM_ORDER[k]
                    dve.wait_ge(rs_ready, b * ST_PER + k + 2)
                    ins = dve.scalar_tensor_tensor(out=oT[:, t, 0:n], in0=oT[:, t, 0:n],
                                                   scalar=prm2[:, R2_ON + t:R2_ON + t + 1],
                                                   in1=rsh[k % 2][:, 0:n], op0=ALU.mult, op1=ALU.mult)
                    if t < 2:
                        chain.link(ins)
                        dve.wait_ge(silu_ready, b + 1)
                        ins = dve.tensor_tensor(oT[:, t, 0:n], oT[:, t, 0:n], ra[:, t, 0:n], ALU.mult)
                    ins.then_inc(norm_done, 1)

                dve.wait_ge(rs_ready, b * ST_PER + 1)
                for f in range(KT):
                    wait(dve, hi_ready, b * KT + f - 1)
                    wait(dve, lo_ready, b * KT + f - 1)
                    t = tmp[f % 2][:, 0:n]
                    chain.link(dve.tensor_tensor(t, xT[:, f, 0:n], tmp[2][:, 0:n], ALU.mult))
                    dve.tensor_scalar(t, t, gs1[:, f, m:m + 1], modT[:, M_SH1 + f, m:m + 1],
                                      ALU.mult, ALU.add).then_inc(hf_ready, 1)
                dve.wait_ge(y_ready, b + 1)
                la, g = tmp[2][:, 0:n], tmp[3][:, 0:n]
                chain.link(dve.scalar_tensor_tensor(out=la, in0=la, scalar=0.0, in1=g, op0=ALU.min, op1=ALU.subtract))
                chain.link(dve.tensor_tensor_scan(g, mixc["scan_mask"][:, 0:n], la, 0.0, ALU.mult, ALU.add))
                g3 = g.rearrange("p (c t) -> p c t", t=CHUNK)
                dve.tensor_tensor(la.rearrange("p (c t) -> p c t", t=CHUNK),
                                  g3[:, :, CHUNK - 1:CHUNK].to_broadcast([P, chunks, CHUNK]), g3,
                                  ALU.subtract).then_inc(gd_ready, 1)
                dve.wait_ge(kdec_ready, b + 1)
                dve.tensor_tensor(ka[:, 0:n], ka[:, 0:n], la, ALU.mult).then_inc(kd_ready, 1)
                dve.wait_ge(zp_free, zb + ZP_B + 4)
                dve.wait_ge(ktok_stored, 16 * (b + 1))
                for j in range(2):
                    y = xcv[:, j, 0:n]
                    chain.link(dve.tensor_scalar(y, xbp[:, j, 0:n], prm2[:, R2_RCW + j:R2_RCW + j + 1],
                                                 prm2[:, R2_RCB + j:R2_RCB + j + 1], ALU.mult, ALU.add))
                    for i in range(1, 4):
                        ins = dve.scalar_tensor_tensor(out=y, in0=xbp[:, j, i:i + n],
                                                       scalar=prm2[:, R2_RCW + 2 * i + j:R2_RCW + 2 * i + j + 1],
                                                       in1=y, op0=ALU.mult, op1=ALU.add)
                        if i < 3:
                            chain.link(ins)
                        else:
                            ins.then_inc(xcv_ready, 1)
                dve.tensor_copy(xbp[:, :, 0:3], xbp[:, :, n:n + 3]).then_inc(halo_ready, 1)
                dve.wait_ge(zp_free, zb + ZP_D + 6)
                chain.link(dve.tensor_tensor(cxp[:, :, 2:2 + n], cd[:, :, 0:n], cxp[:, :, 2:2 + n], ALU.mult))
                for j in range(2):
                    y = oT[:, 6 + j, 0:n]
                    chain.link(dve.tensor_scalar(y, cxp[:, j, 0:n], prm2[:, R2_SCW + j:R2_SCW + j + 1], None, ALU.mult))
                    for i in range(1, 3):
                        chain.link(dve.scalar_tensor_tensor(
                            out=y, in0=cxp[:, j, i:i + n], scalar=prm2[:, R2_SCW + 2 * i + j:R2_SCW + 2 * i + j + 1],
                            in1=y, op0=ALU.mult, op1=ALU.add))
                    dve.tensor_tensor(y, y, bd[:, j, 0:n], ALU.mult).then_inc(d_ready, 1)
                dve.tensor_copy(cxp[:, :, 0:2], cxp[:, :, n:n + 2]).then_inc(dh_ready, 1)
                if sample:
                    dve.wait_ge(state_in, 16 * HEADS)
                for c in range(chunks):
                    dve.wait_ge(u_full, b * CPB + c + 1)
                    dve.tensor_tensor(um[:, :], zs[c % 2][:, 0:GW], mixc["bd_mask"][:, :], ALU.mult).then_inc(u_used, 1)
                    dve.wait_ge(u_used, b * CPB + c + 1)
                    dve.scalar_tensor_tensor(out=S[:, c, :], in0=S[:, (c - 1) % CPB, :], scalar=dec[:, c:c + 1],
                                             in1=um[:, :], op0=ALU.mult, op1=ALU.add).then_inc(s_ready, 1)
                    dve.wait_ge(s_ready, b * CPB + c + 1)
                for j in range(2):
                    a, u, v, w = (tmp[i][:, 0:n] for i in range(4))
                    y = oT[:, 2 + j, 0:n]
                    dve.wait_ge(zp_free, zb + ZP_G + 2 * j + 2)
                    dve.wait_ge(rgate, 2 * b + j + 1)
                    chain.link(dve.tensor_tensor(u, u, xcv[:, j, 0:n], ALU.mult))
                    chain.link(dve.tensor_tensor(w, a, a, ALU.mult))
                    dve.scalar_tensor_tensor(out=v, in0=w, scalar=1.0, in1=v, op0=ALU.add, op1=ALU.mult).then_inc(rg_u, 1)
                    dve.wait_ge(rg_sqrt, 2 * b + j + 1)
                    chain.link(dve.tensor_tensor(u, v, u, ALU.mult))
                    chain.link(dve.tensor_tensor_scan(y, a, u, hst[:, j:j + 1], ALU.mult, ALU.add))
                    chain.link(dve.tensor_copy(hst[:, j:j + 1], oT[:, 2 + j, n - 1:n]))
                    dve.wait_ge(gelu_ready, b + 1)
                    dve.tensor_tensor(y, y, gb[:, j, 0:n], ALU.mult).then_inc(rg_done, 1)
                for k in range(6):
                    norm(k)

                def turned(q, i, w):
                    dve.wait_ge(wtp_full, q + i + 1)
                    wait(dve, pv_done, q + i - 1)
                    kr, nk = (w, 1) if w < P else (P, w // P)
                    dve.tensor_copy(aT[i % 2][0:kr, :, 0:nk * rows], tp2[0:kr, :, 0:nk * rows]).then_inc(wt_ready, 1)

                def key_block(q, width, newest, place):
                    achain.at(2 * q)
                    for i in range(2 * tiles):
                        w = width(i // 2)
                        z, r, cc, x = (v[0:rows, :, 0:w] for v in (score_banks[i % 2], aR[i % 2], aC, aW[i % 2]))
                        sums = carry[0:rows, 2 * i:2 * i + 2]
                        dve.wait_ge(l_ready, q + i + 1)
                        achain.link(dve.scalar_tensor_tensor(out=r, in0=z, scalar=0.0, in1=r, op0=ALU.max, op1=ALU.add))
                        for j in range(2):
                            ins = dve.tensor_tensor_scan(cc[:, j, ::-1], r[:, j, ::-1], r[:, j, ::-1],
                                                         0.0 if newest else sums[:, j:j + 1], ALU.add, ALU.max)
                        achain.link(ins)
                        dve.tensor_copy(sums, cc[:, :, 0])
                        dve.tensor_tensor(x, z, cc, ALU.subtract).then_inc(x_done, 1)
                        if i:
                            turned(q, i - 1, width((i - 1) // 2))
                    turned(q, 2 * tiles - 1, width(tiles - 1))

                attend(dve, b, sample, key_block)
                for k in (6, 7):
                    norm(k)
                for f in range(KT):
                    dve.wait_ge(zp_free, zb + ZP_MIX + f + 1)
                    dve.tensor_tensor(xT[:, f, 0:n], xT[:, f, 0:n], tmp[f % 2][:, 0:n], ALU.add).then_inc(x1_ready, 1)
                if not sample:
                    assert dve_links.setdefault("block", chain.n) == chain.n

            def gather_states(i):
                chain.link(dve.tensor_copy(stout[:, 0:2], hst[:, :]))
                chain.link(dve.tensor_copy(stout[:, 2:8].rearrange("p (i j) -> p j i", j=2), xbp[:, :, 0:3]))
                dve.tensor_copy(stout[:, 8:12].rearrange("p (i j) -> p j i", j=2), cxp[:, :, 0:2]).then_inc(stout_ready, 1)
                dve.wait_ge(strow_full, i + 1)
                dve.tensor_copy(strow[:, :], ob[0:12, 0:P]).then_inc(strow_ready, 1)

            body(0, False)
            with dve.Fori(1, NBLK) as b:
                body(b, False)
            chain.at(setup_links + NBLK * dve_links["block"])
            gather_states(0)
            dve.wait_ge(out_stored, 16 * (HEADS + 3))
            dve.memset(S[:, CPB - 1, :], 0.0).then_inc(init_ok, 1)
            chain.link(dve.tensor_copy(hst[:, :], prm2[:, R2_H:R2_H + 2]))
            chain.link(dve.tensor_copy(xbp[:, :, 0:3], prm2[:, R2_RBUF:R2_RBUF + 6].rearrange("p (i j) -> p j i", j=2)))
            chain.link(dve.tensor_copy(cxp[:, :, 0:2], prm2[:, R2_SBUF:R2_SBUF + 4].rearrange("p (i j) -> p j i", j=2)))
            dve.memset(carry[:, :], 0.0).then_inc(init_ok, 1)
            dve_links["between"] = chain.n
            body(NBLK, True)
            chain.at(chain.base + chain.n)
            gather_states(1)

        @block.tensor
        def _(pe):
            def body(b, sample):
                n, tiles, chunks, rows = shape_of(sample)
                zb, tb, qb = b * ZP_PER, tp_base(b, sample), b * SQ_PER
                idr = ident[0:rows, 0:rows]

                def use(u):
                    wait(pe, zp_free, zb + u - 1)
                    return zp[u % 2]

                def turn(u, parts):
                    wait(pe, tp_free, tb + u - 1)
                    for dst, src, idt in parts:
                        ins = pe.transpose(dst, src, idt)
                    ins.then_inc(tp_full, 1)

                def product3(out, hi, lo):
                    for k in range(KT):
                        pe.matmul(out, hi(k), hn_hi[:, k, 0:n], start=(k == 0), stop=False)
                        pe.matmul(out, hi(k), hn_lo[:, k, 0:n], start=False, stop=False)
                        ins = pe.matmul(out, lo(k), hn_hi[:, k, 0:n], start=False, stop=(k == KT - 1))
                    return ins

                def strip(i):
                    g, slot = b * N_STRIPS + i, i % 2
                    pe.wait_ge(w_hi_ready, g + 1)
                    pe.wait_ge(w_lo_ready, g + 1)
                    bank = use(STRIP_USE[i])
                    product3(bank[:, 0:n], lambda k: w_hi[slot][:, k, :], lambda k: w_lo[slot][:, k, :]).then_inc(zp_full, 1)

                def norm(k):
                    pe.wait_ge(sq_ready, qb + KT + k + 1)
                    pe.wait_ge(st_free, b * ST_PER + k + 1)
                    pe.matmul(st[:, 0:n], head_ones[:, :], sq[k % 2][:, 0:n], start=True, stop=True).then_inc(sq_used, 1)

                def sum_squares(f):
                    pe.wait_ge(sq_ready, qb + f + 1)
                    pe.matmul(st[:, 0:n], ones[:, :], sq[f % 2][:, 0:n], start=(f == 0), stop=(f == KT - 1)).then_inc(sq_used, 1)

                pe.wait_ge(x_loaded, 16 * (b + 1))
                wait(pe, st_free, b * ST_PER)
                for f in range(KT):
                    turn(TP_X + f, [(tp[f % 2][:, i * rows:(i + 1) * rows], xrow[0:rows, i, f * P:(f + 1) * P], idr)
                                    for i in range(tiles)])
                    if f:
                        sum_squares(f - 1)
                sum_squares(KT - 1)
                pe.wait_ge(hi_ready, KT * (b + 1))
                pe.wait_ge(lo_ready, KT * (b + 1))
                bank = use(ZP_LRA)
                product3(bank[:, 0:n], lambda k: mixc["lra_hi"][:, k * RANK:k * RANK + P],
                         lambda k: mixc["lra_lo"][:, k * RANK:k * RANK + P]).then_inc(zp_full, 1)
                for i in range(12):
                    strip(i)
                bank = use(ZP_Y)
                pe.matmul(bank[:, 0:n], mixc["wa2"][:, :], lra[:, 0:n], start=True, stop=True).then_inc(zp_full, 1)
                for u0, src in ((TP_K, kst), (TP_V, vst), (TP_VA, va)):
                    pe.wait_ge(zp_free, zb + ZP_C + (4 if u0 == TP_K else 6))
                    for j in range(2):
                        turn(u0 + j, [(tp[j][0:rows, i * P:(i + 1) * P], src[:, j, i * rows:(i + 1) * rows], ident[:, :])
                                      for i in range(tiles)])
                for i in range(12, 16):
                    strip(i)
                pe.wait_ge(kd_ready, b + 1)
                for i in range((tiles + 1) // 2):
                    turn(TP_KD + i, [(tp[i % 2][0:rows, v * P:(v + 1) * P],
                                      ka[:, (2 * i + v) * rows:(2 * i + v + 1) * rows], ident[:, :])
                                     for v in range(min(2, tiles))])
                for i in range(16, 22):
                    strip(i)
                pe.wait_ge(tp_free, tb + TP_KD + (tiles + 1) // 2)
                for c in range(chunks):
                    r0 = CHUNK * (c % 2)
                    wait(pe, u_used, b * CPB + c - 1)
                    pe.matmul(zs[c % 2][:, 0:GW], kdt[r0:r0 + CHUNK, c // 2, :], vt[r0:r0 + CHUNK, c // 2, :],
                              start=True, stop=True).then_inc(u_full, 1)
                pe.wait_ge(xcv_ready, 2 * (b + 1))
                for j in range(2):
                    for g in range(2):
                        bank = use(ZP_G + 2 * j + g)
                        pe.matmul(bank[:, 0:n], mixc["rgw"][:, g, j, :], xcv[:, j, 0:n], start=True,
                                  stop=True).then_inc(zp_full, 1)
                pe.wait_ge(s_ready, b * CPB + chunks)
                for j in range(2):
                    bank = use(ZP_O + j)
                    for c in range(chunks):
                        ins = pe.matmul(bank[:, c * CHUNK:(c + 1) * CHUNK], S[:, c, j * P:(j + 1) * P],
                                        qa[:, c * CHUNK:(c + 1) * CHUNK], start=True, stop=True)
                    ins.then_inc(zp_full, 1)
                for k in range(6):
                    norm(k)

                pe.wait_ge(kst_placed, 16 * (b + 1))
                pe.wait_ge(v_placed, 32 * (b + 1))

                def key_block(q, width, newest, place):
                    at, vtile = place() * BLK, place() * TPB
                    if not isinstance(at, int):
                        at, vtile = pe.snap(at), pe.snap(vtile)

                    def score(i):
                        s, w = i // 2, width(i // 2)
                        wait(pe, x_done, q + i - 1)
                        for j in range(2):
                            bank = score_banks[i % 2][0:rows, j, 0:w]
                            ins = pe.matmul(bank, qp[:, 2 * (i % 2) + j, s * rows:(s + 1) * rows],
                                            Kt[:, i % 2, bass.ds(at, w)], start=True, stop=not newest)
                            if newest:
                                ins = pe.matmul(score_banks[i % 2][0:rows, j, w - rows:w], idr,
                                                mixc["neg_mask"][0:rows, 0:rows], start=False, stop=True)
                        ins.then_inc(sc_full, 1)

                    def turn_weights(i):
                        w = width(i // 2)
                        kr, nk = (w, 1) if w < P else (P, w // P)
                        pe.wait_ge(w_ready, q + i + 1)
                        wait(pe, wt_ready, q + i)
                        for j in range(2):
                            for v in range(nk):
                                ins = pe.transpose(tp2[0:kr, j, v * rows:(v + 1) * rows],
                                                   aW[i % 2][0:rows, j, v * kr:(v + 1) * kr], idr)
                        ins.then_inc(wtp_full, 1)

                    def values(i):
                        s, w = i // 2, width(i // 2)
                        kr, nk = (w, 1) if w < P else (P, w // P)
                        pe.wait_ge(wt_ready, q + i + 1)
                        for j in range(2):
                            cols = slice(HD * (2 * (i % 2) + j), HD * (2 * (i % 2) + j + 1))
                            at_col = GW * (s % 2) + cols.start
                            for v in range(nk):
                                ins = pe.matmul(ob2[0:rows, s // 2, at_col:at_col + HD],
                                                aT[i % 2][0:kr, j, v * rows:(v + 1) * rows],
                                                Vb[0:kr, vtile + v, cols] if isinstance(vtile, int) else
                                                Vb[0:kr, bass.ds(vtile + v, 1), cols],
                                                start=(newest and i % 4 == 0 and j == 0 and v == 0), stop=False,
                                                skip_group_check=True)
                        ins.then_inc(pv_done, 1)

                    score(0)
                    score(1)
                    for i in range(2 * tiles):
                        if i + 2 < 2 * tiles:
                            score(i + 2)
                        if i:
                            values(i - 1)
                        turn_weights(i)
                    values(2 * tiles - 1)

                pe.wait_ge(zp_free, zb + ZP_O + 2)
                pe.wait_ge(st_free, b * ST_PER + 7)
                attend(pe, b, sample, key_block)
                pe.wait_ge(osb_ready, b + 1)
                for s in range(tiles):
                    for j in range(2):
                        ins = pe.transpose(tp2[:, j, s * rows:(s + 1) * rows],
                                           osb[0:rows, s // 2, GW * (s % 2) + j * P:GW * (s % 2) + (j + 1) * P], idr)
                ins.then_inc(ot_full, 1)
                for k in (6, 7):
                    norm(k)
                pe.wait_ge(oh_ready, KT * (b + 1))
                pe.wait_ge(ol_ready, KT * (b + 1))
                for i in range(N_IN_STRIPS, N_STRIPS):
                    strip(i)

            def turn_states(i):
                pe.wait_ge(stout_ready, i + 1)
                pe.transpose(ob[0:12, 0:P], stout[:, :], ident[:, :]).then_inc(strow_full, 1)

            body(0, False)
            with pe.Fori(1, NBLK) as b:
                body(b, False)
            turn_states(0)
            pe.wait_ge(past_in, 32)
            for j in range(2):
                pe.wait_ge(tp_free, NBLK * TP_PER + j - 1)
                for i in range(PAST // P):
                    ins = pe.transpose(tp[j][:, i * P:(i + 1) * P], ktok[:, i, j * P:(j + 1) * P], ident[:, :])
                ins.then_inc(tp_full, 1)
            body(NBLK, True)
            turn_states(1)


def mlp_phase(nc, const, x1_v, mlp_w1, mlp_w2, y_prompt, y_sample):
    prm2, modT, gs2 = const["prm2"], const["modT"], const["gs2"]
    ident, ones, eps = const["ident"], const["ones"], const["eps"]
    NSB = 3
    T = N_TOK // NSB
    CB = T // 2
    NFT = D_FF // P
    NC = NFT // 2
    TILES = [P] * (T // P) + [T % P]
    assert SEQ == (NSB - 1) * T + T - DEC and CB % 2 == 0
    with ExitStack() as ctx:
        def sb(name, shape, dt=F32):
            return ctx.enter_context(nc.sbuf_tensor(name, shape, dt))

        def ps(name):
            return ctx.enter_context(nc.psum_tensor(name, [P, 512], F32))

        def sem(name):
            return ctx.enter_context(nc.semaphore(name))

        xs = [sb(f"xs{i}", [P, KT, T]) for i in range(2)]
        h_hi, h_lo = sb("h_hi", [P, KT, T], F32R), sb("h_lo", [P, KT, T], F32R)
        g_hi = [sb(f"g_hi{i}", [P, 2, T], F32R) for i in range(2)]
        g_lo = [sb(f"g_lo{i}", [P, 2, T], F32R) for i in range(2)]
        w1r = [sb(f"w1r{i}", [P, KT, P]) for i in range(2)]
        w1h = [sb(f"w1h{i}", [P, KT, P], F32R) for i in range(2)]
        w1l = [sb(f"w1l{i}", [P, KT, P], F32R) for i in range(2)]
        w2r = [sb(f"w2r{i}", [P, D_MODEL]) for i in range(2)]
        w2h = [sb(f"w2h{i}", [P, D_MODEL], F32R) for i in range(4)]
        w2l = [sb(f"w2l{i}", [P, D_MODEL], F32R) for i in range(4)]
        rt = [sb(f"rt{i}", [P, CB]) for i in range(2)]
        sqt = [sb(f"sqt{i}", [P, CB]) for i in range(2)]
        rms = [sb(f"rms{i}", [P, CB]) for i in range(2)]
        yrow = [sb(f"yrow{i}", [P, D_MODEL]) for i in range(2)]
        hp, op = [ps("hp0"), ps("hp1")], [ps(f"op{i}") for i in range(4)]
        stb = [ps("stb0"), ps("stb1")]

        x_in, w1_in, w2_in = [sem("x_in0"), sem("x_in1")], [sem("w1_in0"), sem("w1_in1")], [sem("w2_in0"), sem("w2_in1")]
        w1_hi, w1_lo, w2_hi, w2_lo = sem("w1_hi"), sem("w1_lo"), sem("w2_hi"), sem("w2_lo")
        n_sq, n_sum, n_rms, n_rms_c = sem("n_sq"), sem("n_sum"), sem("n_rms"), sem("n_rms_c")
        hf2, hi2, lo2, chain_d = sem("hf2"), sem("hi2"), sem("lo2"), sem("chain_d")
        h_full, h_relu, h_sq, gh_ready, gl_ready = (
            sem("h_full"), sem("h_relu"), sem("h_sq"), sem("gh_ready"), sem("gl_ready"))
        o_full, o_added, y_norm, yt_full, yt_read, y_out = (
            sem("o_full"), sem("o_added"), sem("y_norm"), sem("yt_full"), sem("yt_read"), [sem("y_out0"), sem("y_out1")])
        w1_v = mlp_w1[0].rearrange("(k p) n -> p k n", p=P)
        NT = NSB * NC
        NORMS = 2
        N_YT = 2 * len(TILES)
        block = ctx.enter_context(nc.Block())

        def each_chunk(eng, sbk, one):
            c = sbk * NC
            one(c, 0)
            one(c + 1, 1)
            with eng.Fori(1, NC // 2 - 1) as i:
                one(c + 2 * i, 0)
                one(c + 2 * i + 1, 1)
            one(c + NC - 2, 0)
            one(c + NC - 1, 1)

        def ranges(sbk, cb):
            if sbk == NSB - 1 and cb == 1:
                return [(0, CB - DEC, 0), (CB - DEC, CB, 1)]
            return [(0, CB, 0)]

        @block.sync
        def _(sp):
            def load_w(kind, g, slot, row):
                sems, hi, lo = (w1_in, w1_hi, w1_lo) if kind == 1 else (w2_in, w2_hi, w2_lo)
                wait(sp, hi, g - 1)
                wait(sp, lo, g - 1)
                if kind == 1:
                    sp.dma_start(w1r[slot][:, :, :], w1_v[:, :, bass.ds(row, P)]).then_inc(sems[slot], 16)
                else:
                    sp.dma_start(w2r[slot][:, :], mlp_w2[0, bass.ds(row, P), :]).then_inc(sems[slot], 16)

            def load_x(sbk):
                if sbk < NSB:
                    wait(sp, yt_read, (sbk - 1) * N_YT)
                    sp.dma_start(xs[sbk % 2][:, :, :], x1_v[:, :, sbk * T:(sbk + 1) * T]).then_inc(x_in[sbk % 2], 16)

            load_x(0)
            for kind in (1, 2):
                for j in range(2):
                    load_w(kind, j, j, j * P)
            for sbk in range(NSB):
                def loads(c, _):
                    if isinstance(c, int) and c == NT - 1:
                        return
                    row = 0 if isinstance(c, int) and (c + 1) % NC == 0 else (c - sbk * NC + 1) * (2 * P)
                    for kind in (1, 2):
                        for j in range(2):
                            load_w(kind, 2 * c + 2 + j, j, row + j * P)

                load_x(sbk + 1)
                each_chunk(sp, sbk, loads)
                for i, rows in enumerate(TILES):
                    sp.wait_ge(yt_read, sbk * N_YT + 2 * i + 2)
                    t0 = sbk * T + i * P
                    dst = y_prompt[0, t0:t0 + rows, :] if t0 < SEQ else y_sample[0, t0 - SEQ:t0 - SEQ + rows, :]
                    sp.dma_start(dst, yrow[i % 2][0:rows, :]).then_inc(y_out[i % 2], 16)
            for i in range(2):
                sp.wait_ge(y_out[i], 16 * NSB * len(TILES) // 2)

        @block.gpsimd
        def _(pool):
            def lo(kind, g, slot4, slot2, used):
                hi, done = (w1_hi, w1_lo) if kind == 1 else (w2_hi, w2_lo)
                pool.wait_ge(hi, g + 1)
                wait(pool, h_full if kind == 1 else o_full, used)
                if kind == 1:
                    pool.tensor_tensor(w1l[slot2][:, :, :], w1r[slot2][:, :, :], w1h[slot2][:, :, :].bitcast(F32),
                                       ALU.subtract).then_inc(done, 1)
                else:
                    pool.tensor_tensor(w2l[slot4][:, :], w2r[slot2][:, :], w2h[slot4][:, :].bitcast(F32),
                                       ALU.subtract).then_inc(done, 1)

            def chunk(c, odd):
                if isinstance(c, int) and c == NT - 1:
                    return
                for j in range(2):
                    lo(1, 2 * c + 2 + j, 0, j, 4 * c + 2 * j + 2)
                for j in range(2):
                    lo(2, 2 * c + 2 + j, (2 * (odd + 1) + j) % 4, j, 16 * c)

            for kind in (1, 2):
                for j in range(2):
                    lo(kind, j, j, j, 0)
            for sbk in range(NSB):
                for f in range(KT):
                    for cb in range(2):
                        u = (sbk * KT + f) * 2 + cb
                        pool.wait_ge(hi2, u + 1)
                        cols = slice(cb * CB, (cb + 1) * CB)
                        pool.tensor_tensor(h_lo[:, f, cols], rt[cb][:, :], h_hi[:, f, cols].bitcast(F32),
                                           ALU.subtract).then_inc(lo2, 1)
                each_chunk(pool, sbk, chunk)

        @block.scalar
        def _(act):
            def hi(kind, g, slot4, slot2, loads, used):
                act.wait_ge((w1_in if kind == 1 else w2_in)[slot2], 16 * loads)
                wait(act, h_full if kind == 1 else o_full, used)
                if kind == 1:
                    act.activation(w1h[slot2][:, :, :], w1r[slot2][:, :, :], ACT.Copy).then_inc(w1_hi, 1)
                else:
                    act.activation(w2h[slot4][:, :], w2r[slot2][:, :], ACT.Copy).then_inc(w2_hi, 1)

            def chunk(c, odd):
                more = not (isinstance(c, int) and c == NT - 1)
                for ft in range(2):
                    for cb in range(2):
                        i = 2 * ft + cb
                        h = 4 * c + i
                        act.wait_ge(h_full, h + 1)
                        wait(act, h_sq, h - 1)
                        act.activation(rt[i % 2][:, :], hp[i % 2][:, 0:CB], ACT.Relu).then_inc(h_relu, 1)
                        act.wait_ge(h_sq, h + 1)
                        wait(act, o_full, 16 * (c - 1) if isinstance(c, int) else 16 * c - 16)
                        act.activation(g_hi[odd][:, ft, cb * CB:(cb + 1) * CB], sqt[i % 2][:, :],
                                       ACT.Copy).then_inc(gh_ready, 1)
                    if more:
                        hi(1, 2 * c + 2 + ft, 0, ft, c + 2, 4 * c + 2 * ft + 2)
                if more:
                    for j in range(2):
                        hi(2, 2 * c + 2 + j, (2 * (odd + 1) + j) % 4, j, c + 2, 16 * c)

            def norm(k, x):
                for f in range(KT):
                    for cb in range(2):
                        u = (k * KT + f) * 2 + cb
                        wait(act, n_sum, u - 1)
                        act.activation(sqt[cb][:, :], x[:, f, cb * CB:(cb + 1) * CB], ACT.Square).then_inc(n_sq, 1)
                for cb in range(2):
                    act.wait_ge(n_sum, (k + 1) * KT * 2)
                    act.activation(rms[cb][:, :], stb[cb][:, 0:CB], ACT.Ln, scale=1.0 / D_MODEL,
                                   bias=eps[:, 0:1]).then_inc(n_rms_c, 1)
                    act.wait_ge(n_rms_c, 2 * k + cb + 1)
                    act.activation(rms[cb][:, :], rms[cb][:, :], ACT.Exp, scale=-0.5).then_inc(n_rms, 1)

            act.preload_act_table_set(EXP_LN)
            for kind in (1, 2):
                for j in range(2):
                    hi(kind, j, j, j, 1, 0)
            for sbk in range(NSB):
                x = xs[sbk % 2]
                act.wait_ge(x_in[sbk % 2], 16 * (sbk // 2 + 1))
                norm(2 * sbk, x)
                for f in range(KT):
                    for cb in range(2):
                        act.wait_ge(hf2, (sbk * KT + f) * 2 + cb + 1)
                        act.activation(h_hi[:, f, cb * CB:(cb + 1) * CB], rt[cb][:, :], ACT.Copy).then_inc(hi2, 1)
                act.wait_ge(lo2, (sbk + 1) * KT * 2)
                each_chunk(act, sbk, chunk)
                act.wait_ge(o_added, (sbk + 1) * NC * 16)
                act.wait_ge(gl_ready, (sbk + 1) * NC * 4)
                norm(2 * sbk + 1, x)
                for i, rows in enumerate(TILES):
                    for v in range(2):
                        u = sbk * N_YT + 2 * i + v
                        act.wait_ge(yt_full, u + 1)
                        wait(act, y_out[i % 2], 16 * ((sbk * len(TILES) + i) // 2))
                        act.activation(yrow[i % 2][0:rows, v * 512:(v + 1) * 512], op[v][0:rows, :],
                                       ACT.Copy).then_inc(yt_read, 1)

        @block.vector
        def _(dve):
            chain = Chain(dve, chain_d)

            def hidden(c, odd):
                for i in range(4):
                    ft, cb = i // 2, i % 2
                    h = 4 * c + i
                    dve.wait_ge(h_relu, h + 1)
                    wait(dve, gh_ready, h - 1)
                    dve.tensor_tensor(sqt[i % 2][:, :], rt[i % 2][:, :], rt[i % 2][:, :], ALU.mult).then_inc(h_sq, 1)
                    dve.wait_ge(gh_ready, h + 1)
                    cols = slice(cb * CB, (cb + 1) * CB)
                    dve.tensor_tensor(g_lo[odd][:, ft, cols], sqt[i % 2][:, :], g_hi[odd][:, ft, cols].bitcast(F32),
                                      ALU.subtract).then_inc(gl_ready, 1)

            def add(c, sbk):
                x = xs[sbk % 2]
                for d in range(KT):
                    for cb in range(2):
                        i = 2 * d + cb
                        dve.wait_ge(o_full, 16 * c + i + 1)
                        if i == 0:
                            wait(dve, o_added, 16 * c)
                        for n, (a, e, m) in enumerate(ranges(sbk, cb)):
                            cols = x[:, d, cb * CB + a:cb * CB + e]
                            ins = dve.scalar_tensor_tensor(out=cols, in0=op[i % 4][:, a:e],
                                                           scalar=modT[:, M_G2 + d, m:m + 1], in1=cols,
                                                           op0=ALU.mult, op1=ALU.add)
                        ins.then_inc(o_added, 1)

            for sbk in range(NSB):
                x = xs[sbk % 2]
                dve.wait_ge(n_rms, 4 * sbk + 2)
                for f in range(KT):
                    for cb in range(2):
                        u = (sbk * KT + f) * 2 + cb
                        wait(dve, hi2, u - 1)
                        wait(dve, lo2, u - 1)
                        chain.link(dve.tensor_tensor(rt[cb][:, :], x[:, f, cb * CB:(cb + 1) * CB], rms[cb][:, :], ALU.mult))
                        for a, e, m in ranges(sbk, cb):
                            ins = dve.tensor_scalar(rt[cb][:, a:e], rt[cb][:, a:e], gs2[:, f, m:m + 1],
                                                    modT[:, M_SH2 + f, m:m + 1], ALU.mult, ALU.add)
                        ins.then_inc(hf2, 1)
                def chunk(c, odd):
                    hidden(c, odd)
                    if not (isinstance(c, int) and c == sbk * NC):
                        add(c - 1, sbk)

                each_chunk(dve, sbk, chunk)
                add(sbk * NC + NC - 1, sbk)
                dve.wait_ge(n_rms, 4 * sbk + 4)
                dve.wait_ge(o_added, 16 * NC * (sbk + 1))
                for f in range(KT):
                    for cb in range(2):
                        cols = x[:, f, cb * CB:(cb + 1) * CB]
                        dve.scalar_tensor_tensor(out=cols, in0=cols, scalar=prm2[:, R2_FIN + f:R2_FIN + f + 1],
                                                 in1=rms[cb][:, :], op0=ALU.mult, op1=ALU.mult).then_inc(y_norm, 1)

        @block.tensor
        def _(pe):
            def hidden(c, odd):
                for ft in range(2):
                    pe.wait_ge(w1_hi, 2 * c + ft + 1)
                    pe.wait_ge(w1_lo, 2 * c + ft + 1)
                    for cb in range(2):
                        wait(pe, h_relu, 4 * c + 2 * ft + cb - 1)
                        cols, bank = slice(cb * CB, (cb + 1) * CB), hp[cb][:, 0:CB]
                        for k in range(KT):
                            pe.matmul(bank, w1h[ft][:, k, :], h_hi[:, k, cols], start=(k == 0), stop=False)
                            pe.matmul(bank, w1h[ft][:, k, :], h_lo[:, k, cols], start=False, stop=False)
                            ins = pe.matmul(bank, w1l[ft][:, k, :], h_hi[:, k, cols], start=False, stop=(k == KT - 1))
                        ins.then_inc(h_full, 1)

            def project(c, odd):
                pe.wait_ge(gh_ready, 4 * c + 4)
                pe.wait_ge(gl_ready, 4 * c + 4)
                pe.wait_ge(w2_hi, 2 * c + 2)
                pe.wait_ge(w2_lo, 2 * c + 2)
                for d in range(KT):
                    for cb in range(2):
                        i = 2 * d + cb
                        wait(pe, o_added, 16 * c + i - 3)
                        cols, bank = slice(cb * CB, (cb + 1) * CB), op[i % 4][:, 0:CB]
                        for ft in range(2):
                            wh = w2h[2 * odd + ft][:, d * P:(d + 1) * P]
                            wl = w2l[2 * odd + ft][:, d * P:(d + 1) * P]
                            pe.matmul(bank, wh, g_hi[odd][:, ft, cols], start=(ft == 0), stop=False)
                            pe.matmul(bank, wh, g_lo[odd][:, ft, cols], start=False, stop=False)
                            ins = pe.matmul(bank, wl, g_hi[odd][:, ft, cols], start=False, stop=(ft == 1))
                        ins.then_inc(o_full, 1)

            def norm(k):
                for f in range(KT):
                    for cb in range(2):
                        pe.wait_ge(n_sq, (k * KT + f) * 2 + cb + 1)
                        pe.matmul(stb[cb][:, 0:CB], ones[:, :], sqt[cb][:, :], start=(f == 0),
                                  stop=(f == KT - 1)).then_inc(n_sum, 1)

            for sbk in range(NSB):
                x = xs[sbk % 2]
                wait(pe, n_rms, 4 * sbk)
                norm(2 * sbk)
                pe.wait_ge(hi2, KT * 2 * (sbk + 1))
                pe.wait_ge(lo2, KT * 2 * (sbk + 1))
                wait(pe, yt_read, sbk * N_YT)
                def chunk(c, odd):
                    hidden(c, odd)
                    if not (isinstance(c, int) and c == sbk * NC):
                        project(c - 1, 1 - odd)

                each_chunk(pe, sbk, chunk)
                project(sbk * NC + NC - 1, 1)
                norm(2 * sbk + 1)
                pe.wait_ge(y_norm, (sbk + 1) * KT * 2)
                for i, rows in enumerate(TILES):
                    for v in range(2):
                        wait(pe, yt_read, sbk * N_YT + 2 * i + v - 1)
                        for f in range(4):
                            ins = pe.transpose(op[v][0:rows, f * P:(f + 1) * P],
                                               x[:, 4 * v + f, i * P:i * P + rows], ident[:, :])
                        ins.then_inc(yt_full, 1)


_INS = ['x_prompt', 'x_sample', 'c_prompt', 'c_sample', 'state_gla', 'state_rg_h', 'state_rg_conv', 'cache_sb_k',
        'cache_sb_v', 'state_sc_conv', 'ln1_g', 'ln2_g', 'w_ada', 'b_ada', 'w_in', 'gla_wa2', 'gla_ba', 'rg_conv_w',
        'rg_conv_b', 'rg_wa', 'rg_ba', 'rg_wx', 'rg_bx', 'rg_lambda', 'sc_conv_w', 'out_norm_g', 'w_out', 'mlp_w1',
        'mlp_w2', 'final_g']
_OUTS = [(1, SEQ, D_MODEL), (1, DEC, D_MODEL), (1, 1, HEADS, GLA_DK, HD), (1, 1, HEADS, GLA_DK, HD),
         (1, 1, GW), (1, 1, GW), (1, 1, 3, GW), (1, 1, 3, GW), (1, 1, SEQ, HEADS, HD), (1, 1, DEC, HEADS, HD),
         (1, 1, SEQ, HEADS, HD), (1, 1, DEC, HEADS, HD), (1, 1, 2, GW), (1, 1, 2, GW)]


def kernel(**inputs):
    import numpy as _np
    import concourse.bacc as _bacc
    from concourse import mybir as _mybir
    from concourse.bass_utils import run_bass_kernel_spmd as _run

    nc = _bacc.Bacc("TRN2", target_bir_lowering=False, num_devices=1)
    arrays, args = {}, []
    for name in _INS:
        a = _np.ascontiguousarray(inputs[name])
        arrays[f"in_{name}_dram"] = a
        args.append(nc.dram_tensor(f"in_{name}_dram", a.shape, _mybir.dt.from_np(a.dtype), kind="ExternalInput").ap())
    for i, shape in enumerate(_OUTS):
        args.append(nc.dram_tensor(f"out_{i}_dram", shape, F32, kind="ExternalOutput").ap())
    build(nc, *args)
    r = _run(nc, [arrays], core_ids=[0])
    return tuple(r.results[0][f"out_{i}_dram"] for i in range(len(_OUTS)))
```

```python
from contextlib import ExitStack

import concourse.bass as bass
from concourse import mybir

ALU = mybir.AluOpType
ACT = mybir.ActivationFunctionType
F32 = mybir.dt.float32
F32R = mybir.dt.float32r

EXP_LN = "natural_log_exp_and_others"
P = 128
D_MODEL = 1024
KT = D_MODEL // P
SEQ = 2048
DEC = 64
PAST = 512
N_TOK = SEQ + DEC
BLK = 512
NBLK = SEQ // BLK
TPB = BLK // P
GW = D_MODEL // 4
HD = 64
HEADS = GW // HD
GLA_DK = 32
CHUNK = 64
CPB = BLK // CHUNK
RANK = 16
D_FF = 4 * D_MODEL
EPS = 1e-6
RG_C = 8.0
GLA_TAU = 16.0
NEG = -1e30

OFF_QA, OFF_KA, OFF_VA, OFF_LRA, OFF_RA, OFF_GB, OFF_XB = 0, 128, 256, 512, 528, 784, 1040
OFF_QC, OFF_KC, OFF_VC, OFF_BD, OFF_CD, OFF_XD = 1296, 1552, 1808, 2064, 2320, 2576

STRIPS_A = [("qa", 0, OFF_QA), ("ka", 0, OFF_KA), ("va", 0, OFF_VA), ("va", 1, OFF_VA + P),
            ("ra", 0, OFF_RA), ("ra", 1, OFF_RA + P)]
STRIPS_C = [(n, j, o + j * P) for n, o in (("qc", OFF_QC), ("kc", OFF_KC), ("vc", OFF_VC)) for j in range(2)]
STRIPS_B = [(n, j, o + j * P) for n, o in (("gb", OFF_GB), ("xb", OFF_XB)) for j in range(2)]
STRIPS_D = [(n, j, o + j * P) for n, o in (("cd", OFF_CD), ("xd", OFF_XD), ("bd", OFF_BD)) for j in range(2)]
STRIPS_IN = STRIPS_A + STRIPS_C + STRIPS_B + STRIPS_D
N_IN_STRIPS = len(STRIPS_IN)
N_STRIPS = N_IN_STRIPS + KT

ZP_LRA = 0
ZP_A = 1
ZP_C = ZP_A + 6
ZP_Y = ZP_C + 6
ZP_B = ZP_Y + 1
ZP_D = ZP_B + 4
ZP_G = ZP_D + 6
ZP_O = ZP_G + 4
ZP_MIX = ZP_O + 2
ZP_PER = ZP_MIX + KT
STRIP_USE = ([ZP_A + i for i in range(6)] + [ZP_C + i for i in range(6)] + [ZP_B + i for i in range(4)]
             + [ZP_D + i for i in range(6)] + [ZP_MIX + i for i in range(KT)])
TP_X = 0
TP_K = KT
TP_V = TP_K + 2
TP_VA = TP_V + 2
TP_KD = TP_VA + 2
TP_PER = TP_KD + 2
NORM_ORDER = [6, 7, 2, 3, 0, 1, 4, 5]
ST_PER = 1 + len(NORM_ORDER)
SQ_PER = KT + len(NORM_ORDER)
assert ZP_PER % 2 == 0 and TP_PER % 2 == 0 and N_STRIPS % 2 == 0

R1_BADA, R1_CP, R1_CS = 0, 48, 56
R2_LN1, R2_LN2, R2_FIN, R2_ON, R2_GBA = 0, 8, 16, 24, 32
R2_RCW, R2_RCB, R2_RBA, R2_RBX, R2_LAM, R2_SCW = 33, 41, 43, 45, 47, 49
R2_H, R2_RBUF, R2_SBUF, R2_ALL = 55, 57, 63, 67
M_SH1, M_SC1, M_G1, M_SH2, M_SC2, M_G2 = 0, 8, 16, 24, 32, 40


def wait(eng, sem, value):
    if not (isinstance(value, int) and value <= 0):
        eng.wait_ge(sem, value)


class Chain:

    def __init__(self, eng, sem):
        self.eng, self.sem, self.base, self.n = eng, sem, 0, 0

    def at(self, base):
        self.base, self.n = base, 0

    def link(self, ins):
        self.n += 1
        ins.then_inc(self.sem, 1)
        self.eng.wait_ge(self.sem, self.base + self.n)


def build(nc, x_prompt, x_sample, c_prompt, c_sample, state_gla, state_rg_h, state_rg_conv,
          cache_sb_k, cache_sb_v, state_sc_conv, ln1_g, ln2_g, w_ada, b_ada, w_in, gla_wa2, gla_ba,
          rg_conv_w, rg_conv_b, rg_wa, rg_ba, rg_wx, rg_bx, rg_lambda, sc_conv_w, out_norm_g, w_out,
          mlp_w1, mlp_w2, final_g, y_prompt, y_sample, gla_p, gla_s, rgh_p, rgh_s, rgc_p, rgc_s,
          sbk_p, sbk_s, sbv_p, sbv_s, scc_p, scc_s):
    x1_dram = nc.dram_tensor("x1_scratch", (D_MODEL, N_TOK), F32, kind="Internal").ap()
    x1_v = x1_dram.rearrange("(f p) t -> p f t", p=P)
    with ExitStack() as ctx:
        def sb(name, shape, dt=F32):
            return ctx.enter_context(nc.sbuf_tensor(name, shape, dt))

        const = dict(
            ident=sb("ident", [P, P]), ones=sb("ones", [P, P]), head_ones=sb("head_ones", [P, P]),
            prm1=sb("prm1", [P, 64]), prm2=sb("prm2", [P, R2_ALL]), modT=sb("modT", [P, 48, 2]),
            gs1=sb("gs1", [P, KT, 2]), gs2=sb("gs2", [P, KT, 2]), eps=sb("eps", [P, 1]))
        mix_ctx = ExitStack()
        with mix_ctx:
            def mb(name, shape, dt=F32):
                return mix_ctx.enter_context(nc.sbuf_tensor(name, shape, dt))

            mixc = dict(
                neg_mask=mb("neg_mask", [P, P]), bd_mask=mb("bd_mask", [P, 2 * P]),
                scan_mask=mb("scan_mask", [P, BLK]), rgw=mb("rgw", [P, 2, 2, P]), c8=mb("c8", [P, 2, 2]),
                wa2=mb("wa2", [RANK, P]), lra_hi=mb("lra_hi", [P, KT * RANK + P], F32R),
                lra_lo=mb("lra_lo", [P, KT * RANK + P], F32R))
            setup_phase(nc, const, mixc, c_prompt, c_sample, w_ada, b_ada, w_in, ln1_g, ln2_g, final_g,
                        out_norm_g, gla_ba, gla_wa2, rg_conv_w, rg_conv_b, rg_wa, rg_ba, rg_wx, rg_bx,
                        rg_lambda, sc_conv_w, state_rg_h, state_rg_conv, state_sc_conv)
            mixer_phase(nc, const, mixc, x_prompt, x_sample, state_gla, cache_sb_k, cache_sb_v, w_in, w_out,
                        x1_v, gla_p, gla_s, rgh_p, rgh_s, rgc_p, rgc_s, sbk_p, sbk_s, sbv_p, sbv_s,
                        scc_p, scc_s)
        mlp_phase(nc, const, x1_v, mlp_w1, mlp_w2, y_prompt, y_sample)


def setup_phase(nc, const, mixc, c_prompt, c_sample, w_ada, b_ada, w_in, ln1_g, ln2_g, final_g,
                out_norm_g, gla_ba, gla_wa2, rg_conv_w, rg_conv_b, rg_wa, rg_ba, rg_wx, rg_bx,
                rg_lambda, sc_conv_w, state_rg_h, state_rg_conv, state_sc_conv):
    CH = 512
    NCH = 6 * D_MODEL // CH
    CT = CH // P
    RING = 4
    with ExitStack() as ctx:
        def sb(name, shape, dt=F32):
            return ctx.enter_context(nc.sbuf_tensor(name, shape, dt))

        def sem(name):
            return ctx.enter_context(nc.semaphore(name))

        rows1, rows2 = sb("rows1", [64, P]), sb("rows2", [R2_ALL, P])
        wada = [sb(f"wada{i}", [P, KT, CH]) for i in range(RING)]
        wada_hi = [sb(f"wada_hi{i}", [P, KT, CH], F32R) for i in range(2)]
        wada_lo = [sb(f"wada_lo{i}", [P, KT, CH], F32R) for i in range(2)]
        chl = sb("chl", [P, KT, 4], F32R)
        mod_rows = sb("mod_rows", [4, 6 * D_MODEL])
        lra_raw = sb("lra_raw", [P, KT * RANK])
        csil = sb("csil", [P, 2, KT])
        lam = sb("lam", [P, 4, 2])
        pt = ctx.enter_context(nc.psum_tensor("pt", [P, 2, 512], F32))
        pr = ctx.enter_context(nc.psum_tensor("pr", [4, 2, CH], F32))
        pm = ctx.enter_context(nc.psum_tensor("pm", [P, 48, 4], F32))
        rows_in, wada_in = sem("rows_in"), [sem(f"wada_in{i}") for i in range(RING)]
        wada_hi_ok, wada_lo_ok, row_full, row_read, c_hi, c_lo = (
            sem("wada_hi_ok"), sem("wada_lo_ok"), sem("row_full"), sem("row_read"), sem("c_hi"), sem("c_lo"))
        zeroed, blocks_in, masks = sem("zeroed"), sem("blocks_in"), sem("masks")
        rows_t, prm, silu_c, mod_full = sem("rows_t"), sem("prm"), sem("silu_c"), sem("mod_full")
        act_chain, dve_chain, lra_hi_ok, lra_in, lam_a = (
            sem("act_chain"), sem("dve_chain"), sem("lra_hi_ok"), sem("lra_in"), sem("lam_a"))
        wa_v = w_ada[0].rearrange("(k p) n -> p k n", p=P)
        block = ctx.enter_context(nc.Block())

        def rows(v):
            return v.rearrange("a (r p) -> (a r) p", p=P)

        def load_wada(eng, c):
            wait(eng, wada_lo_ok, c - RING + 1)
            eng.dma_start(wada[c % RING][:, :, :], wa_v[:, :, c * CH:(c + 1) * CH]).then_inc(wada_in[c % RING], 16)

        @block.sync
        def _(sp):
            parts1 = [(R1_BADA, rows(b_ada)), (R1_CP, rows(c_prompt)), (R1_CS, rows(c_sample))]
            parts2 = [(R2_LN1, rows(ln1_g)), (R2_LN2, rows(ln2_g)),
                      (R2_FIN, final_g.rearrange("(r p) -> r p", p=P)), (R2_ON, rows(out_norm_g)),
                      (R2_GBA, rows(gla_ba)), (R2_RCW, rows(rg_conv_w[0])), (R2_RCB, rows(rg_conv_b)),
                      (R2_RBA, rows(rg_ba)), (R2_RBX, rows(rg_bx)), (R2_LAM, rows(rg_lambda)),
                      (R2_SCW, rows(sc_conv_w[0])), (R2_H, rows(state_rg_h[0])),
                      (R2_RBUF, rows(state_rg_conv[0, 0])), (R2_SBUF, rows(state_sc_conv[0, 0]))]
            for tile, parts in ((rows1, parts1), (rows2, parts2)):
                for r, src in parts:
                    sp.dma_start(tile[r:r + src.shape[0], :], src).then_inc(rows_in, 16)
            for c in range(0, NCH, 2):
                load_wada(sp, c)
                if c == 2:
                    sp.dma_start(lra_raw[:, :].rearrange("p (k n) -> p k n", n=RANK),
                                 w_in[0].rearrange("(k p) n -> p k n", p=P)[:, :, OFF_LRA:OFF_LRA + RANK]
                                 ).then_inc(lra_in, 16)
                    sp.dma_start(mixc["wa2"][:, :], gla_wa2[0]).then_inc(blocks_in, 16)
                    sp.wait_ge(zeroed, 1)
                    for n in range(4):
                        for g, w in enumerate((rg_wa, rg_wx)):
                            sp.dma_start(mixc["rgw"][64 * (n % 2):64 * (n % 2) + 64, g, n // 2,
                                                     64 * (n % 2):64 * (n % 2) + 64], w[0, n]).then_inc(blocks_in, 16)
            sp.wait_ge(blocks_in, 16 * 9)

        @block.gpsimd
        def _(pool):
            n = [0]

            def step(ins):
                n[0] += 1
                ins.then_inc(masks, 1)
                pool.wait_ge(masks, n[0])

            pool.memset(mixc["rgw"][:, :, :, :], 0.0).then_inc(zeroed, 1)
            step(pool.memset(const["ident"][:, :], 0.0))
            step(pool.affine_select(out=const["ident"][:, :], in_=const["ident"][:, :], compare_op=ALU.not_equal,
                                    fill=1.0, base=0, pattern=[[-1, P]], channel_multiplier=1))
            step(pool.memset(const["ones"][:, :], 1.0))
            step(pool.memset(const["eps"][:, :], EPS))
            step(pool.memset(const["head_ones"][:, :], 0.0))
            for i in range(2):
                step(pool.memset(const["head_ones"][64 * i:64 * i + 64, 64 * i:64 * i + 64], 1.0))
            step(pool.memset(mixc["bd_mask"][:, :], 0.0))
            for h in range(HEADS):
                step(pool.memset(mixc["bd_mask"][32 * h:32 * h + 32, HD * h:HD * h + HD], 1.0))
            step(pool.memset(mixc["scan_mask"][:, :], 1.0))
            step(pool.memset(mixc["scan_mask"][:, 0:BLK:CHUNK], 0.0))
            step(pool.memset(mixc["neg_mask"][:, :], 0.0))
            step(pool.affine_select(out=mixc["neg_mask"][:, :], in_=mixc["neg_mask"][:, :], compare_op=ALU.is_ge,
                                    fill=NEG, base=-1, pattern=[[-1, P]], channel_multiplier=1))

        @block.scalar
        def _(act):
            chain = Chain(act, act_chain)
            for c in range(1, RING, 2):
                load_wada(act, c)
            act.wait_ge(prm, 1)
            act.activation(csil[:, :, :], const["prm1"][:, R1_CP:64].rearrange("p (c k) -> p c k", c=2),
                           ACT.Silu).then_inc(silu_c, 1)
            act.wait_ge(silu_c, 1)
            act.activation(chl[:, :, 0:2], csil[:, :, :].rearrange("p c k -> p k c"), ACT.Copy).then_inc(c_hi, 1)
            act.wait_ge(lra_in, 16)
            act.activation(mixc["lra_hi"][:, 0:KT * RANK], lra_raw[:, :], ACT.Copy).then_inc(lra_hi_ok, 1)
            act.wait_ge(prm, 2)
            chain.link(act.activation(lam[:, 0, :], const["prm2"][:, R2_LAM:R2_LAM + 2], ACT.Abs))
            chain.link(act.activation(lam[:, 1, :], lam[:, 0, :], ACT.Exp, scale=-1.0))
            act.activation(lam[:, 2, :], lam[:, 1, :], ACT.Ln, bias=1.0).then_inc(lam_a, 1)
            for c in range(NCH):
                act.wait_ge(wada_in[c % RING], 16 * (c // RING + 1))
                wait(act, row_full, c - 1)
                act.activation(wada_hi[c % 2][:, :, :], wada[c % RING][:, :, :], ACT.Copy).then_inc(wada_hi_ok, 1)
                if c >= 1 and c % 2 == 0 and c + RING - 1 < NCH:
                    load_wada(act, c + RING - 1)

        @block.vector
        def _(dve):
            chain = Chain(dve, dve_chain)
            chain.link(dve.memset(mixc["lra_hi"][:, KT * RANK:].bitcast(F32), 0.0))
            chain.link(dve.memset(mixc["lra_lo"][:, KT * RANK:].bitcast(F32), 0.0))
            dve.wait_ge(rows_t, 1)
            dve.tensor_copy(const["prm1"][:, :], pt[:, 0, 0:64]).then_inc(prm, 1)
            dve.wait_ge(rows_t, 2)
            dve.tensor_copy(const["prm2"][:, :], pt[:, 1, 0:R2_ALL]).then_inc(prm, 1)
            dve.wait_ge(lra_hi_ok, 1)
            dve.tensor_tensor(mixc["lra_lo"][:, 0:KT * RANK], lra_raw[:, :],
                              mixc["lra_hi"][:, 0:KT * RANK].bitcast(F32), ALU.subtract)
            dve.wait_ge(prm, 2)
            chain.link(dve.tensor_scalar(lam[:, 3, :], const["prm2"][:, R2_LAM:R2_LAM + 2], -1.0, 0.0,
                                         ALU.mult, ALU.max))
            dve.wait_ge(lam_a, 1)
            chain.link(dve.tensor_tensor(lam[:, 3, :], lam[:, 3, :], lam[:, 2, :], ALU.add))
            chain.link(dve.tensor_scalar(mixc["c8"][:, 0, :], lam[:, 3, :], -RG_C, None, ALU.mult))
            chain.link(dve.tensor_scalar(mixc["c8"][:, 1, :], lam[:, 3, :], RG_C, None, ALU.mult))
            dve.wait_ge(silu_c, 1)
            dve.wait_ge(c_hi, 1)
            dve.tensor_tensor(chl[:, :, 2:4], csil[:, :, :].rearrange("p c k -> p k c"),
                              chl[:, :, 0:2].bitcast(F32), ALU.subtract).then_inc(c_lo, 1)

            def take_row(c):
                dve.wait_ge(row_full, c + 1)
                dve.tensor_copy(mod_rows[:, c * CH:(c + 1) * CH], pr[:, c % 2, :]).then_inc(row_read, 1)

            for c in range(NCH):
                dve.wait_ge(wada_hi_ok, c + 1)
                dve.tensor_tensor(wada_lo[c % 2][:, :, :], wada[c % RING][:, :, :],
                                  wada_hi[c % 2][:, :, :].bitcast(F32), ALU.subtract).then_inc(wada_lo_ok, 1)
                if c:
                    take_row(c - 1)
            take_row(NCH - 1)
            dve.wait_ge(mod_full, 1)
            for c in range(2):
                chain.link(dve.tensor_tensor(const["modT"][:, :, c], pm[:, :, c],
                                             const["prm1"][:, R1_BADA:R1_BADA + 48], ALU.add))
                chain.link(dve.tensor_tensor(const["modT"][:, :, c], const["modT"][:, :, c], pm[:, :, 2 + c],
                                             ALU.add))
            for gs, m, g in ((const["gs1"], M_SC1, R2_LN1), (const["gs2"], M_SC2, R2_LN2)):
                for c in range(2):
                    chain.link(dve.scalar_tensor_tensor(
                        out=gs[:, :, c], in0=const["modT"][:, m:m + KT, c], scalar=1.0,
                        in1=const["prm2"][:, g:g + KT], op0=ALU.add, op1=ALU.mult))

        @block.tensor
        def _(pe):
            pe.wait_ge(rows_in, 16 * 17)
            pe.wait_ge(masks, 2)
            pe.transpose(pt[:, 0, 0:64], rows1[:, :], const["ident"][0:64, 0:64]).then_inc(rows_t, 1)
            pe.transpose(pt[:, 1, 0:R2_ALL], rows2[:, :], const["ident"][0:R2_ALL, 0:R2_ALL]).then_inc(rows_t, 1)
            pe.wait_ge(c_lo, 1)

            def turn_row(c):
                pe.wait_ge(row_read, c + 1)
                for t in range(CT):
                    ins = pe.transpose(pm[:, c * CT + t, :], mod_rows[:, c * CH + t * P:c * CH + (t + 1) * P],
                                       const["ident"][0:4, 0:4])
                return ins

            for c in range(NCH):
                pe.wait_ge(wada_lo_ok, c + 1)
                wait(pe, row_read, c - 1)
                for k in range(KT):
                    pe.matmul(pr[:, c % 2, :], chl[:, k, :], wada_hi[c % 2][:, k, :], start=(k == 0), stop=False)
                    ins = pe.matmul(pr[:, c % 2, :], chl[:, k, :], wada_lo[c % 2][:, k, :], start=False,
                                    stop=(k == KT - 1))
                ins.then_inc(row_full, 1)
                if c:
                    turn_row(c - 1)
            turn_row(NCH - 1).then_inc(mod_full, 1)


def mixer_phase(nc, const, mixc, x_prompt, x_sample, state_gla, cache_sb_k, cache_sb_v, w_in, w_out,
                x1_v, gla_p, gla_s, rgh_p, rgh_s, rgc_p, rgc_s, sbk_p, sbk_s, sbv_p, sbv_s, scc_p, scc_s):
    prm2, modT, gs1 = const["prm2"], const["modT"], const["gs1"]
    ident, ones, head_ones, eps = const["ident"], const["ones"], const["head_ones"], const["eps"]
    with ExitStack() as ctx:
        def sb(name, shape, dt=F32):
            return ctx.enter_context(nc.sbuf_tensor(name, shape, dt))

        def sem(name):
            return ctx.enter_context(nc.semaphore(name))

        xT = sb("xT", [P, KT, BLK])
        halves_at = nc.sbuf_base
        hn_hi, hn_lo = sb("hn_hi", [P, KT, BLK], F32R), sb("hn_lo", [P, KT, BLK], F32R)
        oT = sb("oT", [P, KT, BLK])
        xrow = oT[:, :, :].rearrange("p k n -> p (k n)").rearrange("p (i n) -> p i n", n=D_MODEL)
        Kt = sb("Kt", [P, 2, SEQ])
        Vb = sb("Vb", [P, SEQ // P, GW])
        qp = sb("qp", [P, HEADS, BLK])
        kst = sb("kst", [P, 2, BLK])
        vst = sb("vst", [P, 2, BLK])
        gb = vst
        qa, ka = sb("qa", [P, BLK]), sb("ka", [P, BLK])
        va = sb("va", [P, 2, BLK])
        cd = va
        ra = sb("ra", [P, 2, BLK])
        lra = sb("lra", [RANK, BLK])
        bd = sb("bd", [P, 2, BLK])
        vtok = bd[:, :, :].rearrange("p j n -> p (j n)").rearrange("p (i c) -> p i c", c=GW)
        cxp = sb("cxp", [P, 2, BLK + 2])
        xbp = sb("xbp", [P, 2, BLK + 3])
        xcv = sb("xcv", [P, 2, BLK])
        ktok = xcv[:, :, :].rearrange("p j n -> p (j n)").rearrange("p (i c) -> p i c", c=GW)
        tmp = [sb(f"tmp{i}", [P, BLK]) for i in range(4)]
        S = sb("S", [P, CPB, 2 * P])
        kdt = sb("kdt", [P, TPB, P])
        vt = sb("vt", [P, TPB, GW])
        dec = sb("dec", [P, CPB])
        sq = [sb(f"sq{i}", [P, BLK]) for i in range(2)]
        rsh = [sb(f"rsh{i}", [P, BLK]) for i in range(2)]
        hst = sb("hst", [P, 2])
        stout = sb("stout", [P, 12])
        strow = sb("strow", [12, P])
        carry = sb("carry", [P, TPB * HEADS])
        wraw = [sb(f"wraw{i}", [P, KT, P]) for i in range(2)]
        w_hi = [sb(f"w_hi{i}", [P, KT, P], F32R) for i in range(2)]
        w_lo = [sb(f"w_lo{i}", [P, KT, P], F32R) for i in range(2)]
        att = nc.alloc_sbuf_tensor_at("att", [P, 2 * KT, BLK], F32, offset=halves_at)
        aR, aW, aT = ([att[:, at + 2 * i:at + 2 * i + 2, :] for i in range(2)] for at in (0, 4, 8))
        aC = osb = att[:, 12:14, :]
        um = att[:, 14, 0:GW]

        def banks(name):
            return ctx.enter_context(nc.psum_tensor(name, [P, 2, 512], F32))

        zp2, tp2, zs2, ob2 = banks("zp"), banks("tp"), banks("zs"), banks("ob")
        zp, tp, zs = ([v[:, i, :] for i in range(2)] for v in (zp2, tp2, zs2))
        ob, st = ob2[:, 0, :], ob2[:, 1, :]
        score_banks = [zs2, zp2]

        x_loaded, tp_full, tp_free = sem("x_loaded"), sem("tp_full"), sem("tp_free")
        zp_full, zp_free, st_free, dh_ready = sem("zp_full"), sem("zp_free"), sem("st_free"), sem("dh_ready")
        sq_ready, sq_used = sem("sq_ready"), sem("sq_used")
        rs_ready, norm_done = sem("rs_ready"), sem("norm_done")
        hf_ready, hi_ready, lo_ready = sem("hf_ready"), sem("hi_ready"), sem("lo_ready")
        w_in_sem = [sem("w_loaded0"), sem("w_loaded1")]
        w_hi_ready, w_lo_ready = sem("w_hi_ready"), sem("w_lo_ready")
        y_ready, gd_ready, kdec_ready, kd_ready = sem("y_ready"), sem("gd_ready"), sem("kdec_ready"), sem("kd_ready")
        u_full, u_used, s_ready = sem("u_full"), sem("u_used"), sem("s_ready")
        xcv_ready, halo_ready = sem("xcv_ready"), sem("halo_ready")
        rgate, rg_u, rg_sqrt, rg_done = sem("rgate"), sem("rg_u"), sem("rg_sqrt"), sem("rg_done")
        gelu_ready, silu_ready, d_ready = sem("gelu_ready"), sem("silu_ready"), sem("d_ready")
        kst_placed, ktok_stored, v_placed = sem("kst_placed"), sem("ktok_stored"), sem("v_placed")
        oh_ready, ol_ready, mixed, x1_ready, x1_stored = (
            sem("oh_ready"), sem("ol_ready"), sem("mixed"), sem("x1_ready"), sem("x1_stored"))
        sc_full, l_ready, x_done, w_ready, wtp_full, wt_ready, pv_done = (
            sem("sc_full"), sem("l_ready"), sem("x_done"), sem("w_ready"), sem("wtp_full"),
            sem("wt_ready"), sem("pv_done"))
        osb_ready, ot_full, ot_done = sem("osb_ready"), sem("ot_full"), sem("ot_done")
        act_c, act_a, dve_c, dve_a = sem("act_c"), sem("act_a"), sem("dve_c"), sem("dve_a")
        init_ok, q_zero, state_in, past_in, halo_zero, stout_ready, strow_full, strow_ready, out_stored = (
            sem("init_ok"), sem("q_zero"), sem("state_in"), sem("past_in"), sem("halo_zero"), sem("stout_ready"),
            sem("strow_full"), sem("strow_ready"), sem("out_stored"))

        win_v = w_in[0].rearrange("(k p) n -> p k n", p=P)
        wout_v = w_out[0].rearrange("(k p) n -> p k n", p=P)
        pastk_v = cache_sb_k[0, 0].rearrange("(i p) h d -> p i (h d)", p=P)
        pastv_v = cache_sb_v[0, 0].rearrange("(i p) h d -> p i (h d)", p=P)

        def strip_src(u):
            return win_v[:, :, STRIPS_IN[u][2]:STRIPS_IN[u][2] + P] if u < N_IN_STRIPS else \
                wout_v[:, :, (u - N_IN_STRIPS) * P:(u - N_IN_STRIPS + 1) * P]

        PAIRS = 2 * TPB

        def pairs_before(b):
            return (PAIRS // 2) * b * (b + 1)

        def pairs_after(b, sample):
            return N_PAIRS + 4 if sample else pairs_before(b) + PAIRS * (b + 1)

        N_PAIRS = pairs_before(NBLK)
        block = ctx.enter_context(nc.Block())

        def tp_base(b, sample):
            return b * TP_PER + (2 if sample else 0)

        def shape_of(sample):
            return (DEC, 1, 1, DEC) if sample else (BLK, TPB, CPB, P)

        def attend(eng, b, sample, key_block):
            rows = shape_of(sample)[3]
            q = N_PAIRS if sample else pairs_before(b)
            key_block(q, lambda s: rows * (s + 1), True, lambda: 1 if sample else b * -1 + (NBLK - 1))
            if sample:
                key_block(q + 2, lambda s: PAST, False, lambda: 0)
            elif not isinstance(b, int):
                with eng.Fori(1, b + 1) as c:
                    key_block(q + PAIRS * c, lambda s: BLK, False, lambda: nc.s_assert_within(
                        b * -1 + c + (NBLK - 1), 0, NBLK - 1, skip_runtime_bounds_check_because="c <= b"))

        @block.sync
        def _(sp):
            def store_states(gla, rgh, rgc, scc, n, last_step):
                sp.wait_ge(s_ready, last_step)
                slot = (CPB - 1) if n == 0 else 0
                for h in range(HEADS):
                    sp.dma_start(gla[0, 0, h], S[32 * h:32 * h + 32, slot, HD * h:HD * h + HD]).then_inc(out_stored, 16)
                sp.wait_ge(strow_ready, n + 1)
                sp.dma_start(rgh[0].rearrange("a (j p) -> (a j) p", p=P), strow[0:2, :]).then_inc(out_stored, 16)
                sp.dma_start(rgc[0, 0].rearrange("i (j p) -> (i j) p", p=P), strow[2:8, :]).then_inc(out_stored, 16)
                sp.dma_start(scc[0, 0].rearrange("i (j p) -> (i j) p", p=P), strow[8:12, :]).then_inc(out_stored, 16)

            def load_strip(g, u):
                wait(sp, w_hi_ready, g - 1)
                wait(sp, w_lo_ready, g - 1)
                sp.dma_start(wraw[u % 2][:, :, :], strip_src(u)).then_inc(w_in_sem[u % 2], 16)

            def body(b, sample):
                wait(sp, oh_ready, b * KT)
                wait(sp, ol_ready, b * KT)
                if sample:
                    sp.dma_start(xrow[0:DEC, 0, :], x_sample[0]).then_inc(x_loaded, 16)
                else:
                    sp.dma_start(xrow[:, :, :], x_prompt[0, bass.ds(b * BLK, BLK), :].rearrange("(i p) n -> p i n", p=P)
                                 ).then_inc(x_loaded, 16)
                for u in range(2, N_STRIPS if sample else N_STRIPS + 2):
                    load_strip(b * N_STRIPS + u, u % N_STRIPS)

            load_strip(0, 0)
            load_strip(1, 1)
            body(0, False)
            with sp.Fori(1, NBLK) as b:
                body(b, False)
            store_states(gla_p, rgh_p, rgc_p, scc_p, 0, NBLK * CPB)
            sp.wait_ge(out_stored, 16 * (HEADS + 3))
            sp.wait_ge(init_ok, 2)
            for h in range(HEADS):
                sp.dma_start(S[32 * h:32 * h + 32, CPB - 1, HD * h:HD * h + HD], state_gla[0, 0, h]).then_inc(state_in, 16)
            sp.wait_ge(pv_done, N_PAIRS)
            sp.dma_start(Vb[:, 0:PAST // P, :], pastv_v).then_inc(past_in, 16)
            sp.dma_start(ktok[:, :, :], pastk_v).then_inc(past_in, 16)
            sp.wait_ge(past_in, 32)
            body(NBLK, True)
            store_states(gla_s, rgh_s, rgc_s, scc_s, 1, NBLK * CPB + 1)
            sp.wait_ge(out_stored, 32 * (HEADS + 3))
            sp.wait_ge(x1_stored, 16 * KT * (NBLK + 1))
            sp.wait_ge(ktok_stored, 16 * (NBLK + 1))
            sp.wait_ge(v_placed, 32 * (NBLK + 1))
            sp.wait_ge(kst_placed, 16 * (NBLK + 1))

        @block.gpsimd
        def _(pool):
            pool.memset(qp[:, :, :], 0.0).then_inc(q_zero, 1)

            def strip_lo(g, slot, used):
                pool.wait_ge(w_hi_ready, g + 1)
                wait(pool, zp_full, used)
                pool.tensor_tensor(w_lo[slot][:, :, :], wraw[slot][:, :, :], w_hi[slot][:, :, :].bitcast(F32),
                                   ALU.subtract).then_inc(w_lo_ready, 1)

            def body(b, sample):
                n = shape_of(sample)[0]
                for f in range(KT):
                    pool.wait_ge(hi_ready, b * KT + f + 1)
                    pool.tensor_tensor(hn_lo[:, f, 0:n], tmp[f % 2][:, 0:n], hn_hi[:, f, 0:n].bitcast(F32),
                                       ALU.subtract).then_inc(lo_ready, 1)
                for u in range(N_STRIPS):
                    if u == N_IN_STRIPS:
                        for f in range(KT):
                            pool.wait_ge(oh_ready, b * KT + f + 1)
                            pool.tensor_tensor(hn_lo[:, f, 0:n], oT[:, f, 0:n], hn_hi[:, f, 0:n].bitcast(F32),
                                               ALU.subtract).then_inc(ol_ready, 1)
                    if not (sample and u >= N_STRIPS - 2):
                        strip_lo(b * N_STRIPS + u + 2, u % 2, b * ZP_PER + STRIP_USE[u] + 1)

            strip_lo(0, 0, 0)
            strip_lo(1, 1, 0)
            body(0, False)
            with pool.Fori(1, NBLK) as b:
                body(b, False)
            body(NBLK, True)

        act_links = {}

        @block.scalar
        def _(act):
            chain, achain = Chain(act, act_c), Chain(act, act_a)

            def strip_hi(g, slot, loads, used):
                act.wait_ge(w_in_sem[slot], 16 * loads)
                wait(act, zp_full, used)
                act.activation(w_hi[slot][:, :, :], wraw[slot][:, :, :], ACT.Copy).then_inc(w_hi_ready, 1)

            def body(b, sample):
                n, tiles, chunks, rows = shape_of(sample)
                m = 1 if sample else 0
                chain.at(b * act_links.get("block", 0))
                zb, tb, qb = b * ZP_PER, tp_base(b, sample), b * SQ_PER

                def evac(u, dst, src=None, func=ACT.Copy, **more):
                    act.wait_ge(zp_full, zb + u + 1)
                    src = zp[u % 2][:, 0:n] if src is None else src
                    return act.activation(dst, src, func, **more)

                def evac_tp(u, dst, src):
                    act.wait_ge(tp_full, tb + u + 1)
                    act.activation(dst, src, ACT.Copy).then_inc(tp_free, 1)

                def next_hi(u):
                    if not (sample and u + 2 >= N_STRIPS):
                        strip_hi(b * N_STRIPS + u + 2, u % 2, b * (N_STRIPS // 2) + (u + 2) // 2 + 1,
                                 zb + STRIP_USE[u] + 1)

                def norm(k):
                    t = NORM_ORDER[k]
                    wait(act, sq_used, qb + KT + k - 1)
                    act.activation(sq[k % 2][:, 0:n], oT[:, t, 0:n], ACT.Square).then_inc(sq_ready, 1)
                    act.wait_ge(sq_used, qb + KT + k + 1)
                    wait(act, norm_done, b * KT + k - 1)
                    act.activation(rsh[k % 2][:, 0:n], st[:, 0:n], ACT.Ln, scale=1.0 / HD,
                                   bias=eps[:, 0:1]).then_inc(st_free, 1)
                    act.wait_ge(st_free, b * ST_PER + k + 2)
                    act.activation(rsh[k % 2][:, 0:n], rsh[k % 2][:, 0:n], ACT.Exp, scale=-0.5).then_inc(rs_ready, 1)

                act.preload_act_table_set(EXP_LN)
                wait(act, x1_stored, 16 * KT * b)
                wait(act, norm_done, b * KT)
                for f in range(KT):
                    act.wait_ge(tp_full, tb + TP_X + f + 1)
                    wait(act, sq_used, qb + f - 1)
                    act.activation(sq[f % 2][:, 0:n], tp[f % 2][:, 0:n], ACT.Square).then_inc(sq_ready, 1)
                    act.activation(xT[:, f, 0:n], tp[f % 2][:, 0:n], ACT.Copy).then_inc(tp_free, 1)
                act.wait_ge(sq_used, qb + KT)
                act.activation(tmp[2][:, 0:n], st[:, 0:n], ACT.Ln, scale=1.0 / D_MODEL,
                               bias=eps[:, 0:1]).then_inc(st_free, 1)
                act.wait_ge(st_free, b * ST_PER + 1)
                act.activation(tmp[2][:, 0:n], tmp[2][:, 0:n], ACT.Exp, scale=-0.5).then_inc(rs_ready, 1)
                for f in range(KT):
                    act.wait_ge(hf_ready, b * KT + f + 1)
                    act.activation(hn_hi[:, f, 0:n], tmp[f % 2][:, 0:n], ACT.Copy).then_inc(hi_ready, 1)

                evac(ZP_LRA, lra[:, 0:n], zp[ZP_LRA % 2][0:RANK, 0:n]).then_inc(zp_free, 1)
                dst_a = [qa[:, 0:n], ka[:, 0:n], va[:, 0, 0:n], va[:, 1, 0:n], ra[:, 0, 0:n], ra[:, 1, 0:n]]
                for i in range(6):
                    evac(ZP_A + i, dst_a[i], scale=GLA_DK ** -0.5 if i == 0 else 1.0).then_inc(zp_free, 1)
                    next_hi(i)
                act.wait_ge(q_zero, 1)
                for i in range(6):
                    u, j = ZP_C + i, i % 2
                    if i < 2:
                        evac(u, qp[0:HD, 2 * j, 0:n], zp[u % 2][0:HD, 0:n], scale=HD ** -0.5)
                        evac(u, qp[HD:P, 2 * j + 1, 0:n], zp[u % 2][HD:P, 0:n], scale=HD ** -0.5).then_inc(zp_free, 1)
                    else:
                        if i == 2:
                            wait(act, kst_placed, 16 * b)
                            wait(act, rg_done, 2 * b)
                        evac(u, (kst if i < 4 else vst)[:, j, 0:n]).then_inc(zp_free, 1)
                    next_hi(6 + i)
                gba = prm2[:, R2_GBA:R2_GBA + 1]
                evac(ZP_Y, tmp[3][:, 0:n], func=ACT.Abs, bias=gba)
                evac(ZP_Y, tmp[2][:, 0:n], func=ACT.Identity, bias=gba).then_inc(zp_free, 1)
                act.wait_ge(zp_free, zb + ZP_Y + 1)
                chain.link(act.activation(tmp[3][:, 0:n], tmp[3][:, 0:n], ACT.Exp, scale=-1.0))
                act.activation(tmp[3][:, 0:n], tmp[3][:, 0:n], ACT.Ln, bias=1.0).then_inc(y_ready, 1)
                for u0, dst in ((TP_K, ktok), (TP_V, vtok), (TP_VA, vt)):
                    for j in range(2):
                        evac_tp(u0 + j, dst[0:rows, 0:tiles, j * P:(j + 1) * P],
                                tp[j][0:rows, 0:tiles * P].rearrange("p (i c) -> p i c", c=P))
                pos = 1 if sample else b * -1 + (NBLK - 1)
                act.wait_ge(tp_free, tb + TP_V + 2)
                act.dma_start(Kt[:, :, bass.ds(pos * BLK, n)], kst[:, :, 0:n]).then_inc(kst_placed, 16)
                if sample:
                    act.dma_start(sbk_s[0, 0].rearrange("t h d -> t (h d)"), ktok[0:DEC, 0, :]).then_inc(ktok_stored, 16)
                    act.dma_start(sbv_s[0, 0].rearrange("t h d -> t (h d)"), vtok[0:DEC, 0, :]).then_inc(v_placed, 16)
                    act.dma_start(Vb[0:DEC, TPB, :], vtok[0:DEC, 0, :]).then_inc(v_placed, 16)
                else:
                    for out, tok, done in ((sbk_p, ktok, ktok_stored), (sbv_p, vtok, v_placed)):
                        act.dma_start(out[0, 0, bass.ds(b * BLK, BLK)].rearrange("(i p) h d -> p i (h d)", p=P),
                                      tok[:, :, :]).then_inc(done, 16)
                    act.dma_start(Vb[:, bass.ds(pos * TPB, TPB), :], vtok[:, :, :]).then_inc(v_placed, 16)
                act.wait_ge(gd_ready, b + 1)
                act.activation(dec[:, 0:chunks], tmp[3][:, CHUNK - 1:n:CHUNK], ACT.Exp, scale=1.0 / GLA_TAU)
                act.activation(tmp[2][:, 0:n], tmp[2][:, 0:n], ACT.Exp, scale=1.0 / GLA_TAU).then_inc(kdec_ready, 1)
                act.wait_ge(halo_ready, b + 1)
                dst_b = [gb[:, 0, 0:n], gb[:, 1, 0:n], xbp[:, 0, 3:3 + n], xbp[:, 1, 3:3 + n]]
                for i in range(4):
                    evac(ZP_B + i, dst_b[i]).then_inc(zp_free, 1)
                    next_hi(12 + i)
                for i in range((tiles + 1) // 2):
                    w = min(2, tiles)
                    evac_tp(TP_KD + i, kdt[0:rows, 2 * i:2 * i + w, :],
                            tp[i % 2][0:rows, 0:w * P].rearrange("p (i c) -> p i c", c=P))
                act.wait_ge(dh_ready, b + 1)
                dst_d = [cd[:, 0, 0:n], cd[:, 1, 0:n], cxp[:, 0, 2:2 + n], cxp[:, 1, 2:2 + n],
                         bd[:, 0, 0:n], bd[:, 1, 0:n]]
                for i in range(6):
                    if i == 4:
                        act.wait_ge(v_placed, 32 * (b + 1))
                    evac(ZP_D + i, dst_d[i]).then_inc(zp_free, 1)
                    next_hi(16 + i)
                act.wait_ge(zp_free, zb + ZP_D + 6)
                act.activation(ra[:, :, 0:n], ra[:, :, 0:n], ACT.Silu).then_inc(silu_ready, 1)
                act.activation(gb[:, :, 0:n], gb[:, :, 0:n], ACT.Gelu_apprx_tanh).then_inc(gelu_ready, 1)
                act.wait_ge(kd_ready, b + 1)
                for j in range(2):
                    wait(act, rg_done, 2 * b + j)
                    evac(ZP_G + 2 * j, tmp[0][:, 0:n], func=ACT.Sigmoid,
                         bias=prm2[:, R2_RBA + j:R2_RBA + j + 1]).then_inc(zp_free, 1)
                    evac(ZP_G + 2 * j + 1, tmp[1][:, 0:n], func=ACT.Sigmoid,
                         bias=prm2[:, R2_RBX + j:R2_RBX + j + 1]).then_inc(zp_free, 1)
                    act.wait_ge(zp_free, zb + ZP_G + 2 * j + 2)
                    act.activation(tmp[2][:, 0:n], tmp[0][:, 0:n], ACT.Tanh, scale=mixc["c8"][:, 1, j:j + 1])
                    act.activation(tmp[0][:, 0:n], tmp[0][:, 0:n], ACT.Exp,
                                   scale=mixc["c8"][:, 0, j:j + 1]).then_inc(rgate, 1)
                    act.wait_ge(rg_u, 2 * b + j + 1)
                    act.activation(tmp[2][:, 0:n], tmp[2][:, 0:n], ACT.Sqrt).then_inc(rg_sqrt, 1)
                for j in range(2):
                    evac(ZP_O + j, oT[:, j, 0:n]).then_inc(zp_free, 1)
                act.preload_act_table_set(EXP_LN)
                act.wait_ge(d_ready, 2 * (b + 1))
                act.wait_ge(rg_done, 2 * (b + 1))
                act.wait_ge(zp_free, zb + ZP_O + 2)
                for k in range(6):
                    norm(k)

                def weights(q, i, w):
                    act.wait_ge(x_done, q + i + 1)
                    x = aW[i % 2][0:rows, :, 0:w]
                    act.activation(x, x, ACT.Exp).then_inc(w_ready, 1)

                def key_block(q, width, newest, place):
                    achain.at(2 * q)
                    for i in range(2 * tiles):
                        w = width(i // 2)
                        act.wait_ge(sc_full, q + i + 1)
                        lt = aR[i % 2][0:rows, :, 0:w]
                        achain.link(act.activation(lt, score_banks[i % 2][0:rows, :, 0:w], ACT.Abs))
                        achain.link(act.activation(lt, lt, ACT.Exp, scale=-1.0))
                        act.activation(lt, lt, ACT.Ln, bias=1.0).then_inc(l_ready, 1)
                        if i:
                            weights(q, i - 1, width((i - 1) // 2))
                    weights(q, 2 * tiles - 1, width(tiles - 1))

                attend(act, b, sample, key_block)
                act.wait_ge(pv_done, pairs_after(b, sample))
                if sample:
                    act.activation(osb[0:rows, 0, 0:GW], ob[0:rows, 0:GW], ACT.Copy).then_inc(osb_ready, 1)
                else:
                    act.activation(osb[:, :, :], ob2[:, :, :], ACT.Copy).then_inc(osb_ready, 1)
                act.wait_ge(ot_full, b + 1)
                act.activation(oT[:, 4:6, 0:n], tp2[:, :, 0:n], ACT.Copy).then_inc(ot_done, 1)
                act.wait_ge(ot_done, b + 1)
                for k in (6, 7):
                    norm(k)

                act.wait_ge(norm_done, KT * (b + 1))
                for f in range(KT):
                    act.activation(hn_hi[:, f, 0:n], oT[:, f, 0:n], ACT.Copy).then_inc(oh_ready, 1)
                def store(f):
                    act.wait_ge(x1_ready, b * KT + f + 1)
                    act.dma_start(x1_v[:, f, bass.ds(b * BLK, n)], xT[:, f, 0:n]).then_inc(x1_stored, 16)

                for f in range(KT):
                    wait(act, x1_ready, b * KT + f - 1)
                    evac(ZP_MIX + f, tmp[f % 2][:, 0:n], func=ACT.Identity,
                         scale=modT[:, M_G1 + f, m:m + 1]).then_inc(zp_free, 1)
                    next_hi(N_IN_STRIPS + f)
                    if f:
                        store(f - 1)
                store(KT - 1)
                if not sample:
                    assert act_links.setdefault("block", chain.n) == chain.n

            strip_hi(0, 0, 1, 0)
            strip_hi(1, 1, 1, 0)
            body(0, False)
            with act.Fori(1, NBLK) as b:
                body(b, False)
            for j in range(2):
                act.wait_ge(tp_full, NBLK * TP_PER + j + 1)
                act.activation(Kt[:, j, 0:PAST], tp[j][:, :], ACT.Copy).then_inc(tp_free, 1)
            body(NBLK, True)

        dve_links = {}

        @block.vector
        def _(dve):
            chain, achain = Chain(dve, dve_c), Chain(dve, dve_a)
            chain.at(0)
            chain.link(dve.memset(hst[:, :], 0.0))
            chain.link(dve.memset(S[:, CPB - 1, :], 0.0))
            dve.memset(xbp[:, :, 0:3], 0.0).then_inc(halo_ready, 1)
            dve.memset(cxp[:, :, 0:2], 0.0).then_inc(dh_ready, 1)
            setup_links = chain.n

            def body(b, sample):
                n, tiles, chunks, rows = shape_of(sample)
                m = 1 if sample else 0
                chain.at(setup_links + b * dve_links.get("block", 0) + (dve_links["between"] if sample else 0))
                zb = b * ZP_PER

                def norm(k):
                    t = NORM_ORDER[k]
                    dve.wait_ge(rs_ready, b * ST_PER + k + 2)
                    ins = dve.scalar_tensor_tensor(out=oT[:, t, 0:n], in0=oT[:, t, 0:n],
                                                   scalar=prm2[:, R2_ON + t:R2_ON + t + 1],
                                                   in1=rsh[k % 2][:, 0:n], op0=ALU.mult, op1=ALU.mult)
                    if t < 2:
                        chain.link(ins)
                        dve.wait_ge(silu_ready, b + 1)
                        ins = dve.tensor_tensor(oT[:, t, 0:n], oT[:, t, 0:n], ra[:, t, 0:n], ALU.mult)
                    ins.then_inc(norm_done, 1)

                dve.wait_ge(rs_ready, b * ST_PER + 1)
                for f in range(KT):
                    wait(dve, hi_ready, b * KT + f - 1)
                    wait(dve, lo_ready, b * KT + f - 1)
                    t = tmp[f % 2][:, 0:n]
                    chain.link(dve.tensor_tensor(t, xT[:, f, 0:n], tmp[2][:, 0:n], ALU.mult))
                    dve.tensor_scalar(t, t, gs1[:, f, m:m + 1], modT[:, M_SH1 + f, m:m + 1],
                                      ALU.mult, ALU.add).then_inc(hf_ready, 1)
                dve.wait_ge(y_ready, b + 1)
                la, g = tmp[2][:, 0:n], tmp[3][:, 0:n]
                chain.link(dve.scalar_tensor_tensor(out=la, in0=la, scalar=0.0, in1=g, op0=ALU.min, op1=ALU.subtract))
                chain.link(dve.tensor_tensor_scan(g, mixc["scan_mask"][:, 0:n], la, 0.0, ALU.mult, ALU.add))
                g3 = g.rearrange("p (c t) -> p c t", t=CHUNK)
                dve.tensor_tensor(la.rearrange("p (c t) -> p c t", t=CHUNK),
                                  g3[:, :, CHUNK - 1:CHUNK].to_broadcast([P, chunks, CHUNK]), g3,
                                  ALU.subtract).then_inc(gd_ready, 1)
                dve.wait_ge(kdec_ready, b + 1)
                dve.tensor_tensor(ka[:, 0:n], ka[:, 0:n], la, ALU.mult).then_inc(kd_ready, 1)
                dve.wait_ge(zp_free, zb + ZP_B + 4)
                dve.wait_ge(ktok_stored, 16 * (b + 1))
                for j in range(2):
                    y = xcv[:, j, 0:n]
                    chain.link(dve.tensor_scalar(y, xbp[:, j, 0:n], prm2[:, R2_RCW + j:R2_RCW + j + 1],
                                                 prm2[:, R2_RCB + j:R2_RCB + j + 1], ALU.mult, ALU.add))
                    for i in range(1, 4):
                        ins = dve.scalar_tensor_tensor(out=y, in0=xbp[:, j, i:i + n],
                                                       scalar=prm2[:, R2_RCW + 2 * i + j:R2_RCW + 2 * i + j + 1],
                                                       in1=y, op0=ALU.mult, op1=ALU.add)
                        if i < 3:
                            chain.link(ins)
                        else:
                            ins.then_inc(xcv_ready, 1)
                dve.tensor_copy(xbp[:, :, 0:3], xbp[:, :, n:n + 3]).then_inc(halo_ready, 1)
                dve.wait_ge(zp_free, zb + ZP_D + 6)
                chain.link(dve.tensor_tensor(cxp[:, :, 2:2 + n], cd[:, :, 0:n], cxp[:, :, 2:2 + n], ALU.mult))
                for j in range(2):
                    y = oT[:, 6 + j, 0:n]
                    chain.link(dve.tensor_scalar(y, cxp[:, j, 0:n], prm2[:, R2_SCW + j:R2_SCW + j + 1], None, ALU.mult))
                    for i in range(1, 3):
                        chain.link(dve.scalar_tensor_tensor(
                            out=y, in0=cxp[:, j, i:i + n], scalar=prm2[:, R2_SCW + 2 * i + j:R2_SCW + 2 * i + j + 1],
                            in1=y, op0=ALU.mult, op1=ALU.add))
                    dve.tensor_tensor(y, y, bd[:, j, 0:n], ALU.mult).then_inc(d_ready, 1)
                dve.tensor_copy(cxp[:, :, 0:2], cxp[:, :, n:n + 2]).then_inc(dh_ready, 1)
                if sample:
                    dve.wait_ge(state_in, 16 * HEADS)
                for c in range(chunks):
                    dve.wait_ge(u_full, b * CPB + c + 1)
                    dve.tensor_tensor(um[:, :], zs[c % 2][:, 0:GW], mixc["bd_mask"][:, :], ALU.mult).then_inc(u_used, 1)
                    dve.wait_ge(u_used, b * CPB + c + 1)
                    dve.scalar_tensor_tensor(out=S[:, c, :], in0=S[:, (c - 1) % CPB, :], scalar=dec[:, c:c + 1],
                                             in1=um[:, :], op0=ALU.mult, op1=ALU.add).then_inc(s_ready, 1)
                    dve.wait_ge(s_ready, b * CPB + c + 1)
                for j in range(2):
                    a, u, v, w = (tmp[i][:, 0:n] for i in range(4))
                    y = oT[:, 2 + j, 0:n]
                    dve.wait_ge(zp_free, zb + ZP_G + 2 * j + 2)
                    dve.wait_ge(rgate, 2 * b + j + 1)
                    chain.link(dve.tensor_tensor(u, u, xcv[:, j, 0:n], ALU.mult))
                    chain.link(dve.tensor_tensor(w, a, a, ALU.mult))
                    dve.scalar_tensor_tensor(out=v, in0=w, scalar=1.0, in1=v, op0=ALU.add, op1=ALU.mult).then_inc(rg_u, 1)
                    dve.wait_ge(rg_sqrt, 2 * b + j + 1)
                    chain.link(dve.tensor_tensor(u, v, u, ALU.mult))
                    chain.link(dve.tensor_tensor_scan(y, a, u, hst[:, j:j + 1], ALU.mult, ALU.add))
                    chain.link(dve.tensor_copy(hst[:, j:j + 1], oT[:, 2 + j, n - 1:n]))
                    dve.wait_ge(gelu_ready, b + 1)
                    dve.tensor_tensor(y, y, gb[:, j, 0:n], ALU.mult).then_inc(rg_done, 1)
                for k in range(6):
                    norm(k)

                def turned(q, i, w):
                    dve.wait_ge(wtp_full, q + i + 1)
                    wait(dve, pv_done, q + i - 1)
                    kr, nk = (w, 1) if w < P else (P, w // P)
                    dve.tensor_copy(aT[i % 2][0:kr, :, 0:nk * rows], tp2[0:kr, :, 0:nk * rows]).then_inc(wt_ready, 1)

                def key_block(q, width, newest, place):
                    achain.at(2 * q)
                    for i in range(2 * tiles):
                        w = width(i // 2)
                        z, r, cc, x = (v[0:rows, :, 0:w] for v in (score_banks[i % 2], aR[i % 2], aC, aW[i % 2]))
                        sums = carry[0:rows, 2 * i:2 * i + 2]
                        dve.wait_ge(l_ready, q + i + 1)
                        achain.link(dve.scalar_tensor_tensor(out=r, in0=z, scalar=0.0, in1=r, op0=ALU.max, op1=ALU.add))
                        for j in range(2):
                            ins = dve.tensor_tensor_scan(cc[:, j, ::-1], r[:, j, ::-1], r[:, j, ::-1],
                                                         0.0 if newest else sums[:, j:j + 1], ALU.add, ALU.max)
                        achain.link(ins)
                        dve.tensor_copy(sums, cc[:, :, 0])
                        dve.tensor_tensor(x, z, cc, ALU.subtract).then_inc(x_done, 1)
                        if i:
                            turned(q, i - 1, width((i - 1) // 2))
                    turned(q, 2 * tiles - 1, width(tiles - 1))

                attend(dve, b, sample, key_block)
                for k in (6, 7):
                    norm(k)
                for f in range(KT):
                    dve.wait_ge(zp_free, zb + ZP_MIX + f + 1)
                    dve.tensor_tensor(xT[:, f, 0:n], xT[:, f, 0:n], tmp[f % 2][:, 0:n], ALU.add).then_inc(x1_ready, 1)
                if not sample:
                    assert dve_links.setdefault("block", chain.n) == chain.n

            def gather_states(i):
                chain.link(dve.tensor_copy(stout[:, 0:2], hst[:, :]))
                chain.link(dve.tensor_copy(stout[:, 2:8].rearrange("p (i j) -> p j i", j=2), xbp[:, :, 0:3]))
                dve.tensor_copy(stout[:, 8:12].rearrange("p (i j) -> p j i", j=2), cxp[:, :, 0:2]).then_inc(stout_ready, 1)
                dve.wait_ge(strow_full, i + 1)
                dve.tensor_copy(strow[:, :], ob[0:12, 0:P]).then_inc(strow_ready, 1)

            body(0, False)
            with dve.Fori(1, NBLK) as b:
                body(b, False)
            chain.at(setup_links + NBLK * dve_links["block"])
            gather_states(0)
            dve.wait_ge(out_stored, 16 * (HEADS + 3))
            dve.memset(S[:, CPB - 1, :], 0.0).then_inc(init_ok, 1)
            chain.link(dve.tensor_copy(hst[:, :], prm2[:, R2_H:R2_H + 2]))
            chain.link(dve.tensor_copy(xbp[:, :, 0:3], prm2[:, R2_RBUF:R2_RBUF + 6].rearrange("p (i j) -> p j i", j=2)))
            chain.link(dve.tensor_copy(cxp[:, :, 0:2], prm2[:, R2_SBUF:R2_SBUF + 4].rearrange("p (i j) -> p j i", j=2)))
            dve.memset(carry[:, :], 0.0).then_inc(init_ok, 1)
            dve_links["between"] = chain.n
            body(NBLK, True)
            chain.at(chain.base + chain.n)
            gather_states(1)

        @block.tensor
        def _(pe):
            def body(b, sample):
                n, tiles, chunks, rows = shape_of(sample)
                zb, tb, qb = b * ZP_PER, tp_base(b, sample), b * SQ_PER
                idr = ident[0:rows, 0:rows]

                def use(u):
                    wait(pe, zp_free, zb + u - 1)
                    return zp[u % 2]

                def turn(u, parts):
                    wait(pe, tp_free, tb + u - 1)
                    for dst, src, idt in parts:
                        ins = pe.transpose(dst, src, idt)
                    ins.then_inc(tp_full, 1)

                def product3(out, hi, lo):
                    for k in range(KT):
                        pe.matmul(out, hi(k), hn_hi[:, k, 0:n], start=(k == 0), stop=False)
                        pe.matmul(out, hi(k), hn_lo[:, k, 0:n], start=False, stop=False)
                        ins = pe.matmul(out, lo(k), hn_hi[:, k, 0:n], start=False, stop=(k == KT - 1))
                    return ins

                def strip(i):
                    g, slot = b * N_STRIPS + i, i % 2
                    pe.wait_ge(w_hi_ready, g + 1)
                    pe.wait_ge(w_lo_ready, g + 1)
                    bank = use(STRIP_USE[i])
                    product3(bank[:, 0:n], lambda k: w_hi[slot][:, k, :], lambda k: w_lo[slot][:, k, :]).then_inc(zp_full, 1)

                def norm(k):
                    pe.wait_ge(sq_ready, qb + KT + k + 1)
                    pe.wait_ge(st_free, b * ST_PER + k + 1)
                    pe.matmul(st[:, 0:n], head_ones[:, :], sq[k % 2][:, 0:n], start=True, stop=True).then_inc(sq_used, 1)

                def sum_squares(f):
                    pe.wait_ge(sq_ready, qb + f + 1)
                    pe.matmul(st[:, 0:n], ones[:, :], sq[f % 2][:, 0:n], start=(f == 0), stop=(f == KT - 1)).then_inc(sq_used, 1)

                pe.wait_ge(x_loaded, 16 * (b + 1))
                wait(pe, st_free, b * ST_PER)
                for f in range(KT):
                    turn(TP_X + f, [(tp[f % 2][:, i * rows:(i + 1) * rows], xrow[0:rows, i, f * P:(f + 1) * P], idr)
                                    for i in range(tiles)])
                    if f:
                        sum_squares(f - 1)
                sum_squares(KT - 1)
                pe.wait_ge(hi_ready, KT * (b + 1))
                pe.wait_ge(lo_ready, KT * (b + 1))
                bank = use(ZP_LRA)
                product3(bank[:, 0:n], lambda k: mixc["lra_hi"][:, k * RANK:k * RANK + P],
                         lambda k: mixc["lra_lo"][:, k * RANK:k * RANK + P]).then_inc(zp_full, 1)
                for i in range(12):
                    strip(i)
                bank = use(ZP_Y)
                pe.matmul(bank[:, 0:n], mixc["wa2"][:, :], lra[:, 0:n], start=True, stop=True).then_inc(zp_full, 1)
                for u0, src in ((TP_K, kst), (TP_V, vst), (TP_VA, va)):
                    pe.wait_ge(zp_free, zb + ZP_C + (4 if u0 == TP_K else 6))
                    for j in range(2):
                        turn(u0 + j, [(tp[j][0:rows, i * P:(i + 1) * P], src[:, j, i * rows:(i + 1) * rows], ident[:, :])
                                      for i in range(tiles)])
                for i in range(12, 16):
                    strip(i)
                pe.wait_ge(kd_ready, b + 1)
                for i in range((tiles + 1) // 2):
                    turn(TP_KD + i, [(tp[i % 2][0:rows, v * P:(v + 1) * P],
                                      ka[:, (2 * i + v) * rows:(2 * i + v + 1) * rows], ident[:, :])
                                     for v in range(min(2, tiles))])
                for i in range(16, 22):
                    strip(i)
                pe.wait_ge(tp_free, tb + TP_KD + (tiles + 1) // 2)
                for c in range(chunks):
                    r0 = CHUNK * (c % 2)
                    wait(pe, u_used, b * CPB + c - 1)
                    pe.matmul(zs[c % 2][:, 0:GW], kdt[r0:r0 + CHUNK, c // 2, :], vt[r0:r0 + CHUNK, c // 2, :],
                              start=True, stop=True).then_inc(u_full, 1)
                pe.wait_ge(xcv_ready, 2 * (b + 1))
                for j in range(2):
                    for g in range(2):
                        bank = use(ZP_G + 2 * j + g)
                        pe.matmul(bank[:, 0:n], mixc["rgw"][:, g, j, :], xcv[:, j, 0:n], start=True,
                                  stop=True).then_inc(zp_full, 1)
                pe.wait_ge(s_ready, b * CPB + chunks)
                for j in range(2):
                    bank = use(ZP_O + j)
                    for c in range(chunks):
                        ins = pe.matmul(bank[:, c * CHUNK:(c + 1) * CHUNK], S[:, c, j * P:(j + 1) * P],
                                        qa[:, c * CHUNK:(c + 1) * CHUNK], start=True, stop=True)
                    ins.then_inc(zp_full, 1)
                for k in range(6):
                    norm(k)

                pe.wait_ge(kst_placed, 16 * (b + 1))
                pe.wait_ge(v_placed, 32 * (b + 1))

                def key_block(q, width, newest, place):
                    at, vtile = place() * BLK, place() * TPB
                    if not isinstance(at, int):
                        at, vtile = pe.snap(at), pe.snap(vtile)

                    def score(i):
                        s, w = i // 2, width(i // 2)
                        wait(pe, x_done, q + i - 1)
                        for j in range(2):
                            bank = score_banks[i % 2][0:rows, j, 0:w]
                            ins = pe.matmul(bank, qp[:, 2 * (i % 2) + j, s * rows:(s + 1) * rows],
                                            Kt[:, i % 2, bass.ds(at, w)], start=True, stop=not newest)
                            if newest:
                                ins = pe.matmul(score_banks[i % 2][0:rows, j, w - rows:w], idr,
                                                mixc["neg_mask"][0:rows, 0:rows], start=False, stop=True)
                        ins.then_inc(sc_full, 1)

                    def turn_weights(i):
                        w = width(i // 2)
                        kr, nk = (w, 1) if w < P else (P, w // P)
                        pe.wait_ge(w_ready, q + i + 1)
                        wait(pe, wt_ready, q + i)
                        for j in range(2):
                            for v in range(nk):
                                ins = pe.transpose(tp2[0:kr, j, v * rows:(v + 1) * rows],
                                                   aW[i % 2][0:rows, j, v * kr:(v + 1) * kr], idr)
                        ins.then_inc(wtp_full, 1)

                    def values(i):
                        s, w = i // 2, width(i // 2)
                        kr, nk = (w, 1) if w < P else (P, w // P)
                        pe.wait_ge(wt_ready, q + i + 1)
                        for j in range(2):
                            cols = slice(HD * (2 * (i % 2) + j), HD * (2 * (i % 2) + j + 1))
                            at_col = GW * (s % 2) + cols.start
                            for v in range(nk):
                                ins = pe.matmul(ob2[0:rows, s // 2, at_col:at_col + HD],
                                                aT[i % 2][0:kr, j, v * rows:(v + 1) * rows],
                                                Vb[0:kr, vtile + v, cols] if isinstance(vtile, int) else
                                                Vb[0:kr, bass.ds(vtile + v, 1), cols],
                                                start=(newest and i % 4 == 0 and j == 0 and v == 0), stop=False,
                                                skip_group_check=True)
                        ins.then_inc(pv_done, 1)

                    score(0)
                    score(1)
                    for i in range(2 * tiles):
                        if i + 2 < 2 * tiles:
                            score(i + 2)
                        if i:
                            values(i - 1)
                        turn_weights(i)
                    values(2 * tiles - 1)

                pe.wait_ge(zp_free, zb + ZP_O + 2)
                pe.wait_ge(st_free, b * ST_PER + 7)
                attend(pe, b, sample, key_block)
                pe.wait_ge(osb_ready, b + 1)
                for s in range(tiles):
                    for j in range(2):
                        ins = pe.transpose(tp2[:, j, s * rows:(s + 1) * rows],
                                           osb[0:rows, s // 2, GW * (s % 2) + j * P:GW * (s % 2) + (j + 1) * P], idr)
                ins.then_inc(ot_full, 1)
                for k in (6, 7):
                    norm(k)
                pe.wait_ge(oh_ready, KT * (b + 1))
                pe.wait_ge(ol_ready, KT * (b + 1))
                for i in range(N_IN_STRIPS, N_STRIPS):
                    strip(i)

            def turn_states(i):
                pe.wait_ge(stout_ready, i + 1)
                pe.transpose(ob[0:12, 0:P], stout[:, :], ident[:, :]).then_inc(strow_full, 1)

            body(0, False)
            with pe.Fori(1, NBLK) as b:
                body(b, False)
            turn_states(0)
            pe.wait_ge(past_in, 32)
            for j in range(2):
                pe.wait_ge(tp_free, NBLK * TP_PER + j - 1)
                for i in range(PAST // P):
                    ins = pe.transpose(tp[j][:, i * P:(i + 1) * P], ktok[:, i, j * P:(j + 1) * P], ident[:, :])
                ins.then_inc(tp_full, 1)
            body(NBLK, True)
            turn_states(1)


def mlp_phase(nc, const, x1_v, mlp_w1, mlp_w2, y_prompt, y_sample):
    prm2, modT, gs2 = const["prm2"], const["modT"], const["gs2"]
    ident, ones, eps = const["ident"], const["ones"], const["eps"]
    NSB = 3
    T = N_TOK // NSB
    CB = T // 2
    NFT = D_FF // P
    NC = NFT // 2
    TILES = [P] * (T // P) + [T % P]
    assert SEQ == (NSB - 1) * T + T - DEC and CB % 2 == 0
    with ExitStack() as ctx:
        def sb(name, shape, dt=F32):
            return ctx.enter_context(nc.sbuf_tensor(name, shape, dt))

        def ps(name):
            return ctx.enter_context(nc.psum_tensor(name, [P, 512], F32))

        def sem(name):
            return ctx.enter_context(nc.semaphore(name))

        xs = [sb(f"xs{i}", [P, KT, T]) for i in range(2)]
        h_hi, h_lo = sb("h_hi", [P, KT, T], F32R), sb("h_lo", [P, KT, T], F32R)
        g_hi = [sb(f"g_hi{i}", [P, 2, T], F32R) for i in range(2)]
        g_lo = [sb(f"g_lo{i}", [P, 2, T], F32R) for i in range(2)]
        w1r = [sb(f"w1r{i}", [P, KT, P]) for i in range(2)]
        w1h = [sb(f"w1h{i}", [P, KT, P], F32R) for i in range(2)]
        w1l = [sb(f"w1l{i}", [P, KT, P], F32R) for i in range(2)]
        w2r = [sb(f"w2r{i}", [P, D_MODEL]) for i in range(2)]
        w2h = [sb(f"w2h{i}", [P, D_MODEL], F32R) for i in range(4)]
        w2l = [sb(f"w2l{i}", [P, D_MODEL], F32R) for i in range(4)]
        rt = [sb(f"rt{i}", [P, CB]) for i in range(2)]
        sqt = [sb(f"sqt{i}", [P, CB]) for i in range(2)]
        rms = [sb(f"rms{i}", [P, CB]) for i in range(2)]
        nsq, nacc = [sb(f"nsq{i}", [P, CB]) for i in range(2)], [sb(f"nacc{i}", [P, CB]) for i in range(2)]
        yrow = [sb(f"yrow{i}", [P, D_MODEL]) for i in range(2)]
        hp, op = [ps("hp0"), ps("hp1")], [ps(f"op{i}") for i in range(4)]
        stb = [ps("stb0"), ps("stb1")]

        x_in, w1_in, w2_in = [sem("x_in0"), sem("x_in1")], [sem("w1_in0"), sem("w1_in1")], [sem("w2_in0"), sem("w2_in1")]
        w1_hi, w1_lo, w2_hi, w2_lo = sem("w1_hi"), sem("w1_lo"), sem("w2_hi"), sem("w2_lo")
        n_sq, n_acc, n_sum, n_rms, n_rms_c = sem("n_sq"), sem("n_acc"), sem("n_sum"), sem("n_rms"), sem("n_rms_c")
        hf2, hi2, lo2, chain_d = sem("hf2"), sem("hi2"), sem("lo2"), sem("chain_d")
        h_full, h_relu, h_sq, gh_ready, gl_ready = (
            sem("h_full"), sem("h_relu"), sem("h_sq"), sem("gh_ready"), sem("gl_ready"))
        o_full, o_added, y_norm, yt_full, yt_read, y_out = (
            sem("o_full"), sem("o_added"), sem("y_norm"), sem("yt_full"), sem("yt_read"), [sem("y_out0"), sem("y_out1")])
        w1_v = mlp_w1[0].rearrange("(k p) n -> p k n", p=P)
        NT = NSB * NC
        N_YT = 2 * len(TILES)
        NV = 2 * KT
        NORMS = [("second", 0), ("second", 1), ("final", 0), ("second", 2), ("final", 1), ("final", 2)]
        block = ctx.enter_context(nc.Block())

        def each_chunk(eng, sbk, one):
            c = sbk * NC
            for j in range(4):
                one(c + j, j % 2, j)
            with eng.Fori(2, NC // 2 - 1) as i:
                one(c + 2 * i, 0, None)
                one(c + 2 * i + 1, 1, None)
            for j in (NC - 2, NC - 1):
                one(c + j, j % 2, j)

        def ranges(sbk, cb):
            if sbk == NSB - 1 and cb == 1:
                return [(0, CB - DEC, 0), (CB - DEC, CB, 1)]
            return [(0, CB, 0)]

        @block.sync
        def _(sp):
            def load_w(kind, g, slot, row):
                sems, hi, lo = (w1_in, w1_hi, w1_lo) if kind == 1 else (w2_in, w2_hi, w2_lo)
                wait(sp, hi, g - 1)
                wait(sp, lo, g - 1)
                if kind == 1:
                    sp.dma_start(w1r[slot][:, :, :], w1_v[:, :, bass.ds(row, P)]).then_inc(sems[slot], 16)
                else:
                    sp.dma_start(w2r[slot][:, :], mlp_w2[0, bass.ds(row, P), :]).then_inc(sems[slot], 16)

            def load_x(sbk):
                if sbk < NSB:
                    wait(sp, yt_read, (sbk - 1) * N_YT)
                    sp.dma_start(xs[sbk % 2][:, :, :], x1_v[:, :, sbk * T:(sbk + 1) * T]).then_inc(x_in[sbk % 2], 16)

            load_x(0)
            for kind in (1, 2):
                for j in range(2):
                    load_w(kind, j, j, j * P)
            def store_rows(sbk):
                for i, rows in enumerate(TILES):
                    sp.wait_ge(yt_read, sbk * N_YT + 2 * i + 2)
                    t0 = sbk * T + i * P
                    dst = y_prompt[0, t0:t0 + rows, :] if t0 < SEQ else y_sample[0, t0 - SEQ:t0 - SEQ + rows, :]
                    sp.dma_start(dst, yrow[i % 2][0:rows, :]).then_inc(y_out[i % 2], 16)

            load_x(1)
            for sbk in range(NSB):
                def loads(c, _, nth):
                    if isinstance(c, int) and c == NT - 1:
                        return
                    row = 0 if isinstance(c, int) and (c + 1) % NC == 0 else (c - sbk * NC + 1) * (2 * P)
                    for kind in (1, 2):
                        for j in range(2):
                            load_w(kind, 2 * c + 2 + j, j, row + j * P)
                    if nth == 3 and sbk:
                        store_rows(sbk - 1)
                        load_x(sbk + 1)

                each_chunk(sp, sbk, loads)
            store_rows(NSB - 1)
            for i in range(2):
                sp.wait_ge(y_out[i], 16 * NSB * len(TILES) // 2)

        @block.gpsimd
        def _(pool):
            def lo(kind, g, slot4, slot2, used):
                hi, done = (w1_hi, w1_lo) if kind == 1 else (w2_hi, w2_lo)
                pool.wait_ge(hi, g + 1)
                wait(pool, h_full if kind == 1 else o_full, used)
                if kind == 1:
                    pool.tensor_tensor(w1l[slot2][:, :, :], w1r[slot2][:, :, :], w1h[slot2][:, :, :].bitcast(F32),
                                       ALU.subtract).then_inc(done, 1)
                else:
                    pool.tensor_tensor(w2l[slot4][:, :], w2r[slot2][:, :], w2h[slot4][:, :].bitcast(F32),
                                       ALU.subtract).then_inc(done, 1)

            def sum_squares(kind, sbk):
                k = NORMS.index((kind, sbk))
                for f in range(1, KT):
                    for cb in range(2):
                        a = (k * (KT - 1) + f - 1) * 2 + cb
                        pool.wait_ge(n_sq, (k * KT + f) * 2 + cb + 1)
                        wait(pool, n_acc, a - 1)
                        pool.tensor_tensor(nacc[cb][:, :], nacc[cb][:, :], nsq[cb][:, :], ALU.add).then_inc(n_acc, 1)

            def h2_lo(sbk):
                for v in range(NV):
                    f, cb = v // 2, v % 2
                    pool.wait_ge(hi2, sbk * NV + v + 1)
                    cols = slice(cb * CB, (cb + 1) * CB)
                    pool.tensor_tensor(h_lo[:, f, cols], rt[cb][:, :], h_hi[:, f, cols].bitcast(F32),
                                       ALU.subtract).then_inc(lo2, 1)

            for kind in (1, 2):
                for j in range(2):
                    lo(kind, j, j, j, 0)
            sum_squares("second", 0)
            h2_lo(0)
            for sbk in range(NSB):
                def chunk(c, odd, nth):
                    more = not (isinstance(c, int) and c == NT - 1)
                    if more:
                        for j in range(2):
                            lo(1, 2 * c + 2 + j, 0, j, 4 * c + 2 * j + 2)
                    if nth == 0 and sbk:
                        sum_squares("final", sbk - 1)
                    if nth == NC - 2 and sbk + 1 < NSB:
                        sum_squares("second", sbk + 1)
                    if nth == NC - 1 and sbk + 1 < NSB:
                        h2_lo(sbk + 1)
                    if more:
                        for j in range(2):
                            lo(2, 2 * c + 2 + j, (2 * (odd + 1) + j) % 4, j, 16 * c)

                each_chunk(pool, sbk, chunk)
            sum_squares("final", NSB - 1)

        @block.scalar
        def _(act):
            def hi(kind, g, slot4, slot2, loads, used):
                act.wait_ge((w1_in if kind == 1 else w2_in)[slot2], 16 * loads)
                wait(act, h_full if kind == 1 else o_full, used)
                if kind == 1:
                    act.activation(w1h[slot2][:, :, :], w1r[slot2][:, :, :], ACT.Copy).then_inc(w1_hi, 1)
                else:
                    act.activation(w2h[slot4][:, :], w2r[slot2][:, :], ACT.Copy).then_inc(w2_hi, 1)

            def chunk(c, odd, between):
                more = not (isinstance(c, int) and c == NT - 1)
                for ft in range(2):
                    for cb in range(2):
                        i = 2 * ft + cb
                        h = 4 * c + i
                        act.wait_ge(h_full, h + 1)
                        wait(act, h_sq, h - 1)
                        act.activation(rt[i % 2][:, :], hp[i % 2][:, 0:CB], ACT.Relu).then_inc(h_relu, 1)
                        act.wait_ge(h_sq, h + 1)
                        wait(act, o_full, 16 * (c - 1) if isinstance(c, int) else 16 * c - 16)
                        act.activation(g_hi[odd][:, ft, cb * CB:(cb + 1) * CB], sqt[i % 2][:, :],
                                       ACT.Copy).then_inc(gh_ready, 1)
                    if more:
                        hi(1, 2 * c + 2 + ft, 0, ft, c + 2, 4 * c + 2 * ft + 2)
                between()
                if more:
                    for j in range(2):
                        hi(2, 2 * c + 2 + j, (2 * (odd + 1) + j) % 4, j, c + 2, 16 * c)

            def squares(kind, sbk):
                k, x = NORMS.index((kind, sbk)), xs[sbk % 2]
                if kind == "second":
                    act.wait_ge(x_in[sbk % 2], 16 * (sbk // 2 + 1))
                else:
                    act.wait_ge(o_added, (sbk + 1) * NC * 16)
                wait(act, n_sum, 2 * k)
                for f in range(KT):
                    for cb in range(2):
                        if f:
                            wait(act, n_acc, (k * (KT - 1) + f - 1) * 2 + cb - 1)
                        act.activation((nsq if f else nacc)[cb][:, :], x[:, f, cb * CB:(cb + 1) * CB],
                                       ACT.Square).then_inc(n_sq, 1)

            def inverse_rms(kind, sbk):
                k = NORMS.index((kind, sbk))
                if k:
                    before, third = NORMS[k - 1]
                    act.wait_ge(hf2 if before == "second" else y_norm, NV * (third + 1))
                for cb in range(2):
                    act.wait_ge(n_sum, 2 * k + cb + 1)
                    act.activation(rms[cb][:, :], stb[cb][:, 0:CB], ACT.Ln, scale=1.0 / D_MODEL,
                                   bias=eps[:, 0:1]).then_inc(n_rms_c, 1)
                for cb in range(2):
                    act.wait_ge(n_rms_c, 2 * k + cb + 1)
                    act.activation(rms[cb][:, :], rms[cb][:, :], ACT.Exp, scale=-0.5).then_inc(n_rms, 1)

            def h2_hi(sbk):
                for v in range(NV):
                    f, cb = v // 2, v % 2
                    act.wait_ge(hf2, sbk * NV + v + 1)
                    act.activation(h_hi[:, f, cb * CB:(cb + 1) * CB], rt[cb][:, :], ACT.Copy).then_inc(hi2, 1)

            def rows_of(sbk):
                for i, rows in enumerate(TILES):
                    for v in range(2):
                        u = sbk * N_YT + 2 * i + v
                        act.wait_ge(yt_full, u + 1)
                        wait(act, y_out[i % 2], 16 * ((sbk * len(TILES) + i) // 2))
                        act.activation(yrow[i % 2][0:rows, v * 512:(v + 1) * 512], stb[v][0:rows, :],
                                       ACT.Copy).then_inc(yt_read, 1)

            act.preload_act_table_set(EXP_LN)
            for kind in (1, 2):
                for j in range(2):
                    hi(kind, j, j, j, 1, 0)
            squares("second", 0)
            inverse_rms("second", 0)
            h2_hi(0)
            for sbk in range(NSB):
                act.wait_ge(lo2, (sbk + 1) * NV)

                def one(c, odd, nth):
                    def between():
                        if nth == 0 and sbk:
                            squares("final", sbk - 1)
                        if nth == 1 and sbk:
                            inverse_rms("final", sbk - 1)
                        if nth == 3 and sbk:
                            rows_of(sbk - 1)
                        if nth == NC - 2 and sbk + 1 < NSB:
                            squares("second", sbk + 1)
                        if nth == NC - 1 and sbk + 1 < NSB:
                            inverse_rms("second", sbk + 1)
                            h2_hi(sbk + 1)

                    chunk(c, odd, between)

                each_chunk(act, sbk, one)
            squares("final", NSB - 1)
            inverse_rms("final", NSB - 1)
            rows_of(NSB - 1)

        @block.vector
        def _(dve):
            chain = Chain(dve, chain_d)

            def hidden(c, odd):
                for i in range(4):
                    ft, cb = i // 2, i % 2
                    h = 4 * c + i
                    dve.wait_ge(h_relu, h + 1)
                    wait(dve, gh_ready, h - 1)
                    dve.tensor_tensor(sqt[i % 2][:, :], rt[i % 2][:, :], rt[i % 2][:, :], ALU.mult).then_inc(h_sq, 1)
                    dve.wait_ge(gh_ready, h + 1)
                    cols = slice(cb * CB, (cb + 1) * CB)
                    dve.tensor_tensor(g_lo[odd][:, ft, cols], sqt[i % 2][:, :], g_hi[odd][:, ft, cols].bitcast(F32),
                                      ALU.subtract).then_inc(gl_ready, 1)

            def add(c, sbk, between=lambda i: None):
                x = xs[sbk % 2]
                for d in range(KT):
                    for cb in range(2):
                        i = 2 * d + cb
                        dve.wait_ge(o_full, 16 * c + i + 1)
                        if i == 0:
                            wait(dve, o_added, 16 * c)
                        for n, (a, e, m) in enumerate(ranges(sbk, cb)):
                            cols = x[:, d, cb * CB + a:cb * CB + e]
                            ins = dve.scalar_tensor_tensor(out=cols, in0=op[i % 4][:, a:e],
                                                           scalar=modT[:, M_G2 + d, m:m + 1], in1=cols,
                                                           op0=ALU.mult, op1=ALU.add)
                        ins.then_inc(o_added, 1)
                        between(i)

            def h2(sbk, v):
                f, cb = v // 2, v % 2
                u = sbk * NV + v
                dve.wait_ge(n_rms, 2 * NORMS.index(("second", sbk)) + 2)
                wait(dve, hi2, u - 1)
                wait(dve, lo2, u - 1)
                chain.link(dve.tensor_tensor(rt[cb][:, :], xs[sbk % 2][:, f, cb * CB:(cb + 1) * CB], rms[cb][:, :],
                                             ALU.mult))
                for a, e, m in ranges(sbk, cb):
                    ins = dve.tensor_scalar(rt[cb][:, a:e], rt[cb][:, a:e], gs2[:, f, m:m + 1],
                                            modT[:, M_SH2 + f, m:m + 1], ALU.mult, ALU.add)
                ins.then_inc(hf2, 1)

            def final(sbk, v):
                f, cb = v // 2, v % 2
                dve.wait_ge(n_rms, 2 * NORMS.index(("final", sbk)) + 2)
                cols = xs[sbk % 2][:, f, cb * CB:(cb + 1) * CB]
                dve.scalar_tensor_tensor(out=cols, in0=cols, scalar=prm2[:, R2_FIN + f:R2_FIN + f + 1],
                                         in1=rms[cb][:, :], op0=ALU.mult, op1=ALU.mult).then_inc(y_norm, 1)

            for v in range(NV):
                h2(0, v)
            for sbk in range(NSB):
                def next_h2(early):
                    def between(i):
                        v = (i - 7) // 2 if early and i % 2 and i >= 7 else i + 5 if not early else NV
                        if sbk + 1 < NSB and v < NV:
                            h2(sbk + 1, v)
                    return between

                def chunk(c, odd, nth):
                    hidden(c, odd)
                    if nth == 0:
                        return
                    if nth == 2 and sbk:
                        add(c - 1, sbk, lambda i: final(sbk - 1, i))
                    elif nth == NC - 1:
                        add(c - 1, sbk, next_h2(True))
                    else:
                        add(c - 1, sbk)

                each_chunk(dve, sbk, chunk)
                add(sbk * NC + NC - 1, sbk, next_h2(False))
            dve.wait_ge(o_added, 16 * NT)
            for v in range(NV):
                final(NSB - 1, v)

        @block.tensor
        def _(pe):
            def hidden(c, odd):
                for ft in range(2):
                    pe.wait_ge(w1_hi, 2 * c + ft + 1)
                    pe.wait_ge(w1_lo, 2 * c + ft + 1)
                    for cb in range(2):
                        wait(pe, h_relu, 4 * c + 2 * ft + cb - 1)
                        cols, bank = slice(cb * CB, (cb + 1) * CB), hp[cb][:, 0:CB]
                        for k in range(KT):
                            pe.matmul(bank, w1h[ft][:, k, :], h_hi[:, k, cols], start=(k == 0), stop=False)
                            pe.matmul(bank, w1h[ft][:, k, :], h_lo[:, k, cols], start=False, stop=False)
                            ins = pe.matmul(bank, w1l[ft][:, k, :], h_hi[:, k, cols], start=False, stop=(k == KT - 1))
                        ins.then_inc(h_full, 1)

            def project(c, odd, between=lambda i: None):
                pe.wait_ge(gh_ready, 4 * c + 4)
                pe.wait_ge(gl_ready, 4 * c + 4)
                pe.wait_ge(w2_hi, 2 * c + 2)
                pe.wait_ge(w2_lo, 2 * c + 2)
                for d in range(KT):
                    for cb in range(2):
                        i = 2 * d + cb
                        wait(pe, o_added, 16 * c + i - 3)
                        cols, bank = slice(cb * CB, (cb + 1) * CB), op[i % 4][:, 0:CB]
                        for ft in range(2):
                            wh = w2h[2 * odd + ft][:, d * P:(d + 1) * P]
                            wl = w2l[2 * odd + ft][:, d * P:(d + 1) * P]
                            pe.matmul(bank, wh, g_hi[odd][:, ft, cols], start=(ft == 0), stop=False)
                            pe.matmul(bank, wh, g_lo[odd][:, ft, cols], start=False, stop=False)
                            ins = pe.matmul(bank, wl, g_hi[odd][:, ft, cols], start=False, stop=(ft == 1))
                        ins.then_inc(o_full, 1)
                        between(i)

            def norm(kind, sbk):
                k = NORMS.index((kind, sbk))
                pe.wait_ge(n_acc, 2 * (KT - 1) * (k + 1))
                wait(pe, n_rms_c, 2 * k)
                if ("final", 0) in NORMS[:k]:
                    pe.wait_ge(yt_read, N_YT * sum(kd == "final" for kd, _ in NORMS[:k]))
                for cb in range(2):
                    pe.matmul(stb[cb][:, 0:CB], ones[:, :], nacc[cb][:, :], start=True, stop=True).then_inc(n_sum, 1)

            def turn(sbk, u):
                i, v = u // 2, u % 2
                rows = TILES[i]
                pe.wait_ge(y_norm, (sbk + 1) * NV)
                pe.wait_ge(n_rms_c, 2 * NORMS.index(("final", sbk)) + 2)
                wait(pe, yt_read, sbk * N_YT + u - 1)
                for f in range(4):
                    ins = pe.transpose(stb[v][0:rows, f * P:(f + 1) * P],
                                       xs[sbk % 2][:, 4 * v + f, i * P:i * P + rows], ident[:, :])
                ins.then_inc(yt_full, 1)

            norm("second", 0)
            for sbk in range(NSB):
                pe.wait_ge(hi2, NV * (sbk + 1))
                pe.wait_ge(lo2, NV * (sbk + 1))

                def chunk(c, odd, nth):
                    hidden(c, odd)
                    if nth == NC - 1 and sbk + 1 < NSB:
                        norm("second", sbk + 1)
                    if nth == 0:
                        return
                    if nth == 1 and sbk:
                        project(c - 1, 1 - odd, lambda i: norm("final", sbk - 1) if i == 8 else None)
                    elif nth == 3 and sbk:
                        project(c - 1, 1 - odd, lambda i: turn(sbk - 1, i) if i < N_YT else None)
                    else:
                        project(c - 1, 1 - odd)

                each_chunk(pe, sbk, chunk)
                project(sbk * NC + NC - 1, 1)
            norm("final", NSB - 1)
            for u in range(N_YT):
                turn(NSB - 1, u)


_INS = ['x_prompt', 'x_sample', 'c_prompt', 'c_sample', 'state_gla', 'state_rg_h', 'state_rg_conv', 'cache_sb_k',
        'cache_sb_v', 'state_sc_conv', 'ln1_g', 'ln2_g', 'w_ada', 'b_ada', 'w_in', 'gla_wa2', 'gla_ba', 'rg_conv_w',
        'rg_conv_b', 'rg_wa', 'rg_ba', 'rg_wx', 'rg_bx', 'rg_lambda', 'sc_conv_w', 'out_norm_g', 'w_out', 'mlp_w1',
        'mlp_w2', 'final_g']
_OUTS = [(1, SEQ, D_MODEL), (1, DEC, D_MODEL), (1, 1, HEADS, GLA_DK, HD), (1, 1, HEADS, GLA_DK, HD),
         (1, 1, GW), (1, 1, GW), (1, 1, 3, GW), (1, 1, 3, GW), (1, 1, SEQ, HEADS, HD), (1, 1, DEC, HEADS, HD),
         (1, 1, SEQ, HEADS, HD), (1, 1, DEC, HEADS, HD), (1, 1, 2, GW), (1, 1, 2, GW)]


def kernel(**inputs):
    import numpy as _np
    import concourse.bacc as _bacc
    from concourse import mybir as _mybir
    from concourse.bass_utils import run_bass_kernel_spmd as _run

    nc = _bacc.Bacc("TRN2", target_bir_lowering=False, num_devices=1)
    arrays, args = {}, []
    for name in _INS:
        a = _np.ascontiguousarray(inputs[name])
        arrays[f"in_{name}_dram"] = a
        args.append(nc.dram_tensor(f"in_{name}_dram", a.shape, _mybir.dt.from_np(a.dtype), kind="ExternalInput").ap())
    for i, shape in enumerate(_OUTS):
        args.append(nc.dram_tensor(f"out_{i}_dram", shape, F32, kind="ExternalOutput").ap())
    build(nc, *args)
    r = _run(nc, [arrays], core_ids=[0])
    return tuple(r.results[0][f"out_{i}_dram"] for i in range(len(_OUTS)))
```

```python
from contextlib import ExitStack

import concourse.bass as bass
from concourse import mybir

ALU = mybir.AluOpType
ACT = mybir.ActivationFunctionType
F32 = mybir.dt.float32
F32R = mybir.dt.float32r

EXP_LN = "natural_log_exp_and_others"
P = 128
D_MODEL = 1024
KT = D_MODEL // P
SEQ = 2048
DEC = 64
PAST = 512
N_TOK = SEQ + DEC
BLK = 512
NBLK = SEQ // BLK
TPB = BLK // P
GW = D_MODEL // 4
HD = 64
HEADS = GW // HD
GLA_DK = 32
CHUNK = 64
CPB = BLK // CHUNK
RANK = 16
D_FF = 4 * D_MODEL
EPS = 1e-6
RG_C = 8.0
GLA_TAU = 16.0
NEG = -1e30

OFF_QA, OFF_KA, OFF_VA, OFF_LRA, OFF_RA, OFF_GB, OFF_XB = 0, 128, 256, 512, 528, 784, 1040
OFF_QC, OFF_KC, OFF_VC, OFF_BD, OFF_CD, OFF_XD = 1296, 1552, 1808, 2064, 2320, 2576

STRIPS_A = [("qa", 0, OFF_QA), ("ka", 0, OFF_KA), ("va", 0, OFF_VA), ("va", 1, OFF_VA + P),
            ("ra", 0, OFF_RA), ("ra", 1, OFF_RA + P)]
STRIPS_C = [(n, j, o + j * P) for n, o in (("qc", OFF_QC), ("kc", OFF_KC), ("vc", OFF_VC)) for j in range(2)]
STRIPS_B = [(n, j, o + j * P) for n, o in (("gb", OFF_GB), ("xb", OFF_XB)) for j in range(2)]
STRIPS_D = [(n, j, o + j * P) for n, o in (("cd", OFF_CD), ("xd", OFF_XD), ("bd", OFF_BD)) for j in range(2)]
STRIPS_IN = STRIPS_A + STRIPS_C + STRIPS_B + STRIPS_D
N_IN_STRIPS = len(STRIPS_IN)
N_STRIPS = N_IN_STRIPS + KT

ZP_LRA = 0
ZP_A = 1
ZP_C = ZP_A + 6
ZP_Y = ZP_C + 6
ZP_B = ZP_Y + 1
ZP_D = ZP_B + 4
ZP_G = ZP_D + 2
ZP_D2 = ZP_G + 4
ZP_O = ZP_D2 + 4
ZP_MIX = ZP_O + 2
ZP_PER = ZP_MIX + KT
STRIP_USE = ([ZP_A + i for i in range(6)] + [ZP_C + i for i in range(6)] + [ZP_B + i for i in range(4)]
             + [ZP_D + i for i in range(2)] + [ZP_D2 + i for i in range(4)] + [ZP_MIX + i for i in range(KT)])
TP_X = 0
TP_K = KT
TP_V = TP_K + 2
TP_VA = TP_V + 2
TP_KD = TP_VA + 2
TP_PER = TP_KD + 2
NORM_PAIRS = [2, 0, 6, 4]
NORM_C = 3
OUT_ORDER = [0, 1, 2, 3, 6, 7, 4, 5]
assert ZP_PER % 2 == 0 and TP_PER % 2 == 0 and N_STRIPS % 2 == 0

R1_BADA, R1_CP, R1_CS = 0, 48, 56
R2_LN1, R2_LN2, R2_FIN, R2_ON, R2_GBA = 0, 8, 16, 24, 32
R2_RCW, R2_RCB, R2_RBA, R2_RBX, R2_LAM, R2_SCW = 33, 41, 43, 45, 47, 49
R2_H, R2_RBUF, R2_SBUF, R2_ALL = 55, 57, 63, 67
M_SH1, M_SC1, M_G1, M_SH2, M_SC2, M_G2 = 0, 8, 16, 24, 32, 40


def wait(eng, sem, value):
    if not (isinstance(value, int) and value <= 0):
        eng.wait_ge(sem, value)


def rows_view(oT):
    return oT[:, :, :].rearrange("p k n -> p (k n)").rearrange("p (i n) -> p i n", n=D_MODEL)


class Chain:

    def __init__(self, eng, sem):
        self.eng, self.sem, self.base, self.n = eng, sem, 0, 0

    def at(self, base):
        self.base, self.n = base, 0

    def link(self, ins):
        self.n += 1
        ins.then_inc(self.sem, 1)
        self.eng.wait_ge(self.sem, self.base + self.n)


def build(nc, x_prompt, x_sample, c_prompt, c_sample, state_gla, state_rg_h, state_rg_conv,
          cache_sb_k, cache_sb_v, state_sc_conv, ln1_g, ln2_g, w_ada, b_ada, w_in, gla_wa2, gla_ba,
          rg_conv_w, rg_conv_b, rg_wa, rg_ba, rg_wx, rg_bx, rg_lambda, sc_conv_w, out_norm_g, w_out,
          mlp_w1, mlp_w2, final_g, y_prompt, y_sample, gla_p, gla_s, rgh_p, rgh_s, rgc_p, rgc_s,
          sbk_p, sbk_s, sbv_p, sbv_s, scc_p, scc_s):
    x1_dram = nc.dram_tensor("x1_scratch", (D_MODEL, N_TOK), F32, kind="Internal").ap()
    x1_v = x1_dram.rearrange("(f p) t -> p f t", p=P)
    with ExitStack() as ctx:
        def sb(name, shape, dt=F32):
            return ctx.enter_context(nc.sbuf_tensor(name, shape, dt))

        const = dict(
            ident=sb("ident", [P, P]), ones=sb("ones", [P, P]), head_ones=sb("head_ones", [P, P]),
            prm1=sb("prm1", [P, 64]), prm2=sb("prm2", [P, R2_ALL]), modT=sb("modT", [P, 48, 2]),
            gs1=sb("gs1", [P, KT, 2]), gs2=sb("gs2", [P, KT, 2]), eps=sb("eps", [P, 1]))
        mix_ctx = ExitStack()
        with mix_ctx:
            def mb(name, shape, dt=F32):
                return mix_ctx.enter_context(nc.sbuf_tensor(name, shape, dt))

            mixc = dict(
                oT=mb("oT", [P, KT, BLK]), x_loaded=mix_ctx.enter_context(nc.semaphore("x_loaded")),
                neg_mask=mb("neg_mask", [P, P]), bd_mask=mb("bd_mask", [P, 2 * P]),
                scan_mask=mb("scan_mask", [P, BLK]), rgw=mb("rgw", [P, 2, 2, P]), c8=mb("c8", [P, 2, 2]),
                wa2=mb("wa2", [RANK, P]), lra_hi=mb("lra_hi", [P, KT * RANK + P], F32R),
                lra_lo=mb("lra_lo", [P, KT * RANK + P], F32R))
            setup_phase(nc, const, mixc, x_prompt, c_prompt, c_sample, w_ada, b_ada, w_in, ln1_g, ln2_g, final_g,
                        out_norm_g, gla_ba, gla_wa2, rg_conv_w, rg_conv_b, rg_wa, rg_ba, rg_wx, rg_bx,
                        rg_lambda, sc_conv_w, state_rg_h, state_rg_conv, state_sc_conv)
            mixer_phase(nc, const, mixc, x_prompt, x_sample, state_gla, cache_sb_k, cache_sb_v, w_in, w_out,
                        x1_v, gla_p, gla_s, rgh_p, rgh_s, rgc_p, rgc_s, sbk_p, sbk_s, sbv_p, sbv_s,
                        scc_p, scc_s)
        mlp_phase(nc, const, x1_v, mlp_w1, mlp_w2, y_prompt, y_sample)


def setup_phase(nc, const, mixc, x_prompt, c_prompt, c_sample, w_ada, b_ada, w_in, ln1_g, ln2_g, final_g,
                out_norm_g, gla_ba, gla_wa2, rg_conv_w, rg_conv_b, rg_wa, rg_ba, rg_wx, rg_bx,
                rg_lambda, sc_conv_w, state_rg_h, state_rg_conv, state_sc_conv):
    CH = 512
    NCH = 6 * D_MODEL // CH
    CT = CH // P
    RING = 4
    with ExitStack() as ctx:
        def sb(name, shape, dt=F32):
            return ctx.enter_context(nc.sbuf_tensor(name, shape, dt))

        def sem(name):
            return ctx.enter_context(nc.semaphore(name))

        rows1, rows2 = sb("rows1", [64, P]), sb("rows2", [R2_ALL, P])
        wada = [sb(f"wada{i}", [P, KT, CH]) for i in range(RING)]
        wada_hi = [sb(f"wada_hi{i}", [P, KT, CH], F32R) for i in range(2)]
        wada_lo = [sb(f"wada_lo{i}", [P, KT, CH], F32R) for i in range(2)]
        chl = sb("chl", [P, KT, 4], F32R)
        mod_rows = sb("mod_rows", [4, 6 * D_MODEL])
        lra_raw = sb("lra_raw", [P, KT * RANK])
        csil = sb("csil", [P, 2, KT])
        lam = sb("lam", [P, 4, 2])
        pt = ctx.enter_context(nc.psum_tensor("pt", [P, 2, 512], F32))
        pr = ctx.enter_context(nc.psum_tensor("pr", [4, 2, CH], F32))
        pm = ctx.enter_context(nc.psum_tensor("pm", [P, 48, 4], F32))
        rows_in, wada_in = [sem("rows_in1"), sem("rows_in2")], [sem(f"wada_in{i}") for i in range(RING)]
        wada_hi_ok, wada_lo_ok, row_full, row_read, c_hi, c_lo = (
            sem("wada_hi_ok"), sem("wada_lo_ok"), sem("row_full"), sem("row_read"), sem("c_hi"), sem("c_lo"))
        zeroed, blocks_in, masks = sem("zeroed"), sem("blocks_in"), sem("masks")
        rows_t, prm, silu_c, mod_full = sem("rows_t"), sem("prm"), sem("silu_c"), sem("mod_full")
        act_chain, dve_chain, lra_hi_ok, lra_in, lam_a = (
            sem("act_chain"), sem("dve_chain"), sem("lra_hi_ok"), sem("lra_in"), sem("lam_a"))
        wa_v = w_ada[0].rearrange("(k p) n -> p k n", p=P)
        block = ctx.enter_context(nc.Block())

        def rows(v):
            return v.rearrange("a (r p) -> (a r) p", p=P)

        def load_wada(eng, c):
            wait(eng, wada_lo_ok, c - RING + 1)
            eng.dma_start(wada[c % RING][:, :, :], wa_v[:, :, c * CH:(c + 1) * CH]).then_inc(wada_in[c % RING], 16)

        @block.sync
        def _(sp):
            parts1 = [(R1_BADA, rows(b_ada)), (R1_CP, rows(c_prompt)), (R1_CS, rows(c_sample))]
            parts2 = [(R2_LN1, rows(ln1_g)), (R2_LN2, rows(ln2_g)),
                      (R2_FIN, final_g.rearrange("(r p) -> r p", p=P)), (R2_ON, rows(out_norm_g)),
                      (R2_GBA, rows(gla_ba)), (R2_RCW, rows(rg_conv_w[0])), (R2_RCB, rows(rg_conv_b)),
                      (R2_RBA, rows(rg_ba)), (R2_RBX, rows(rg_bx)), (R2_LAM, rows(rg_lambda)),
                      (R2_SCW, rows(sc_conv_w[0])), (R2_H, rows(state_rg_h[0])),
                      (R2_RBUF, rows(state_rg_conv[0, 0])), (R2_SBUF, rows(state_sc_conv[0, 0]))]

            def load_rows(tile, parts, done):
                for r, src in parts:
                    sp.dma_start(tile[r:r + src.shape[0], :], src).then_inc(done, 16)

            load_rows(rows1, parts1, rows_in[0])
            for c in range(0, NCH, 2):
                load_wada(sp, c)
                if c == 2:
                    load_rows(rows2, parts2, rows_in[1])
                    sp.dma_start(lra_raw[:, :].rearrange("p (k n) -> p k n", n=RANK),
                                 w_in[0].rearrange("(k p) n -> p k n", p=P)[:, :, OFF_LRA:OFF_LRA + RANK]
                                 ).then_inc(lra_in, 16)
                    sp.dma_start(mixc["wa2"][:, :], gla_wa2[0]).then_inc(blocks_in, 16)
                    sp.wait_ge(zeroed, 1)
                    for n in range(4):
                        for g, w in enumerate((rg_wa, rg_wx)):
                            sp.dma_start(mixc["rgw"][64 * (n % 2):64 * (n % 2) + 64, g, n // 2,
                                                     64 * (n % 2):64 * (n % 2) + 64], w[0, n]).then_inc(blocks_in, 16)
            sp.dma_start(rows_view(mixc["oT"]), x_prompt[0, 0:BLK, :].rearrange("(i p) n -> p i n", p=P)
                         ).then_inc(mixc["x_loaded"], 16)
            sp.wait_ge(blocks_in, 16 * 9)

        @block.gpsimd
        def _(pool):
            n = [0]

            def step(ins):
                n[0] += 1
                ins.then_inc(masks, 1)
                pool.wait_ge(masks, n[0])

            pool.memset(mixc["rgw"][:, :, :, :], 0.0).then_inc(zeroed, 1)
            step(pool.memset(const["ident"][:, :], 0.0))
            step(pool.affine_select(out=const["ident"][:, :], in_=const["ident"][:, :], compare_op=ALU.not_equal,
                                    fill=1.0, base=0, pattern=[[-1, P]], channel_multiplier=1))
            step(pool.memset(const["ones"][:, :], 1.0))
            step(pool.memset(const["eps"][:, :], EPS))
            step(pool.memset(const["head_ones"][:, :], 0.0))
            for i in range(2):
                step(pool.memset(const["head_ones"][64 * i:64 * i + 64, 64 * i:64 * i + 64], 1.0))
            step(pool.memset(mixc["bd_mask"][:, :], 0.0))
            for h in range(HEADS):
                step(pool.memset(mixc["bd_mask"][32 * h:32 * h + 32, HD * h:HD * h + HD], 1.0))
            step(pool.memset(mixc["scan_mask"][:, :], 1.0))
            step(pool.memset(mixc["scan_mask"][:, 0:BLK:CHUNK], 0.0))
            step(pool.memset(mixc["neg_mask"][:, :], 0.0))
            step(pool.affine_select(out=mixc["neg_mask"][:, :], in_=mixc["neg_mask"][:, :], compare_op=ALU.is_ge,
                                    fill=NEG, base=-1, pattern=[[-1, P]], channel_multiplier=1))

        @block.scalar
        def _(act):
            chain = Chain(act, act_chain)
            for c in range(1, RING, 2):
                load_wada(act, c)
            act.wait_ge(prm, 1)
            act.activation(csil[:, :, :], const["prm1"][:, R1_CP:64].rearrange("p (c k) -> p c k", c=2),
                           ACT.Silu).then_inc(silu_c, 1)
            act.wait_ge(silu_c, 1)
            act.activation(chl[:, :, 0:2], csil[:, :, :].rearrange("p c k -> p k c"), ACT.Copy).then_inc(c_hi, 1)
            act.wait_ge(lra_in, 16)
            act.activation(mixc["lra_hi"][:, 0:KT * RANK], lra_raw[:, :], ACT.Copy).then_inc(lra_hi_ok, 1)
            act.wait_ge(prm, 2)
            chain.link(act.activation(lam[:, 0, :], const["prm2"][:, R2_LAM:R2_LAM + 2], ACT.Abs))
            chain.link(act.activation(lam[:, 1, :], lam[:, 0, :], ACT.Exp, scale=-1.0))
            act.activation(lam[:, 2, :], lam[:, 1, :], ACT.Ln, bias=1.0).then_inc(lam_a, 1)
            for c in range(NCH):
                act.wait_ge(wada_in[c % RING], 16 * (c // RING + 1))
                wait(act, row_full, c - 1)
                act.activation(wada_hi[c % 2][:, :, :], wada[c % RING][:, :, :], ACT.Copy).then_inc(wada_hi_ok, 1)
                if c >= 1 and c % 2 == 0 and c + RING - 1 < NCH:
                    load_wada(act, c + RING - 1)

        @block.vector
        def _(dve):
            chain = Chain(dve, dve_chain)
            chain.link(dve.memset(mixc["lra_hi"][:, KT * RANK:].bitcast(F32), 0.0))
            chain.link(dve.memset(mixc["lra_lo"][:, KT * RANK:].bitcast(F32), 0.0))
            dve.wait_ge(rows_t, 1)
            dve.tensor_copy(const["prm1"][:, :], pt[:, 0, 0:64]).then_inc(prm, 1)
            dve.wait_ge(rows_t, 2)
            dve.tensor_copy(const["prm2"][:, :], pt[:, 1, 0:R2_ALL]).then_inc(prm, 1)
            dve.wait_ge(lra_hi_ok, 1)
            dve.tensor_tensor(mixc["lra_lo"][:, 0:KT * RANK], lra_raw[:, :],
                              mixc["lra_hi"][:, 0:KT * RANK].bitcast(F32), ALU.subtract)
            dve.wait_ge(prm, 2)
            chain.link(dve.tensor_scalar(lam[:, 3, :], const["prm2"][:, R2_LAM:R2_LAM + 2], -1.0, 0.0,
                                         ALU.mult, ALU.max))
            dve.wait_ge(lam_a, 1)
            chain.link(dve.tensor_tensor(lam[:, 3, :], lam[:, 3, :], lam[:, 2, :], ALU.add))
            chain.link(dve.tensor_scalar(mixc["c8"][:, 0, :], lam[:, 3, :], -RG_C, None, ALU.mult))
            chain.link(dve.tensor_scalar(mixc["c8"][:, 1, :], lam[:, 3, :], RG_C, None, ALU.mult))
            dve.wait_ge(silu_c, 1)
            dve.wait_ge(c_hi, 1)
            dve.tensor_tensor(chl[:, :, 2:4], csil[:, :, :].rearrange("p c k -> p k c"),
                              chl[:, :, 0:2].bitcast(F32), ALU.subtract).then_inc(c_lo, 1)

            def take_row(c):
                dve.wait_ge(row_full, c + 1)
                dve.tensor_copy(mod_rows[:, c * CH:(c + 1) * CH], pr[:, c % 2, :]).then_inc(row_read, 1)

            for c in range(NCH):
                dve.wait_ge(wada_hi_ok, c + 1)
                dve.tensor_tensor(wada_lo[c % 2][:, :, :], wada[c % RING][:, :, :],
                                  wada_hi[c % 2][:, :, :].bitcast(F32), ALU.subtract).then_inc(wada_lo_ok, 1)
                if c:
                    take_row(c - 1)
            take_row(NCH - 1)
            dve.wait_ge(mod_full, 1)
            for c in range(2):
                chain.link(dve.tensor_tensor(const["modT"][:, :, c], pm[:, :, c],
                                             const["prm1"][:, R1_BADA:R1_BADA + 48], ALU.add))
                chain.link(dve.tensor_tensor(const["modT"][:, :, c], const["modT"][:, :, c], pm[:, :, 2 + c],
                                             ALU.add))
            for gs, m, g in ((const["gs1"], M_SC1, R2_LN1), (const["gs2"], M_SC2, R2_LN2)):
                for c in range(2):
                    chain.link(dve.scalar_tensor_tensor(
                        out=gs[:, :, c], in0=const["modT"][:, m:m + KT, c], scalar=1.0,
                        in1=const["prm2"][:, g:g + KT], op0=ALU.add, op1=ALU.mult))

        @block.tensor
        def _(pe):
            pe.wait_ge(rows_in[0], 16 * 3)
            pe.wait_ge(masks, 2)
            pe.transpose(pt[:, 0, 0:64], rows1[:, :], const["ident"][0:64, 0:64]).then_inc(rows_t, 1)
            pe.wait_ge(rows_in[1], 16 * 14)
            pe.transpose(pt[:, 1, 0:R2_ALL], rows2[:, :], const["ident"][0:R2_ALL, 0:R2_ALL]).then_inc(rows_t, 1)
            pe.wait_ge(c_lo, 1)

            def turn_row(c):
                pe.wait_ge(row_read, c + 1)
                for t in range(CT):
                    ins = pe.transpose(pm[:, c * CT + t, :], mod_rows[:, c * CH + t * P:c * CH + (t + 1) * P],
                                       const["ident"][0:4, 0:4])
                return ins

            for c in range(NCH):
                pe.wait_ge(wada_lo_ok, c + 1)
                wait(pe, row_read, c - 1)
                for k in range(KT):
                    pe.matmul(pr[:, c % 2, :], chl[:, k, :], wada_hi[c % 2][:, k, :], start=(k == 0), stop=False)
                    ins = pe.matmul(pr[:, c % 2, :], chl[:, k, :], wada_lo[c % 2][:, k, :], start=False,
                                    stop=(k == KT - 1))
                ins.then_inc(row_full, 1)
                if c:
                    turn_row(c - 1)
            turn_row(NCH - 1).then_inc(mod_full, 1)


def mixer_phase(nc, const, mixc, x_prompt, x_sample, state_gla, cache_sb_k, cache_sb_v, w_in, w_out,
                x1_v, gla_p, gla_s, rgh_p, rgh_s, rgc_p, rgc_s, sbk_p, sbk_s, sbv_p, sbv_s, scc_p, scc_s):
    prm2, modT, gs1 = const["prm2"], const["modT"], const["gs1"]
    ident, ones, head_ones, eps = const["ident"], const["ones"], const["head_ones"], const["eps"]
    with ExitStack() as ctx:
        def sb(name, shape, dt=F32):
            return ctx.enter_context(nc.sbuf_tensor(name, shape, dt))

        def sem(name):
            return ctx.enter_context(nc.semaphore(name))

        xT = sb("xT", [P, KT, BLK])
        halves_at = nc.sbuf_base
        hn_hi, hn_lo = sb("hn_hi", [P, KT, BLK], F32R), sb("hn_lo", [P, KT, BLK], F32R)
        oT, x_loaded = mixc["oT"], mixc["x_loaded"]
        xrow = rows_view(oT)
        Kt = sb("Kt", [P, 2, SEQ])
        Vb = sb("Vb", [P, SEQ // P, GW])
        qp = sb("qp", [P, HEADS, BLK])
        kst = sb("kst", [P, 2, BLK])
        vst = sb("vst", [P, 2, BLK])
        gb = vst
        qa, ka = sb("qa", [P, BLK]), sb("ka", [P, BLK])
        va = sb("va", [P, 2, BLK])
        cd = va
        ra = sb("ra", [P, 2, BLK])
        lra = sb("lra", [RANK, BLK])
        bd = sb("bd", [P, 2, BLK])
        vtok = bd[:, :, :].rearrange("p j n -> p (j n)").rearrange("p (i c) -> p i c", c=GW)
        cxp = sb("cxp", [P, 2, BLK + 2])
        xbp = sb("xbp", [P, 2, BLK + 3])
        xcv = sb("xcv", [P, 2, BLK])
        ktok = xcv[:, :, :].rearrange("p j n -> p (j n)").rearrange("p (i c) -> p i c", c=GW)
        tmp = [sb(f"tmp{i}", [P, BLK]) for i in range(4)]
        htmp = [tmp[0], tmp[1], tmp[3]]
        S = sb("S", [P, CPB, 2 * P])
        kdt = sb("kdt", [P, TPB, P])
        vt = sb("vt", [P, TPB, GW])
        dec = sb("dec", [P, CPB])
        sq2, rs2 = sb("sq", [P, 2, BLK]), sb("rsh", [P, 2, BLK])
        sq = [sq2[:, i, :] for i in range(2)]
        hst = sb("hst", [P, 2])
        stout = sb("stout", [P, 12])
        strow = sb("strow", [12, P])
        carry = sb("carry", [P, TPB * HEADS])
        wraw = [sb(f"wraw{i}", [P, KT, P]) for i in range(2)]
        w_halves_at = nc.sbuf_base
        w_hi = [sb(f"w_hi{i}", [P, KT, P], F32R) for i in range(2)]
        w_lo = [sb(f"w_lo{i}", [P, KT, P], F32R) for i in range(2)]
        w_more = nc.alloc_sbuf_tensor_at("w_more", [P, 4, KT, P], F32, offset=w_halves_at)
        w_whole = [v[:, :, :] for v in wraw] + [w_more[:, i, :, :] for i in range(4)]
        RING_S = len(w_whole)
        att = nc.alloc_sbuf_tensor_at("att", [P, 2 * KT, BLK], F32, offset=halves_at)
        aR, aW, aT = ([att[:, at + 2 * i:at + 2 * i + 2, :] for i in range(2)] for at in (0, 4, 8))
        aC = osb = att[:, 12:14, :]
        um, rg_v, rg_w = rs2[:, 0, 0:GW], sq2, rs2[:, 1, :]
        h_whole = att[:, 0:KT, :]

        def banks(name):
            return ctx.enter_context(nc.psum_tensor(name, [P, 2, 512], F32))

        zp2, tp2, zs2, ob2 = banks("zp"), banks("tp"), banks("zs"), banks("ob")
        zp, tp, zs = ([v[:, i, :] for i in range(2)] for v in (zp2, tp2, zs2))
        ob, st = ob2[:, 0, :], ob2[:, 1, :]
        nsq = [att[:, 2 * g:2 * g + 2, :] for g in range(NORM_C)] + [sq2]
        nrs = [att[:, 6 + 2 * g:8 + 2 * g, :] for g in range(NORM_C)] + [rs2]
        norm_bank = [tp2, zs2, ob2, zs2]
        score_banks = [zs2, zp2]

        tp_full, tp_free = sem("tp_full"), sem("tp_free")
        zp_full, zp_free, st_free, dh_ready = sem("zp_full"), sem("zp_free"), sem("st_free"), sem("dh_ready")
        sq_ready, sq_used = sem("sq_ready"), sem("sq_used")
        rs_ready, norm_done = sem("rs_ready"), sem("norm_done")
        nsq_ready, nsum_full, nln_ready, nrs_ready = (
            sem("nsq_ready"), sem("nsum_full"), sem("nln_ready"), sem("nrs_ready"))
        hf_ready, hi_ready = sem("hf_ready"), sem("hi_ready")
        lo_ready, ol_ready = [sem("lo_pool"), sem("lo_dve")], [sem("ol_pool"), sem("ol_dve")]
        w_in_sem = [sem("w_loaded0"), sem("w_loaded1")]
        w_hi_ready, w_lo_ready = sem("w_hi_ready"), sem("w_lo_ready")
        whole_in = [sem(f"whole_in{i}") for i in range(RING_S)]
        y_ready, gd_ready, kdec_ready, kd_ready = sem("y_ready"), sem("gd_ready"), sem("kdec_ready"), sem("kd_ready")
        u_full, u_used, s_ready = sem("u_full"), sem("u_used"), sem("s_ready")
        xcv_ready, halo_ready = sem("xcv_ready"), sem("halo_ready")
        rgate, rg_u, rg_sqrt, rg_done = sem("rgate"), sem("rg_u"), sem("rg_sqrt"), sem("rg_done")
        gelu_ready, silu_ready, d_ready = sem("gelu_ready"), sem("silu_ready"), sem("d_ready")
        kst_placed, ktok_stored, v_placed = sem("kst_placed"), sem("ktok_stored"), sem("v_placed")
        oh_ready, x1_ready, x1_stored = sem("oh_ready"), sem("x1_ready"), sem("x1_stored")
        sc_full, l_ready, x_done, w_ready, wtp_full, wt_ready, pv_done = (
            sem("sc_full"), sem("l_ready"), sem("x_done"), sem("w_ready"), sem("wtp_full"),
            sem("wt_ready"), sem("pv_done"))
        osb_ready, ot_full, ot_done = sem("osb_ready"), sem("ot_full"), sem("ot_done")
        act_c, act_a, dve_c, dve_a = sem("act_c"), sem("act_a"), sem("dve_c"), sem("dve_a")
        init_ok, q_zero, state_in, past_in, halo_zero, stout_ready, strow_full, strow_ready, out_stored = (
            sem("init_ok"), sem("q_zero"), sem("state_in"), sem("past_in"), sem("halo_zero"), sem("stout_ready"),
            sem("strow_full"), sem("strow_ready"), sem("out_stored"))

        win_v = w_in[0].rearrange("(k p) n -> p k n", p=P)
        wout_v = w_out[0].rearrange("(k p) n -> p k n", p=P)
        pastk_v = cache_sb_k[0, 0].rearrange("(i p) h d -> p i (h d)", p=P)
        pastv_v = cache_sb_v[0, 0].rearrange("(i p) h d -> p i (h d)", p=P)

        def strip_src(u):
            return win_v[:, :, STRIPS_IN[u][2]:STRIPS_IN[u][2] + P] if u < N_IN_STRIPS else \
                wout_v[:, :, (u - N_IN_STRIPS) * P:(u - N_IN_STRIPS + 1) * P]

        PAIRS = 2 * TPB

        def pairs_before(b):
            return (PAIRS // 2) * b * (b + 1)

        def pairs_after(b, sample):
            return N_PAIRS + 4 if sample else pairs_before(b) + PAIRS * (b + 1)

        N_PAIRS = pairs_before(NBLK)
        block = ctx.enter_context(nc.Block())

        def tp_base(b, sample):
            return b * TP_PER + (2 if sample else 0)

        def shape_of(sample):
            return (DEC, 1, 1, DEC) if sample else (BLK, TPB, CPB, P)

        def attend(eng, b, sample, key_block):
            rows = shape_of(sample)[3]
            q = N_PAIRS if sample else pairs_before(b)
            key_block(q, lambda s: rows * (s + 1), True, lambda: 1 if sample else b * -1 + (NBLK - 1))
            if sample:
                key_block(q + 2, lambda s: PAST, False, lambda: 0)
            elif not isinstance(b, int):
                with eng.Fori(1, b + 1) as c:
                    key_block(q + PAIRS * c, lambda s: BLK, False, lambda: nc.s_assert_within(
                        b * -1 + c + (NBLK - 1), 0, NBLK - 1, skip_runtime_bounds_check_because="c <= b"))

        @block.sync
        def _(sp):
            def store_states(gla, rgh, rgc, scc, n, last_step):
                sp.wait_ge(s_ready, last_step)
                slot = (CPB - 1) if n == 0 else 0
                for h in range(HEADS):
                    sp.dma_start(gla[0, 0, h], S[32 * h:32 * h + 32, slot, HD * h:HD * h + HD]).then_inc(out_stored, 16)
                sp.wait_ge(strow_ready, n + 1)
                sp.dma_start(rgh[0].rearrange("a (j p) -> (a j) p", p=P), strow[0:2, :]).then_inc(out_stored, 16)
                sp.dma_start(rgc[0, 0].rearrange("i (j p) -> (i j) p", p=P), strow[2:8, :]).then_inc(out_stored, 16)
                sp.dma_start(scc[0, 0].rearrange("i (j p) -> (i j) p", p=P), strow[8:12, :]).then_inc(out_stored, 16)

            def load_strip(g, u):
                wait(sp, w_hi_ready, g - 1)
                wait(sp, w_lo_ready, g - 1)
                sp.dma_start(wraw[u % 2][:, :, :], strip_src(u)).then_inc(w_in_sem[u % 2], 16)

            def load_whole(u):
                if u < RING_S:
                    sp.wait_ge(zp_full, NBLK * ZP_PER)
                    sp.wait_ge(w_hi_ready, NBLK * N_STRIPS + 2)
                    sp.wait_ge(w_lo_ready, NBLK * N_STRIPS + 2)
                else:
                    sp.wait_ge(zp_full, NBLK * ZP_PER + STRIP_USE[u - RING_S] + 1)
                sp.dma_start(w_whole[u % RING_S], strip_src(u)).then_inc(whole_in[u % RING_S], 16)

            def load_tokens(b, sample):
                for i in range(2):
                    wait(sp, ol_ready[i], b * (KT // 2))
                if sample:
                    sp.dma_start(xrow[0:DEC, 0, :], x_sample[0]).then_inc(x_loaded, 16)
                else:
                    sp.dma_start(xrow[:, :, :], x_prompt[0, bass.ds(b * BLK, BLK), :].rearrange("(i p) n -> p i n", p=P)
                                 ).then_inc(x_loaded, 16)

            LATE = N_IN_STRIPS + 4

            def early(b):
                for u in range(2, LATE):
                    load_strip(b * N_STRIPS + u, u)

            def late(after):
                for u in range(LATE, N_STRIPS + 2):
                    load_strip(after * N_STRIPS + (u - N_STRIPS), u % N_STRIPS)

            load_strip(0, 0)
            load_strip(1, 1)
            early(0)
            with sp.Fori(1, NBLK) as b:
                load_tokens(b, False)
                late(b)
                early(b)
            sp.wait_ge(pv_done, N_PAIRS)
            sp.dma_start(Vb[:, 0:PAST // P, :], pastv_v).then_inc(past_in, 16)
            sp.dma_start(ktok[:, :, :], pastk_v).then_inc(past_in, 16)
            load_tokens(NBLK, True)
            late(NBLK)
            store_states(gla_p, rgh_p, rgc_p, scc_p, 0, NBLK * CPB)
            for u in range(2, RING_S):
                load_whole(u)
            sp.wait_ge(init_ok, 2)
            for h in range(HEADS):
                sp.dma_start(S[32 * h:32 * h + 32, CPB - 1, HD * h:HD * h + HD], state_gla[0, 0, h]).then_inc(state_in, 16)
            for u in range(RING_S, N_STRIPS):
                load_whole(u)
            store_states(gla_s, rgh_s, rgc_s, scc_s, 1, NBLK * CPB + 1)
            sp.wait_ge(out_stored, 32 * (HEADS + 3))
            sp.wait_ge(x1_stored, 16 * KT * (NBLK + 1))
            sp.wait_ge(ktok_stored, 16 * (NBLK + 1))
            sp.wait_ge(v_placed, 32 * (NBLK + 1))
            sp.wait_ge(kst_placed, 16 * (NBLK + 1))

        @block.gpsimd
        def _(pool):
            pool.memset(qp[:, :, :], 0.0).then_inc(q_zero, 1)

            def strip_lo(g, slot, used):
                pool.wait_ge(w_hi_ready, g + 1)
                wait(pool, zp_full, used)
                pool.tensor_tensor(w_lo[slot][:, :, :], wraw[slot][:, :, :], w_hi[slot][:, :, :].bitcast(F32),
                                   ALU.subtract).then_inc(w_lo_ready, 1)

            def body(b):
                n = BLK
                for f in range(0, KT, 2):
                    pool.wait_ge(hi_ready, b * KT + f + 1)
                    pool.tensor_tensor(hn_lo[:, f, 0:n], htmp[f % 3][:, 0:n], hn_hi[:, f, 0:n].bitcast(F32),
                                       ALU.subtract).then_inc(lo_ready[0], 1)
                if isinstance(b, int):
                    strip_lo(0, 0, 0)
                    strip_lo(1, 1, 0)
                for u in range(N_STRIPS):
                    if u == N_IN_STRIPS:
                        for i in range(0, KT, 2):
                            f = OUT_ORDER[i]
                            pool.wait_ge(oh_ready, b * KT + i + 1)
                            pool.tensor_tensor(hn_lo[:, f, 0:n], oT[:, f, 0:n], hn_hi[:, f, 0:n].bitcast(F32),
                                               ALU.subtract).then_inc(ol_ready[0], 1)
                    strip_lo(b * N_STRIPS + u + 2, u % 2, b * ZP_PER + STRIP_USE[u] + 1)

            body(0)
            with pool.Fori(1, NBLK) as b:
                body(b)

        act_links = {}

        @block.scalar
        def _(act):
            chain, achain = Chain(act, act_c), Chain(act, act_a)

            def strip_hi(g, slot, loads, used):
                act.wait_ge(w_in_sem[slot], 16 * loads)
                wait(act, zp_full, used)
                act.activation(w_hi[slot][:, :, :], wraw[slot][:, :, :], ACT.Copy).then_inc(w_hi_ready, 1)

            def body(b, sample):
                n, tiles, chunks, rows = shape_of(sample)
                m = 1 if sample else 0
                chain.at(b * act_links.get("block", 0))
                zb, tb, qb = b * ZP_PER, tp_base(b, sample), b * KT

                def evac(u, dst, src=None, func=ACT.Copy, **more):
                    act.wait_ge(zp_full, zb + u + 1)
                    src = zp[u % 2][:, 0:n] if src is None else src
                    return act.activation(dst, src, func, **more)

                def evac_tp(u, dst, src):
                    act.wait_ge(tp_full, tb + u + 1)
                    act.activation(dst, src, ACT.Copy).then_inc(tp_free, 1)

                def next_hi(u):
                    if not sample:
                        strip_hi(b * N_STRIPS + u + 2, u % 2, b * (N_STRIPS // 2) + (u + 2) // 2 + 1,
                                 zb + STRIP_USE[u] + 1)

                def norm_squares(g):
                    t = NORM_PAIRS[g]
                    act.activation(nsq[g][:, :, 0:n], oT[:, t:t + 2, 0:n], ACT.Square).then_inc(nsq_ready, 1)

                def norm_ln(g):
                    act.wait_ge(nsum_full, 4 * b + g + 1)
                    act.activation(nrs[g][:, :, 0:n], norm_bank[g][:, :, 0:n], ACT.Ln, scale=1.0 / HD,
                                   bias=eps[:, 0:1]).then_inc(nln_ready, 1)

                def norm_exp(g):
                    act.wait_ge(nln_ready, 4 * b + g + 1)
                    act.activation(nrs[g][:, :, 0:n], nrs[g][:, :, 0:n], ACT.Exp, scale=-0.5).then_inc(nrs_ready, 1)

                def out_hi(i):
                    act.activation(hn_hi[:, OUT_ORDER[i], 0:n], oT[:, OUT_ORDER[i], 0:n], ACT.Copy).then_inc(oh_ready, 1)

                act.preload_act_table_set(EXP_LN)
                wait(act, x1_stored, 16 * KT * b)
                wait(act, norm_done, b * KT)
                for f in range(KT):
                    act.wait_ge(tp_full, tb + TP_X + f + 1)
                    wait(act, sq_used, qb + f - 1)
                    act.activation(sq[f % 2][:, 0:n], tp[f % 2][:, 0:n], ACT.Square).then_inc(sq_ready, 1)
                    act.activation(xT[:, f, 0:n], tp[f % 2][:, 0:n], ACT.Copy).then_inc(tp_free, 1)
                act.wait_ge(sq_used, qb + KT)
                act.activation(tmp[2][:, 0:n], st[:, 0:n], ACT.Ln, scale=1.0 / D_MODEL,
                               bias=eps[:, 0:1]).then_inc(st_free, 1)
                act.wait_ge(st_free, b + 1)
                act.activation(tmp[2][:, 0:n], tmp[2][:, 0:n], ACT.Exp, scale=-0.5).then_inc(rs_ready, 1)
                for f in range(0 if sample else KT):
                    act.wait_ge(hf_ready, b * KT + f + 1)
                    act.activation(hn_hi[:, f, 0:n], htmp[f % 3][:, 0:n], ACT.Copy).then_inc(hi_ready, 1)

                if isinstance(b, int) and not sample:
                    strip_hi(0, 0, 1, 0)
                    strip_hi(1, 1, 1, 0)
                evac(ZP_LRA, lra[:, 0:n], zp[ZP_LRA % 2][0:RANK, 0:n]).then_inc(zp_free, 1)
                dst_a = [qa[:, 0:n], ka[:, 0:n], va[:, 0, 0:n], va[:, 1, 0:n], ra[:, 0, 0:n], ra[:, 1, 0:n]]
                for i in range(6):
                    evac(ZP_A + i, dst_a[i], scale=GLA_DK ** -0.5 if i == 0 else 1.0).then_inc(zp_free, 1)
                    next_hi(i)
                act.wait_ge(q_zero, 1)
                for i in range(6):
                    u, j = ZP_C + i, i % 2
                    if i < 2:
                        evac(u, qp[0:HD, 2 * j, 0:n], zp[u % 2][0:HD, 0:n], scale=HD ** -0.5)
                        evac(u, qp[HD:P, 2 * j + 1, 0:n], zp[u % 2][HD:P, 0:n], scale=HD ** -0.5).then_inc(zp_free, 1)
                    else:
                        if i == 2:
                            wait(act, kst_placed, 16 * b)
                            wait(act, rg_done, 2 * b)
                        evac(u, (kst if i < 4 else vst)[:, j, 0:n]).then_inc(zp_free, 1)
                    next_hi(6 + i)
                gba = prm2[:, R2_GBA:R2_GBA + 1]
                evac(ZP_Y, tmp[3][:, 0:n], func=ACT.Abs, bias=gba)
                evac(ZP_Y, tmp[2][:, 0:n], func=ACT.Identity, bias=gba).then_inc(zp_free, 1)
                act.wait_ge(zp_free, zb + ZP_Y + 1)
                chain.link(act.activation(tmp[3][:, 0:n], tmp[3][:, 0:n], ACT.Exp, scale=-1.0))
                act.activation(tmp[3][:, 0:n], tmp[3][:, 0:n], ACT.Ln, bias=1.0).then_inc(y_ready, 1)
                for u0, dst in ((TP_K, ktok), (TP_V, vtok), (TP_VA, vt)):
                    for j in range(2):
                        evac_tp(u0 + j, dst[0:rows, 0:tiles, j * P:(j + 1) * P],
                                tp[j][0:rows, 0:tiles * P].rearrange("p (i c) -> p i c", c=P))
                pos = 1 if sample else b * -1 + (NBLK - 1)
                act.wait_ge(tp_free, tb + TP_V + 2)
                act.dma_start(Kt[:, :, bass.ds(pos * BLK, n)], kst[:, :, 0:n]).then_inc(kst_placed, 16)
                if sample:
                    act.dma_start(sbk_s[0, 0].rearrange("t h d -> t (h d)"), ktok[0:DEC, 0, :]).then_inc(ktok_stored, 16)
                    act.dma_start(sbv_s[0, 0].rearrange("t h d -> t (h d)"), vtok[0:DEC, 0, :]).then_inc(v_placed, 16)
                    act.dma_start(Vb[0:DEC, TPB, :], vtok[0:DEC, 0, :]).then_inc(v_placed, 16)
                else:
                    for out, tok, done in ((sbk_p, ktok, ktok_stored), (sbv_p, vtok, v_placed)):
                        act.dma_start(out[0, 0, bass.ds(b * BLK, BLK)].rearrange("(i p) h d -> p i (h d)", p=P),
                                      tok[:, :, :]).then_inc(done, 16)
                    act.dma_start(Vb[:, bass.ds(pos * TPB, TPB), :], vtok[:, :, :]).then_inc(v_placed, 16)
                act.wait_ge(gd_ready, b + 1)
                act.activation(dec[:, 0:chunks], tmp[3][:, CHUNK - 1:n:CHUNK], ACT.Exp, scale=1.0 / GLA_TAU)
                act.activation(tmp[2][:, 0:n], tmp[2][:, 0:n], ACT.Exp, scale=1.0 / GLA_TAU).then_inc(kdec_ready, 1)
                act.wait_ge(halo_ready, b + 1)
                dst_b = [gb[:, 0, 0:n], gb[:, 1, 0:n], xbp[:, 0, 3:3 + n], xbp[:, 1, 3:3 + n]]
                for i in range(4):
                    evac(ZP_B + i, dst_b[i]).then_inc(zp_free, 1)
                    next_hi(12 + i)
                for i in range((tiles + 1) // 2):
                    w = min(2, tiles)
                    evac_tp(TP_KD + i, kdt[0:rows, 2 * i:2 * i + w, :],
                            tp[i % 2][0:rows, 0:w * P].rearrange("p (i c) -> p i c", c=P))
                act.wait_ge(dh_ready, b + 1)
                dst_d = [cd[:, 0, 0:n], cd[:, 1, 0:n], cxp[:, 0, 2:2 + n], cxp[:, 1, 2:2 + n],
                         bd[:, 0, 0:n], bd[:, 1, 0:n]]

                def evac_d(i):
                    evac(STRIP_USE[16 + i], dst_d[i]).then_inc(zp_free, 1)
                    next_hi(16 + i)

                evac_d(0)
                evac_d(1)
                act.wait_ge(kd_ready, b + 1)
                r, gi = tmp[0:2], tmp[2:4]
                for j in range(2):
                    for g, dst in ((0, r[j]), (1, gi[j])):
                        bias = (R2_RBA, R2_RBX)[g] + j
                        evac(ZP_G + 2 * j + g, dst[:, 0:n], func=ACT.Sigmoid,
                             bias=prm2[:, bias:bias + 1]).then_inc(zp_free, 1)
                act.wait_ge(zp_free, zb + ZP_G + 4)
                for j in range(2):
                    act.activation(rg_v[:, j, 0:n], r[j][:, 0:n], ACT.Tanh, scale=mixc["c8"][:, 1, j:j + 1])
                for j in range(2):
                    act.activation(r[j][:, 0:n], r[j][:, 0:n], ACT.Exp,
                                   scale=mixc["c8"][:, 0, j:j + 1]).then_inc(rgate, 1)
                evac_d(2)
                act.wait_ge(rg_u, 2 * (b + 1))
                act.activation(rg_v[:, :, 0:n], rg_v[:, :, 0:n], ACT.Sqrt).then_inc(rg_sqrt, 1)
                evac_d(3)
                act.activation(gb[:, :, 0:n], gb[:, :, 0:n], ACT.Gelu_apprx_tanh).then_inc(gelu_ready, 1)
                act.wait_ge(v_placed, 32 * (b + 1))
                evac_d(4)
                act.activation(ra[:, :, 0:n], ra[:, :, 0:n], ACT.Silu).then_inc(silu_ready, 1)
                evac_d(5)
                for j in range(2):
                    evac(ZP_O + j, oT[:, j, 0:n]).then_inc(zp_free, 1)
                act.preload_act_table_set(EXP_LN)
                act.wait_ge(rg_done, 2 * (b + 1))
                norm_squares(0)
                act.wait_ge(zp_free, zb + ZP_O + 2)
                norm_squares(1)
                act.wait_ge(d_ready, 2 * (b + 1))
                norm_squares(2)
                for g in range(NORM_C):
                    norm_ln(g)
                for g in range(NORM_C):
                    norm_exp(g)

                def weights(q, i, w):
                    act.wait_ge(x_done, q + i + 1)
                    x = aW[i % 2][0:rows, :, 0:w]
                    act.activation(x, x, ACT.Exp).then_inc(w_ready, 1)

                def key_block(q, width, newest, place):
                    achain.at(2 * q)
                    for i in range(2 * tiles):
                        w = width(i // 2)
                        act.wait_ge(sc_full, q + i + 1)
                        lt = aR[i % 2][0:rows, :, 0:w]
                        achain.link(act.activation(lt, score_banks[i % 2][0:rows, :, 0:w], ACT.Abs))
                        achain.link(act.activation(lt, lt, ACT.Exp, scale=-1.0))
                        act.activation(lt, lt, ACT.Ln, bias=1.0).then_inc(l_ready, 1)
                        if i:
                            weights(q, i - 1, width((i - 1) // 2))
                    weights(q, 2 * tiles - 1, width(tiles - 1))

                attend(act, b, sample, key_block)
                act.wait_ge(pv_done, pairs_after(b, sample))
                if sample:
                    act.activation(osb[0:rows, 0, 0:GW], ob[0:rows, 0:GW], ACT.Copy).then_inc(osb_ready, 1)
                else:
                    act.activation(osb[:, :, :], ob2[:, :, :], ACT.Copy).then_inc(osb_ready, 1)
                if not sample:
                    act.wait_ge(norm_done, KT * b + 2 * NORM_C)
                    for i in range(3):
                        out_hi(i)
                act.wait_ge(ot_full, b + 1)
                act.activation(oT[:, 4:6, 0:n], tp2[:, :, 0:n], ACT.Copy).then_inc(ot_done, 1)
                act.wait_ge(ot_done, b + 1)
                norm_squares(NORM_C)
                if not sample:
                    for i in range(3, 6):
                        out_hi(i)
                norm_ln(NORM_C)
                norm_exp(NORM_C)
                act.wait_ge(norm_done, KT * (b + 1))
                if not sample:
                    for i in (6, 7):
                        out_hi(i)

                def store(f):
                    act.wait_ge(x1_ready, b * KT + f + 1)
                    act.dma_start(x1_v[:, f, bass.ds(b * BLK, n)], xT[:, f, 0:n]).then_inc(x1_stored, 16)

                for f in range(KT):
                    wait(act, x1_ready, b * KT + f - 1)
                    evac(ZP_MIX + f, tmp[f % 2][:, 0:n], func=ACT.Identity,
                         scale=modT[:, M_G1 + f, m:m + 1]).then_inc(zp_free, 1)
                    next_hi(N_IN_STRIPS + f)
                    if f:
                        store(f - 1)
                store(KT - 1)
                if not sample:
                    assert act_links.setdefault("block", chain.n) == chain.n

            body(0, False)
            with act.Fori(1, NBLK) as b:
                body(b, False)
            for j in range(2):
                act.wait_ge(tp_full, NBLK * TP_PER + j + 1)
                act.activation(Kt[:, j, 0:PAST], tp[j][:, :], ACT.Copy).then_inc(tp_free, 1)
            body(NBLK, True)

        dve_links = {}

        @block.vector
        def _(dve):
            chain, achain = Chain(dve, dve_c), Chain(dve, dve_a)
            chain.at(0)
            chain.link(dve.memset(hst[:, :], 0.0))
            chain.link(dve.memset(S[:, CPB - 1, :], 0.0))
            dve.memset(xbp[:, :, 0:3], 0.0).then_inc(halo_ready, 1)
            dve.memset(cxp[:, :, 0:2], 0.0).then_inc(dh_ready, 1)
            setup_links = chain.n

            def body(b, sample):
                n, tiles, chunks, rows = shape_of(sample)
                m = 1 if sample else 0
                chain.at(setup_links + b * dve_links.get("block", 0) + (dve_links["between"] if sample else 0))
                zb = b * ZP_PER

                def norm(g):
                    dve.wait_ge(nrs_ready, 4 * b + g + 1)
                    for j in range(2):
                        t = NORM_PAIRS[g] + j
                        ins = dve.scalar_tensor_tensor(out=oT[:, t, 0:n], in0=oT[:, t, 0:n],
                                                       scalar=prm2[:, R2_ON + t:R2_ON + t + 1],
                                                       in1=nrs[g][:, j, 0:n], op0=ALU.mult, op1=ALU.mult)
                        if t < 2:
                            chain.link(ins)
                            dve.wait_ge(silu_ready, b + 1)
                            ins = dve.tensor_tensor(oT[:, t, 0:n], oT[:, t, 0:n], ra[:, t, 0:n], ALU.mult)
                        ins.then_inc(norm_done, 1)

                def h_lo(f):
                    dve.wait_ge(hi_ready, b * KT + f + 1)
                    dve.tensor_tensor(hn_lo[:, f, 0:n], htmp[f % 3][:, 0:n], hn_hi[:, f, 0:n].bitcast(F32),
                                      ALU.subtract).then_inc(lo_ready[1], 1)

                def out_lo(i):
                    f = OUT_ORDER[i]
                    dve.wait_ge(oh_ready, b * KT + i + 1)
                    dve.tensor_tensor(hn_lo[:, f, 0:n], oT[:, f, 0:n], hn_hi[:, f, 0:n].bitcast(F32),
                                      ALU.subtract).then_inc(ol_ready[1], 1)

                dve.wait_ge(rs_ready, b + 1)
                for f in range(KT):
                    t = htmp[f % 3][:, 0:n]
                    if sample:
                        t = h_whole[:, f, 0:n]
                    elif f >= 3:
                        dve.wait_ge(hi_ready, b * KT + f - 2)
                        dve.wait_ge(lo_ready[(f - 3) % 2], b * (KT // 2) + (f - 3) // 2 + 1)
                    chain.link(dve.tensor_tensor(t, xT[:, f, 0:n], tmp[2][:, 0:n], ALU.mult))
                    dve.tensor_scalar(t, t, gs1[:, f, m:m + 1], modT[:, M_SH1 + f, m:m + 1],
                                      ALU.mult, ALU.add).then_inc(hf_ready, 1)
                    if not sample and f and f % 2 == 0:
                        h_lo(f - 1)
                if not sample:
                    h_lo(KT - 1)
                dve.wait_ge(y_ready, b + 1)
                la, g = tmp[2][:, 0:n], tmp[3][:, 0:n]
                chain.link(dve.scalar_tensor_tensor(out=la, in0=la, scalar=0.0, in1=g, op0=ALU.min, op1=ALU.subtract))
                chain.link(dve.tensor_tensor_scan(g, mixc["scan_mask"][:, 0:n], la, 0.0, ALU.mult, ALU.add))
                g3 = g.rearrange("p (c t) -> p c t", t=CHUNK)
                dve.tensor_tensor(la.rearrange("p (c t) -> p c t", t=CHUNK),
                                  g3[:, :, CHUNK - 1:CHUNK].to_broadcast([P, chunks, CHUNK]), g3,
                                  ALU.subtract).then_inc(gd_ready, 1)
                dve.wait_ge(kdec_ready, b + 1)
                dve.tensor_tensor(ka[:, 0:n], ka[:, 0:n], la, ALU.mult).then_inc(kd_ready, 1)
                dve.wait_ge(zp_free, zb + ZP_B + 4)
                dve.wait_ge(ktok_stored, 16 * (b + 1))
                for j in range(2):
                    y = xcv[:, j, 0:n]
                    chain.link(dve.tensor_scalar(y, xbp[:, j, 0:n], prm2[:, R2_RCW + j:R2_RCW + j + 1],
                                                 prm2[:, R2_RCB + j:R2_RCB + j + 1], ALU.mult, ALU.add))
                    for i in range(1, 4):
                        ins = dve.scalar_tensor_tensor(out=y, in0=xbp[:, j, i:i + n],
                                                       scalar=prm2[:, R2_RCW + 2 * i + j:R2_RCW + 2 * i + j + 1],
                                                       in1=y, op0=ALU.mult, op1=ALU.add)
                        if i < 3:
                            chain.link(ins)
                        else:
                            ins.then_inc(xcv_ready, 1)
                dve.tensor_copy(xbp[:, :, 0:3], xbp[:, :, n:n + 3]).then_inc(halo_ready, 1)
                def states(c0, c1):
                    for c in range(c0, min(c1, chunks)):
                        dve.wait_ge(u_full, b * CPB + c + 1)
                        dve.tensor_tensor(um[:, :], zs[c % 2][:, 0:GW], mixc["bd_mask"][:, :], ALU.mult).then_inc(u_used, 1)
                        dve.wait_ge(u_used, b * CPB + c + 1)
                        dve.scalar_tensor_tensor(out=S[:, c, :], in0=S[:, (c - 1) % CPB, :], scalar=dec[:, c:c + 1],
                                                 in1=um[:, :], op0=ALU.mult, op1=ALU.add).then_inc(s_ready, 1)
                        dve.wait_ge(s_ready, b * CPB + c + 1)

                if sample:
                    dve.wait_ge(state_in, 16 * HEADS)
                states(0, 2)
                r, gi = tmp[0:2], tmp[2:4]
                for j in range(2):
                    a, u, v, w = r[j][:, 0:n], gi[j][:, 0:n], rg_v[:, j, 0:n], rg_w[:, 0:n]
                    dve.wait_ge(rgate, 2 * b + j + 1)
                    chain.link(dve.tensor_tensor(w, a, a, ALU.mult))
                    dve.tensor_tensor(u, u, xcv[:, j, 0:n], ALU.mult)
                    dve.scalar_tensor_tensor(out=v, in0=w, scalar=1.0, in1=v, op0=ALU.add, op1=ALU.mult).then_inc(rg_u, 1)
                    dve.wait_ge(rg_u, 2 * b + j + 1)
                states(2, 6)
                dve.wait_ge(rg_sqrt, b + 1)
                for j in range(2):
                    chain.link(dve.tensor_tensor(gi[j][:, 0:n], rg_v[:, j, 0:n], gi[j][:, 0:n], ALU.mult))
                    chain.link(dve.tensor_tensor_scan(oT[:, 2 + j, 0:n], r[j][:, 0:n], gi[j][:, 0:n], hst[:, j:j + 1],
                                                      ALU.mult, ALU.add))
                    chain.link(dve.tensor_copy(hst[:, j:j + 1], oT[:, 2 + j, n - 1:n]))
                dve.wait_ge(gelu_ready, b + 1)
                for j in range(2):
                    y = oT[:, 2 + j, 0:n]
                    dve.tensor_tensor(y, y, gb[:, j, 0:n], ALU.mult).then_inc(rg_done, 1)
                states(6, 8)
                dve.wait_ge(zp_free, zb + ZP_D2 + 4)
                chain.link(dve.tensor_tensor(cxp[:, :, 2:2 + n], cd[:, :, 0:n], cxp[:, :, 2:2 + n], ALU.mult))
                for j in range(2):
                    y = oT[:, 6 + j, 0:n]
                    chain.link(dve.tensor_scalar(y, cxp[:, j, 0:n], prm2[:, R2_SCW + j:R2_SCW + j + 1], None, ALU.mult))
                    for i in range(1, 3):
                        chain.link(dve.scalar_tensor_tensor(
                            out=y, in0=cxp[:, j, i:i + n], scalar=prm2[:, R2_SCW + 2 * i + j:R2_SCW + 2 * i + j + 1],
                            in1=y, op0=ALU.mult, op1=ALU.add))
                    dve.tensor_tensor(y, y, bd[:, j, 0:n], ALU.mult).then_inc(d_ready, 1)
                dve.tensor_copy(cxp[:, :, 0:2], cxp[:, :, n:n + 2]).then_inc(dh_ready, 1)
                for g in range(NORM_C):
                    norm(g)

                def turned(q, i, w):
                    dve.wait_ge(wtp_full, q + i + 1)
                    wait(dve, pv_done, q + i - 1)
                    kr, nk = (w, 1) if w < P else (P, w // P)
                    dve.tensor_copy(aT[i % 2][0:kr, :, 0:nk * rows], tp2[0:kr, :, 0:nk * rows]).then_inc(wt_ready, 1)

                def key_block(q, width, newest, place):
                    achain.at(2 * q)
                    for i in range(2 * tiles):
                        w = width(i // 2)
                        z, r, cc, x = (v[0:rows, :, 0:w] for v in (score_banks[i % 2], aR[i % 2], aC, aW[i % 2]))
                        sums = carry[0:rows, 2 * i:2 * i + 2]
                        dve.wait_ge(l_ready, q + i + 1)
                        achain.link(dve.scalar_tensor_tensor(out=r, in0=z, scalar=0.0, in1=r, op0=ALU.max, op1=ALU.add))
                        for j in range(2):
                            ins = dve.tensor_tensor_scan(cc[:, j, ::-1], r[:, j, ::-1], r[:, j, ::-1],
                                                         0.0 if newest else sums[:, j:j + 1], ALU.add, ALU.max)
                        achain.link(ins)
                        dve.tensor_copy(sums, cc[:, :, 0])
                        dve.tensor_tensor(x, z, cc, ALU.subtract).then_inc(x_done, 1)
                        if i:
                            turned(q, i - 1, width((i - 1) // 2))
                    turned(q, 2 * tiles - 1, width(tiles - 1))

                attend(dve, b, sample, key_block)
                for i in range(1, 0 if sample else 6, 2):
                    out_lo(i)
                norm(NORM_C)
                if not sample:
                    out_lo(7)
                for f in range(KT):
                    dve.wait_ge(zp_free, zb + ZP_MIX + f + 1)
                    dve.tensor_tensor(xT[:, f, 0:n], xT[:, f, 0:n], tmp[f % 2][:, 0:n], ALU.add).then_inc(x1_ready, 1)
                if not sample:
                    assert dve_links.setdefault("block", chain.n) == chain.n

            def gather_states(i):
                chain.link(dve.tensor_copy(stout[:, 0:2], hst[:, :]))
                chain.link(dve.tensor_copy(stout[:, 2:8].rearrange("p (i j) -> p j i", j=2), xbp[:, :, 0:3]))
                dve.tensor_copy(stout[:, 8:12].rearrange("p (i j) -> p j i", j=2), cxp[:, :, 0:2]).then_inc(stout_ready, 1)
                dve.wait_ge(strow_full, i + 1)
                dve.tensor_copy(strow[:, :], ob[0:12, 0:P]).then_inc(strow_ready, 1)

            body(0, False)
            with dve.Fori(1, NBLK) as b:
                body(b, False)
            chain.at(setup_links + NBLK * dve_links["block"])
            gather_states(0)
            dve.wait_ge(out_stored, 16 * (HEADS + 3))
            dve.memset(S[:, CPB - 1, :], 0.0).then_inc(init_ok, 1)
            chain.link(dve.tensor_copy(hst[:, :], prm2[:, R2_H:R2_H + 2]))
            chain.link(dve.tensor_copy(xbp[:, :, 0:3], prm2[:, R2_RBUF:R2_RBUF + 6].rearrange("p (i j) -> p j i", j=2)))
            chain.link(dve.tensor_copy(cxp[:, :, 0:2], prm2[:, R2_SBUF:R2_SBUF + 4].rearrange("p (i j) -> p j i", j=2)))
            dve.memset(carry[:, :], 0.0).then_inc(init_ok, 1)
            dve_links["between"] = chain.n
            body(NBLK, True)
            chain.at(chain.base + chain.n)
            gather_states(1)

        @block.tensor
        def _(pe):
            def body(b, sample):
                n, tiles, chunks, rows = shape_of(sample)
                zb, tb, qb = b * ZP_PER, tp_base(b, sample), b * KT
                idr = ident[0:rows, 0:rows]

                def use(u):
                    wait(pe, zp_free, zb + u - 1)
                    return zp[u % 2]

                def turn(u, parts):
                    wait(pe, tp_free, tb + u - 1)
                    for dst, src, idt in parts:
                        ins = pe.transpose(dst, src, idt)
                    ins.then_inc(tp_full, 1)

                def product3(out, hi, lo, order=range(KT), halves=None):
                    for i, k in enumerate(order):
                        if halves:
                            pe.wait_ge(halves[0], KT * b + i + 1)
                        pe.matmul(out, hi(k), hn_hi[:, k, 0:n], start=(i == 0), stop=False)
                        ins = pe.matmul(out, lo(k), hn_hi[:, k, 0:n], start=False, stop=False)
                        if halves:
                            pe.wait_ge(halves[1][i % 2], (KT // 2) * b + i // 2 + 1)
                        ins = pe.matmul(out, hi(k), hn_lo[:, k, 0:n], start=False, stop=(i == KT - 1))
                    return ins

                def product1(out, parts, stop_at):
                    for k, (w, x) in enumerate(parts):
                        ins = pe.matmul(out, w, x, start=(k == 0), stop=(k == stop_at - 1))
                    return ins

                def strip(i):
                    if sample:
                        if i < 2:
                            pe.wait_ge(w_in_sem[i], 16 * (NBLK * N_STRIPS // 2 + 1))
                        else:
                            pe.wait_ge(whole_in[i % RING_S], 16 * (i // RING_S + (i % RING_S >= 2)))
                        bank = use(STRIP_USE[i])
                        src = h_whole if i < N_IN_STRIPS else oT
                        product1(bank[:, 0:n], [(w_whole[i % RING_S][:, k, :], src[:, k, 0:n]) for k in range(KT)],
                                 KT).then_inc(zp_full, 1)
                        return
                    g, slot = b * N_STRIPS + i, i % 2
                    pe.wait_ge(w_hi_ready, g + 1)
                    pe.wait_ge(w_lo_ready, g + 1)
                    bank = use(STRIP_USE[i])
                    product3(bank[:, 0:n], lambda k: w_hi[slot][:, k, :], lambda k: w_lo[slot][:, k, :],
                             OUT_ORDER if i >= N_IN_STRIPS else range(KT),
                             (oh_ready, ol_ready) if i == N_IN_STRIPS else None).then_inc(zp_full, 1)

                def norm(g):
                    pe.wait_ge(nsq_ready, 4 * b + g + 1)
                    for j in range(2):
                        ins = pe.matmul(norm_bank[g][:, j, 0:n], head_ones[:, :], nsq[g][:, j, 0:n], start=True, stop=True)
                    ins.then_inc(nsum_full, 1)

                def sum_squares(f):
                    pe.wait_ge(sq_ready, qb + f + 1)
                    pe.matmul(st[:, 0:n], ones[:, :], sq[f % 2][:, 0:n], start=(f == 0), stop=(f == KT - 1)).then_inc(sq_used, 1)

                pe.wait_ge(x_loaded, 16 * (b + 1))
                for f in range(KT):
                    turn(TP_X + f, [(tp[f % 2][:, i * rows:(i + 1) * rows], xrow[0:rows, i, f * P:(f + 1) * P], idr)
                                    for i in range(tiles)])
                    if f:
                        sum_squares(f - 1)
                sum_squares(KT - 1)
                bank = use(ZP_LRA)
                if sample:
                    pe.wait_ge(hf_ready, KT * (b + 1))
                    product1(bank[:, 0:n], [(mixc[half][:, k * RANK:k * RANK + P].bitcast(F32), h_whole[:, k, 0:n])
                                            for k in range(KT) for half in ("lra_hi", "lra_lo")],
                             2 * KT).then_inc(zp_full, 1)
                else:
                    product3(bank[:, 0:n], lambda k: mixc["lra_hi"][:, k * RANK:k * RANK + P],
                             lambda k: mixc["lra_lo"][:, k * RANK:k * RANK + P],
                             halves=(hi_ready, lo_ready)).then_inc(zp_full, 1)
                for i in range(12):
                    strip(i)
                bank = use(ZP_Y)
                pe.matmul(bank[:, 0:n], mixc["wa2"][:, :], lra[:, 0:n], start=True, stop=True).then_inc(zp_full, 1)
                for u0, src in ((TP_K, kst), (TP_V, vst), (TP_VA, va)):
                    pe.wait_ge(zp_free, zb + ZP_C + (4 if u0 == TP_K else 6))
                    for j in range(2):
                        turn(u0 + j, [(tp[j][0:rows, i * P:(i + 1) * P], src[:, j, i * rows:(i + 1) * rows], ident[:, :])
                                      for i in range(tiles)])
                for i in range(12, 16):
                    strip(i)
                pe.wait_ge(kd_ready, b + 1)
                for i in range((tiles + 1) // 2):
                    turn(TP_KD + i, [(tp[i % 2][0:rows, v * P:(v + 1) * P],
                                      ka[:, (2 * i + v) * rows:(2 * i + v + 1) * rows], ident[:, :])
                                     for v in range(min(2, tiles))])
                def updates(c0, c1):
                    for c in range(c0, min(c1, chunks)):
                        r0 = CHUNK * (c % 2)
                        wait(pe, u_used, b * CPB + c - 1)
                        pe.matmul(zs[c % 2][:, 0:GW], kdt[r0:r0 + CHUNK, c // 2, :], vt[r0:r0 + CHUNK, c // 2, :],
                                  start=True, stop=True).then_inc(u_full, 1)

                strip(16)
                strip(17)
                pe.wait_ge(tp_free, tb + TP_KD + (tiles + 1) // 2)
                updates(0, 2)
                pe.wait_ge(xcv_ready, 2 * (b + 1))
                for j in range(2):
                    for g in range(2):
                        bank = use(ZP_G + 2 * j + g)
                        pe.matmul(bank[:, 0:n], mixc["rgw"][:, g, j, :], xcv[:, j, 0:n], start=True,
                                  stop=True).then_inc(zp_full, 1)
                for i in range(3):
                    strip(18 + i)
                    updates(2 + 2 * i, 4 + 2 * i)
                strip(21)
                pe.wait_ge(s_ready, b * CPB + chunks)
                for j in range(2):
                    bank = use(ZP_O + j)
                    for c in range(chunks):
                        ins = pe.matmul(bank[:, c * CHUNK:(c + 1) * CHUNK], S[:, c, j * P:(j + 1) * P],
                                        qa[:, c * CHUNK:(c + 1) * CHUNK], start=True, stop=True)
                    ins.then_inc(zp_full, 1)
                for g in range(NORM_C):
                    norm(g)

                pe.wait_ge(kst_placed, 16 * (b + 1))
                pe.wait_ge(v_placed, 32 * (b + 1))

                def key_block(q, width, newest, place):
                    at, vtile = place() * BLK, place() * TPB
                    if not isinstance(at, int):
                        at, vtile = pe.snap(at), pe.snap(vtile)

                    def score(i):
                        s, w = i // 2, width(i // 2)
                        wait(pe, x_done, q + i - 1)
                        for j in range(2):
                            bank = score_banks[i % 2][0:rows, j, 0:w]
                            ins = pe.matmul(bank, qp[:, 2 * (i % 2) + j, s * rows:(s + 1) * rows],
                                            Kt[:, i % 2, bass.ds(at, w)], start=True, stop=not newest)
                            if newest:
                                ins = pe.matmul(score_banks[i % 2][0:rows, j, w - rows:w], idr,
                                                mixc["neg_mask"][0:rows, 0:rows], start=False, stop=True)
                        ins.then_inc(sc_full, 1)

                    def turn_weights(i):
                        w = width(i // 2)
                        kr, nk = (w, 1) if w < P else (P, w // P)
                        pe.wait_ge(w_ready, q + i + 1)
                        wait(pe, wt_ready, q + i)
                        for j in range(2):
                            for v in range(nk):
                                ins = pe.transpose(tp2[0:kr, j, v * rows:(v + 1) * rows],
                                                   aW[i % 2][0:rows, j, v * kr:(v + 1) * kr], idr)
                        ins.then_inc(wtp_full, 1)

                    def values(i):
                        s, w = i // 2, width(i // 2)
                        kr, nk = (w, 1) if w < P else (P, w // P)
                        pe.wait_ge(wt_ready, q + i + 1)
                        for j in range(2):
                            cols = slice(HD * (2 * (i % 2) + j), HD * (2 * (i % 2) + j + 1))
                            at_col = GW * (s % 2) + cols.start
                            for v in range(nk):
                                ins = pe.matmul(ob2[0:rows, s // 2, at_col:at_col + HD],
                                                aT[i % 2][0:kr, j, v * rows:(v + 1) * rows],
                                                Vb[0:kr, vtile + v, cols] if isinstance(vtile, int) else
                                                Vb[0:kr, bass.ds(vtile + v, 1), cols],
                                                start=(newest and i % 4 == 0 and j == 0 and v == 0), stop=False,
                                                skip_group_check=True)
                        ins.then_inc(pv_done, 1)

                    score(0)
                    score(1)
                    for i in range(2 * tiles):
                        if i + 2 < 2 * tiles:
                            score(i + 2)
                        if i:
                            values(i - 1)
                        turn_weights(i)
                    values(2 * tiles - 1)

                pe.wait_ge(zp_free, zb + ZP_O + 2)
                pe.wait_ge(nln_ready, 4 * b + NORM_C)
                attend(pe, b, sample, key_block)
                pe.wait_ge(osb_ready, b + 1)
                for s in range(tiles):
                    for j in range(2):
                        ins = pe.transpose(tp2[:, j, s * rows:(s + 1) * rows],
                                           osb[0:rows, s // 2, GW * (s % 2) + j * P:GW * (s % 2) + (j + 1) * P], idr)
                ins.then_inc(ot_full, 1)
                norm(NORM_C)
                if sample:
                    pe.wait_ge(norm_done, KT * (b + 1))
                for i in range(N_IN_STRIPS, N_STRIPS):
                    strip(i)

            def turn_states(i):
                pe.wait_ge(stout_ready, i + 1)
                pe.transpose(ob[0:12, 0:P], stout[:, :], ident[:, :]).then_inc(strow_full, 1)

            body(0, False)
            with pe.Fori(1, NBLK) as b:
                body(b, False)
            turn_states(0)
            pe.wait_ge(past_in, 32)
            for j in range(2):
                pe.wait_ge(tp_free, NBLK * TP_PER + j - 1)
                for i in range(PAST // P):
                    ins = pe.transpose(tp[j][:, i * P:(i + 1) * P], ktok[:, i, j * P:(j + 1) * P], ident[:, :])
                ins.then_inc(tp_full, 1)
            body(NBLK, True)
            turn_states(1)


def mlp_phase(nc, const, x1_v, mlp_w1, mlp_w2, y_prompt, y_sample):
    prm2, modT, gs2 = const["prm2"], const["modT"], const["gs2"]
    ident, ones, eps = const["ident"], const["ones"], const["eps"]
    NSB = 3
    T = N_TOK // NSB
    CB = T // 2
    NFT = D_FF // P
    NC = NFT // 2
    TILES = [P] * (T // P) + [T % P]
    assert SEQ == (NSB - 1) * T + T - DEC and CB % 2 == 0
    with ExitStack() as ctx:
        def sb(name, shape, dt=F32):
            return ctx.enter_context(nc.sbuf_tensor(name, shape, dt))

        def ps(name):
            return ctx.enter_context(nc.psum_tensor(name, [P, 512], F32))

        def sem(name):
            return ctx.enter_context(nc.semaphore(name))

        xs = [sb(f"xs{i}", [P, KT, T]) for i in range(2)]
        h_hi, h_lo = sb("h_hi", [P, KT, T], F32R), sb("h_lo", [P, KT, T], F32R)
        g_hi = [sb(f"g_hi{i}", [P, 2, T], F32R) for i in range(2)]
        g_lo = [sb(f"g_lo{i}", [P, 2, T], F32R) for i in range(2)]
        w1r = [sb(f"w1r{i}", [P, KT, P]) for i in range(2)]
        w1h = [sb(f"w1h{i}", [P, KT, P], F32R) for i in range(2)]
        w1l = [sb(f"w1l{i}", [P, KT, P], F32R) for i in range(2)]
        w2r = [sb(f"w2r{i}", [P, D_MODEL]) for i in range(2)]
        w2h = [sb(f"w2h{i}", [P, D_MODEL], F32R) for i in range(4)]
        w2l = [sb(f"w2l{i}", [P, D_MODEL], F32R) for i in range(4)]
        rt = [sb(f"rt{i}", [P, CB]) for i in range(2)]
        sqt = [sb(f"sqt{i}", [P, CB]) for i in range(2)]
        rms = [sb(f"rms{i}", [P, CB]) for i in range(2)]
        nsq, nacc = [sb(f"nsq{i}", [P, CB]) for i in range(2)], [sb(f"nacc{i}", [P, CB]) for i in range(2)]
        yrow = [sb(f"yrow{i}", [P, D_MODEL]) for i in range(2)]
        h2t = [rt[0], rt[1], nsq[0], nsq[1]]
        hp, op = [ps("hp0"), ps("hp1")], [ps(f"op{i}") for i in range(4)]
        stb = [ps("stb0"), ps("stb1")]

        x_in, w1_in, w2_in = [sem("x_in0"), sem("x_in1")], [sem("w1_in0"), sem("w1_in1")], [sem("w2_in0"), sem("w2_in1")]
        w1_hi, w1_lo, w2_hi, w2_lo = sem("w1_hi"), sem("w1_lo"), sem("w2_hi"), sem("w2_lo")
        n_sq, n_acc, n_sum, n_rms, n_rms_c = sem("n_sq"), sem("n_acc"), sem("n_sum"), sem("n_rms"), sem("n_rms_c")
        hf2, h2_whole, hi2, lo2 = sem("hf2"), sem("h2_whole"), sem("hi2"), sem("lo2")
        h_full, h_relu, h_sq, gh_ready, gl_ready = (
            sem("h_full"), sem("h_relu"), sem("h_sq"), sem("gh_ready"), sem("gl_ready"))
        o_full, o_added, y_norm, yt_full, yt_read, y_out = (
            sem("o_full"), sem("o_added"), sem("y_norm"), sem("yt_full"), sem("yt_read"), [sem("y_out0"), sem("y_out1")])
        w1_v = mlp_w1[0].rearrange("(k p) n -> p k n", p=P)
        NT = NSB * NC
        N_YT = 2 * len(TILES)
        NV = 2 * KT
        NORMS = [("second", 0), ("second", 1), ("final", 0), ("second", 2), ("final", 1), ("final", 2)]
        block = ctx.enter_context(nc.Block())

        def each_chunk(eng, sbk, one):
            c = sbk * NC
            for j in range(4):
                one(c + j, j % 2, j)
            with eng.Fori(2, NC // 2 - 1) as i:
                one(c + 2 * i, 0, None)
                one(c + 2 * i + 1, 1, None)
            for j in (NC - 2, NC - 1):
                one(c + j, j % 2, j)

        def sum_squares(eng, kind, sbk):
            for v in range(2, NV):
                square_sum(eng, kind, sbk, v)

        def square_sum(eng, kind, sbk, v):
            k, (f, cb) = NORMS.index((kind, sbk)), divmod(v, 2)
            eng.wait_ge(n_sq, k * NV + v + 1)
            wait(eng, n_acc, k * (NV - 2) + v - 3)
            eng.tensor_tensor(nacc[cb][:, :], nacc[cb][:, :], nsq[cb][:, :], ALU.add).then_inc(n_acc, 1)

        def ranges(sbk, cb):
            if sbk == NSB - 1 and cb == 1:
                return [(0, CB - DEC, 0), (CB - DEC, CB, 1)]
            return [(0, CB, 0)]

        @block.sync
        def _(sp):
            def load_w(kind, g, slot, row):
                sems, hi, lo = (w1_in, w1_hi, w1_lo) if kind == 1 else (w2_in, w2_hi, w2_lo)
                wait(sp, hi, g - 1)
                wait(sp, lo, g - 1)
                if kind == 1:
                    sp.dma_start(w1r[slot][:, :, :], w1_v[:, :, bass.ds(row, P)]).then_inc(sems[slot], 16)
                else:
                    sp.dma_start(w2r[slot][:, :], mlp_w2[0, bass.ds(row, P), :]).then_inc(sems[slot], 16)

            def load_x(sbk):
                if sbk < NSB:
                    wait(sp, yt_read, (sbk - 1) * N_YT)
                    sp.dma_start(xs[sbk % 2][:, :, :], x1_v[:, :, sbk * T:(sbk + 1) * T]).then_inc(x_in[sbk % 2], 16)

            for j in range(2):
                load_w(1, j, j, j * P)
            load_x(0)
            for j in range(2):
                load_w(2, j, j, j * P)
            def store_rows(sbk):
                for i, rows in enumerate(TILES):
                    sp.wait_ge(yt_read, sbk * N_YT + 2 * i + 2)
                    t0 = sbk * T + i * P
                    dst = y_prompt[0, t0:t0 + rows, :] if t0 < SEQ else y_sample[0, t0 - SEQ:t0 - SEQ + rows, :]
                    sp.dma_start(dst, yrow[i % 2][0:rows, :]).then_inc(y_out[i % 2], 16)

            load_x(1)
            for sbk in range(NSB):
                def loads(c, _, nth):
                    if isinstance(c, int) and c == NT - 1:
                        return
                    row = 0 if isinstance(c, int) and (c + 1) % NC == 0 else (c - sbk * NC + 1) * (2 * P)
                    for kind in (1, 2):
                        for j in range(2):
                            load_w(kind, 2 * c + 2 + j, j, row + j * P)
                    if nth == 3 and sbk:
                        store_rows(sbk - 1)
                        load_x(sbk + 1)

                each_chunk(sp, sbk, loads)
            store_rows(NSB - 1)
            for i in range(2):
                sp.wait_ge(y_out[i], 16 * NSB * len(TILES) // 2)

        @block.gpsimd
        def _(pool):
            def lo(kind, g, slot4, slot2, used):
                hi, done = (w1_hi, w1_lo) if kind == 1 else (w2_hi, w2_lo)
                pool.wait_ge(hi, g + 1)
                wait(pool, h_full if kind == 1 else o_full, used)
                if kind == 1:
                    pool.tensor_tensor(w1l[slot2][:, :, :], w1r[slot2][:, :, :], w1h[slot2][:, :, :].bitcast(F32),
                                       ALU.subtract).then_inc(done, 1)
                else:
                    pool.tensor_tensor(w2l[slot4][:, :], w2r[slot2][:, :], w2h[slot4][:, :].bitcast(F32),
                                       ALU.subtract).then_inc(done, 1)

            def h2_lo(sbk):
                for v in range(NV):
                    f, cb = v // 2, v % 2
                    pool.wait_ge(hi2, sbk * NV + v + 1)
                    cols = slice(cb * CB, (cb + 1) * CB)
                    pool.tensor_tensor(h_lo[:, f, cols], h2t[v % 4][:, :], h_hi[:, f, cols].bitcast(F32),
                                       ALU.subtract).then_inc(lo2, 1)

            for kind in (1, 2):
                for j in range(2):
                    lo(kind, j, j, j, 0)
            h2_lo(0)
            for sbk in range(NSB):
                def chunk(c, odd, nth):
                    more = not (isinstance(c, int) and c == NT - 1)
                    if more:
                        for j in range(2):
                            lo(1, 2 * c + 2 + j, 0, j, 4 * c + 2 * j + 2)
                    if nth == 1 and sbk:
                        sum_squares(pool, "final", sbk - 1)
                    if nth == NC - 2 and sbk + 1 < NSB:
                        sum_squares(pool, "second", sbk + 1)
                    if nth == NC - 1 and sbk + 1 < NSB:
                        h2_lo(sbk + 1)
                    if more:
                        for j in range(2):
                            lo(2, 2 * c + 2 + j, (2 * (odd + 1) + j) % 4, j, 16 * c)

                each_chunk(pool, sbk, chunk)

        @block.scalar
        def _(act):
            def hi(kind, g, slot4, slot2, loads, used):
                act.wait_ge((w1_in if kind == 1 else w2_in)[slot2], 16 * loads)
                wait(act, h_full if kind == 1 else o_full, used)
                if kind == 1:
                    act.activation(w1h[slot2][:, :, :], w1r[slot2][:, :, :], ACT.Copy).then_inc(w1_hi, 1)
                else:
                    act.activation(w2h[slot4][:, :], w2r[slot2][:, :], ACT.Copy).then_inc(w2_hi, 1)

            def chunk(c, odd, between):
                more = not (isinstance(c, int) and c == NT - 1)
                for ft in range(2):
                    for cb in range(2):
                        i = 2 * ft + cb
                        h = 4 * c + i
                        act.wait_ge(h_full, h + 1)
                        wait(act, h_sq, h - 1)
                        act.activation(rt[i % 2][:, :], hp[i % 2][:, 0:CB], ACT.Relu).then_inc(h_relu, 1)
                        act.wait_ge(h_sq, h + 1)
                        wait(act, o_full, 16 * (c - 1) if isinstance(c, int) else 16 * c - 16)
                        act.activation(g_hi[odd][:, ft, cb * CB:(cb + 1) * CB], sqt[i % 2][:, :],
                                       ACT.Copy).then_inc(gh_ready, 1)
                    if more:
                        hi(1, 2 * c + 2 + ft, 0, ft, c + 2, 4 * c + 2 * ft + 2)
                between()
                if more:
                    for j in range(2):
                        hi(2, 2 * c + 2 + j, (2 * (odd + 1) + j) % 4, j, c + 2, 16 * c)

            def squares(kind, sbk):
                k, x = NORMS.index((kind, sbk)), xs[sbk % 2]
                if kind == "second":
                    act.wait_ge(x_in[sbk % 2], 16 * (sbk // 2 + 1))
                wait(act, n_sum, 2 * k)
                for f in range(KT):
                    for cb in range(2):
                        if kind == "final":
                            act.wait_ge(o_added, ((sbk + 1) * NC - 1) * 16 + 2 * f + cb + 1)
                        if f:
                            wait(act, n_acc, (k * (KT - 1) + f - 1) * 2 + cb - 1)
                        act.activation((nsq if f else nacc)[cb][:, :], x[:, f, cb * CB:(cb + 1) * CB],
                                       ACT.Square).then_inc(n_sq, 1)

            def inverse_rms(kind, sbk):
                k = NORMS.index((kind, sbk))
                if k:
                    before, third = NORMS[k - 1]
                    act.wait_ge(hf2 if before == "second" else y_norm, NV * (third + 1))
                for cb in range(2):
                    act.wait_ge(n_sum, 2 * k + cb + 1)
                    act.activation(rms[cb][:, :], stb[cb][:, 0:CB], ACT.Ln, scale=1.0 / D_MODEL,
                                   bias=eps[:, 0:1]).then_inc(n_rms_c, 1)
                for cb in range(2):
                    act.wait_ge(n_rms_c, 2 * k + cb + 1)
                    act.activation(rms[cb][:, :], rms[cb][:, :], ACT.Exp, scale=-0.5).then_inc(n_rms, 1)

            def h2_hi(sbk):
                for v in range(NV + 1):
                    if v < NV:
                        f, cb = v // 2, v % 2
                        act.wait_ge(hf2, sbk * NV + v + 1)
                        for a, e, m in ranges(sbk, cb):
                            t = h2t[v % 4][:, a:e]
                            ins = act.activation(t, t, ACT.Identity, scale=gs2[:, f, m:m + 1],
                                                 bias=modT[:, M_SH2 + f, m:m + 1])
                        ins.then_inc(h2_whole, 1)
                    if v:
                        f, cb = (v - 1) // 2, (v - 1) % 2
                        act.wait_ge(h2_whole, sbk * NV + v)
                        act.activation(h_hi[:, f, cb * CB:(cb + 1) * CB], h2t[(v - 1) % 4][:, :],
                                       ACT.Copy).then_inc(hi2, 1)

            def rows_of(sbk):
                for i, rows in enumerate(TILES):
                    for v in range(2):
                        u = sbk * N_YT + 2 * i + v
                        act.wait_ge(yt_full, u + 1)
                        wait(act, y_out[i % 2], 16 * ((sbk * len(TILES) + i) // 2))
                        act.activation(yrow[i % 2][0:rows, v * 512:(v + 1) * 512], stb[v][0:rows, :],
                                       ACT.Copy).then_inc(yt_read, 1)

            act.preload_act_table_set(EXP_LN)
            for j in range(2):
                hi(1, j, j, j, 1, 0)
            squares("second", 0)
            for j in range(2):
                hi(2, j, j, j, 1, 0)
            inverse_rms("second", 0)
            h2_hi(0)
            for sbk in range(NSB):
                act.wait_ge(lo2, (sbk + 1) * NV)

                def one(c, odd, nth):
                    def between():
                        if nth == 1 and sbk:
                            squares("final", sbk - 1)
                        if nth == 2 and sbk:
                            inverse_rms("final", sbk - 1)
                        if nth == 3 and sbk:
                            rows_of(sbk - 1)
                        if nth == NC - 2 and sbk + 1 < NSB:
                            squares("second", sbk + 1)
                        if nth == NC - 1 and sbk + 1 < NSB:
                            inverse_rms("second", sbk + 1)
                            h2_hi(sbk + 1)

                    chunk(c, odd, between)

                each_chunk(act, sbk, one)
            squares("final", NSB - 1)
            inverse_rms("final", NSB - 1)
            rows_of(NSB - 1)

        @block.vector
        def _(dve):
            def hidden(c, odd):
                for i in range(4):
                    ft, cb = i // 2, i % 2
                    h = 4 * c + i
                    dve.wait_ge(h_relu, h + 1)
                    wait(dve, gh_ready, h - 1)
                    dve.tensor_tensor(sqt[i % 2][:, :], rt[i % 2][:, :], rt[i % 2][:, :], ALU.mult).then_inc(h_sq, 1)
                    dve.wait_ge(gh_ready, h + 1)
                    cols = slice(cb * CB, (cb + 1) * CB)
                    dve.tensor_tensor(g_lo[odd][:, ft, cols], sqt[i % 2][:, :], g_hi[odd][:, ft, cols].bitcast(F32),
                                      ALU.subtract).then_inc(gl_ready, 1)

            def add(c, sbk, between=lambda i: None):
                x = xs[sbk % 2]
                for d in range(KT):
                    for cb in range(2):
                        i = 2 * d + cb
                        dve.wait_ge(o_full, 16 * c + i + 1)
                        if i == 0:
                            wait(dve, o_added, 16 * c)
                        for n, (a, e, m) in enumerate(ranges(sbk, cb)):
                            cols = x[:, d, cb * CB + a:cb * CB + e]
                            ins = dve.scalar_tensor_tensor(out=cols, in0=op[i % 4][:, a:e],
                                                           scalar=modT[:, M_G2 + d, m:m + 1], in1=cols,
                                                           op0=ALU.mult, op1=ALU.add)
                        ins.then_inc(o_added, 1)
                        between(i)

            def h2(sbk, v):
                f, cb = v // 2, v % 2
                u, t = sbk * NV + v, h2t[v % 4]
                dve.wait_ge(n_rms, 2 * NORMS.index(("second", sbk)) + 2)
                wait(dve, hi2, u - 3)
                wait(dve, lo2, u - 3)
                dve.tensor_tensor(t[:, :], xs[sbk % 2][:, f, cb * CB:(cb + 1) * CB], rms[cb][:, :],
                                  ALU.mult).then_inc(hf2, 1)

            def final(sbk, v):
                f, cb = v // 2, v % 2
                dve.wait_ge(n_rms, 2 * NORMS.index(("final", sbk)) + 2)
                cols = xs[sbk % 2][:, f, cb * CB:(cb + 1) * CB]
                dve.scalar_tensor_tensor(out=cols, in0=cols, scalar=prm2[:, R2_FIN + f:R2_FIN + f + 1],
                                         in1=rms[cb][:, :], op0=ALU.mult, op1=ALU.mult).then_inc(y_norm, 1)

            sum_squares(dve, "second", 0)
            for v in range(NV):
                h2(0, v)
            for sbk in range(NSB):
                def next_h2(early):
                    def between(i):
                        v = (i - 7) // 2 if early and i % 2 and i >= 7 else i + 5 if not early else NV
                        if sbk + 1 < NSB and v < NV:
                            h2(sbk + 1, v)
                    return between

                def chunk(c, odd, nth):
                    hidden(c, odd)
                    if nth == 0:
                        return
                    if nth == 2 and sbk:
                        add(c - 1, sbk, lambda i: final(sbk - 1, i))
                    elif nth == NC - 1:
                        add(c - 1, sbk, next_h2(True))
                    else:
                        add(c - 1, sbk)

                each_chunk(dve, sbk, chunk)
                if sbk + 1 < NSB:
                    add(sbk * NC + NC - 1, sbk, next_h2(False))
            add(NT - 1, NSB - 1, lambda i: square_sum(dve, "final", NSB - 1, i - 2) if i >= 4 else None)
            for v in (NV - 2, NV - 1):
                square_sum(dve, "final", NSB - 1, v)
            dve.wait_ge(o_added, 16 * NT)
            for v in range(NV):
                final(NSB - 1, v)

        @block.tensor
        def _(pe):
            def hidden(c, odd, third=None):
                for ft in range(2):
                    pe.wait_ge(w1_hi, 2 * c + ft + 1)
                    pe.wait_ge(w1_lo, 2 * c + ft + 1)
                    for cb in range(2):
                        wait(pe, h_relu, 4 * c + 2 * ft + cb - 1)
                        cols, bank = slice(cb * CB, (cb + 1) * CB), hp[cb][:, 0:CB]
                        for k in range(KT):
                            if third is not None and ft == 0:
                                pe.wait_ge(hi2, NV * third + 2 * k + cb + 1)
                                pe.wait_ge(lo2, NV * third + 2 * k + cb + 1)
                            pe.matmul(bank, w1h[ft][:, k, :], h_hi[:, k, cols], start=(k == 0), stop=False)
                            pe.matmul(bank, w1h[ft][:, k, :], h_lo[:, k, cols], start=False, stop=False)
                            ins = pe.matmul(bank, w1l[ft][:, k, :], h_hi[:, k, cols], start=False, stop=(k == KT - 1))
                        ins.then_inc(h_full, 1)

            def project(c, odd, between=lambda i: None):
                pe.wait_ge(gh_ready, 4 * c + 4)
                pe.wait_ge(gl_ready, 4 * c + 4)
                pe.wait_ge(w2_hi, 2 * c + 2)
                pe.wait_ge(w2_lo, 2 * c + 2)
                for d in range(KT):
                    for cb in range(2):
                        i = 2 * d + cb
                        wait(pe, o_added, 16 * c + i - 3)
                        cols, bank = slice(cb * CB, (cb + 1) * CB), op[i % 4][:, 0:CB]
                        for ft in range(2):
                            wh = w2h[2 * odd + ft][:, d * P:(d + 1) * P]
                            wl = w2l[2 * odd + ft][:, d * P:(d + 1) * P]
                            pe.matmul(bank, wh, g_hi[odd][:, ft, cols], start=(ft == 0), stop=False)
                            pe.matmul(bank, wh, g_lo[odd][:, ft, cols], start=False, stop=False)
                            ins = pe.matmul(bank, wl, g_hi[odd][:, ft, cols], start=False, stop=(ft == 1))
                        ins.then_inc(o_full, 1)
                        between(i)

            def norm(kind, sbk):
                k = NORMS.index((kind, sbk))
                pe.wait_ge(n_acc, 2 * (KT - 1) * (k + 1))
                wait(pe, n_rms_c, 2 * k)
                if ("final", 0) in NORMS[:k]:
                    pe.wait_ge(yt_read, N_YT * sum(kd == "final" for kd, _ in NORMS[:k]))
                for cb in range(2):
                    pe.matmul(stb[cb][:, 0:CB], ones[:, :], nacc[cb][:, :], start=True, stop=True).then_inc(n_sum, 1)

            def turn(sbk, u):
                i, v = u // 2, u % 2
                rows = TILES[i]
                pe.wait_ge(y_norm, (sbk + 1) * NV)
                pe.wait_ge(n_rms_c, 2 * NORMS.index(("final", sbk)) + 2)
                wait(pe, yt_read, sbk * N_YT + u - 1)
                for f in range(4):
                    ins = pe.transpose(stb[v][0:rows, f * P:(f + 1) * P],
                                       xs[sbk % 2][:, 4 * v + f, i * P:i * P + rows], ident[:, :])
                ins.then_inc(yt_full, 1)

            norm("second", 0)
            for sbk in range(NSB):
                def chunk(c, odd, nth):
                    hidden(c, odd, sbk if nth == 0 else None)
                    if nth == NC - 1 and sbk + 1 < NSB:
                        norm("second", sbk + 1)
                    if nth == 0:
                        return
                    if nth == 2 and sbk:
                        norm("final", sbk - 1)
                    if nth == 3 and sbk:
                        project(c - 1, 1 - odd, lambda i: turn(sbk - 1, i) if i < N_YT else None)
                    else:
                        project(c - 1, 1 - odd)

                each_chunk(pe, sbk, chunk)
                project(sbk * NC + NC - 1, 1)
            norm("final", NSB - 1)
            for u in range(N_YT):
                turn(NSB - 1, u)


_INS = ['x_prompt', 'x_sample', 'c_prompt', 'c_sample', 'state_gla', 'state_rg_h', 'state_rg_conv', 'cache_sb_k',
        'cache_sb_v', 'state_sc_conv', 'ln1_g', 'ln2_g', 'w_ada', 'b_ada', 'w_in', 'gla_wa2', 'gla_ba', 'rg_conv_w',
        'rg_conv_b', 'rg_wa', 'rg_ba', 'rg_wx', 'rg_bx', 'rg_lambda', 'sc_conv_w', 'out_norm_g', 'w_out', 'mlp_w1',
        'mlp_w2', 'final_g']
_OUTS = [(1, SEQ, D_MODEL), (1, DEC, D_MODEL), (1, 1, HEADS, GLA_DK, HD), (1, 1, HEADS, GLA_DK, HD),
         (1, 1, GW), (1, 1, GW), (1, 1, 3, GW), (1, 1, 3, GW), (1, 1, SEQ, HEADS, HD), (1, 1, DEC, HEADS, HD),
         (1, 1, SEQ, HEADS, HD), (1, 1, DEC, HEADS, HD), (1, 1, 2, GW), (1, 1, 2, GW)]


def kernel(**inputs):
    import numpy as _np
    import concourse.bacc as _bacc
    from concourse import mybir as _mybir
    from concourse.bass_utils import run_bass_kernel_spmd as _run

    nc = _bacc.Bacc("TRN2", target_bir_lowering=False, num_devices=1)
    arrays, args = {}, []
    for name in _INS:
        a = _np.ascontiguousarray(inputs[name])
        arrays[f"in_{name}_dram"] = a
        args.append(nc.dram_tensor(f"in_{name}_dram", a.shape, _mybir.dt.from_np(a.dtype), kind="ExternalInput").ap())
    for i, shape in enumerate(_OUTS):
        args.append(nc.dram_tensor(f"out_{i}_dram", shape, F32, kind="ExternalOutput").ap())
    build(nc, *args)
    r = _run(nc, [arrays], core_ids=[0])
    return tuple(r.results[0][f"out_{i}_dram"] for i in range(len(_OUTS)))
```
